# Optimizing a Trainium2 kernel written in Bass

```python
import math
import jax, jax.numpy as jnp
from jax import lax
import numpy as np

D_MODEL = 1024
BATCH = 1
SEQ = 1024
DEPTH = 1

N_MEM = 256
D_MIX = D_MODEL
CHUNK = 128
GM_GROUPS = 4
GM_WIDTH = D_MIX // 2
GM_DIM = GM_WIDTH // GM_GROUPS
SB_WIDTH = D_MIX - GM_WIDTH
SB_HEADS = 8
SB_HEAD_DIM = SB_WIDTH // SB_HEADS
Q_BLOCK = 128
IN_COLS = 2 * GM_WIDTH + 3 * SB_WIDTH
X_HEADS = 4
X_HEAD_DIM = D_MODEL // X_HEADS
D_FF = 4 * D_MODEL
EPS = 1e-6

kernel_name = "hybrid_gmlp_stickbreaking_memxattn_block"

def rms_norm(x, g):
    xf = x.astype(jnp.float32)
    y = xf * lax.rsqrt(jnp.mean(xf * xf, axis=-1, keepdims=True) + EPS)
    return (y * g.astype(jnp.float32)).astype(x.dtype)

def head_rms(x):
    xf = x.astype(jnp.float32)
    return (xf * lax.rsqrt(jnp.mean(xf * xf, axis=-1, keepdims=True) + EPS)).astype(x.dtype)

def spatial_gating(u, v, v_norm_g, w_spatial, b_spatial):
    b, s, _ = u.shape
    n_chunks = s // CHUNK
    u = u.reshape(b, n_chunks, CHUNK, GM_GROUPS, GM_DIM)
    v = v.reshape(b, n_chunks, CHUNK, GM_GROUPS, GM_DIM)
    v = rms_norm(v, v_norm_g.reshape(GM_GROUPS, GM_DIM))
    mask = jnp.tril(jnp.ones((CHUNK, CHUNK), dtype=bool))
    w = jnp.where(mask[None], w_spatial, jnp.zeros_like(w_spatial))
    mixed = jnp.einsum('gts,bcsgd->bctgd', w, v) + b_spatial.T[None, None, :, :, None]
    return u * mixed

def stick_breaking_attention(q, k, v):
    s_len = q.shape[2]
    scale = 1.0 / math.sqrt(SB_HEAD_DIM)
    outs = []
    for blk in range(s_len // Q_BLOCK):
        q0 = blk * Q_BLOCK
        k_end = q0 + Q_BLOCK
        qb = q[:, :, q0:k_end]
        kb = k[:, :, :k_end]
        vb = v[:, :, :k_end]
        z = jnp.einsum('bhtd,bhsd->bhts', qb, kb, preferred_element_type=jnp.float32) * scale
        t_idx = q0 + jnp.arange(Q_BLOCK)[:, None]
        s_idx = jnp.arange(k_end)[None, :]
        causal = s_idx < t_idx
        log_beta = jax.nn.log_sigmoid(z)
        log_1m = jnp.where(causal, jax.nn.log_sigmoid(-z), 0.0)
        cum = jnp.cumsum(log_1m, axis=-1)
        total = cum[..., -1:]
        log_a = log_beta + (total - cum)
        a = jnp.where(causal, jnp.exp(log_a), 0.0)
        outs.append(jnp.einsum('bhts,bhsd->bhtd', a.astype(vb.dtype), vb))
    return jnp.concatenate(outs, axis=2)

def mixer(xn, w_in, gm_v_norm_g, w_spatial, b_spatial, head_norm_g, w_out):
    b, s, _ = xn.shape
    proj = xn @ w_in
    u = jax.nn.gelu(proj[..., :GM_WIDTH])
    gv = jax.nn.gelu(proj[..., GM_WIDTH:2 * GM_WIDTH])
    qkv = proj[..., 2 * GM_WIDTH:].reshape(b, s, 3, SB_HEADS, SB_HEAD_DIM)
    q = qkv[:, :, 0].transpose(0, 2, 1, 3)
    k = qkv[:, :, 1].transpose(0, 2, 1, 3)
    v = qkv[:, :, 2].transpose(0, 2, 1, 3)
    a_out = head_rms(spatial_gating(u, gv, gm_v_norm_g, w_spatial, b_spatial)).reshape(b, s, GM_WIDTH)
    sb = stick_breaking_attention(q, k, v).transpose(0, 2, 1, 3)
    b_out = head_rms(sb).reshape(b, s, SB_WIDTH)
    merged = jnp.concatenate([a_out, b_out], axis=-1) * head_norm_g
    return merged @ w_out

def cross_attention(hn, mem_n, w_cq, w_ckv, w_co):
    b, s, _ = hn.shape
    m = mem_n.shape[1]
    q = (hn @ w_cq).reshape(b, s, X_HEADS, X_HEAD_DIM)
    kv = (mem_n @ w_ckv).reshape(b, m, 2, X_HEADS, X_HEAD_DIM)
    k, v = kv[:, :, 0], kv[:, :, 1]
    scores = jnp.einsum('bshd,bmhd->bhsm', q, k, preferred_element_type=jnp.float32) / math.sqrt(X_HEAD_DIM)
    p = jax.nn.softmax(scores, axis=-1)
    o = jnp.einsum('bhsm,bmhd->bshd', p.astype(v.dtype), v).reshape(b, s, D_MODEL)
    return o @ w_co

def sq_relu_mlp(hn, w_ff1, w_ff2):
    h = jax.nn.relu(hn @ w_ff1)
    return (h * h) @ w_ff2

def setup_inputs(seed: int = 0) -> dict:
    key = jax.random.key(seed)
    ks = jax.random.split(key, 20)
    f32 = jnp.float32

    def nrm(k, shape, scale):
        return jax.random.normal(k, shape, f32) * scale

    def gain(k, shape):
        return 1.0 + 0.02 * jax.random.normal(k, shape, f32)

    L = DEPTH
    return {
        "x": jax.random.normal(ks[0], (BATCH, SEQ, D_MODEL), f32),
        "mem": jax.random.normal(ks[1], (BATCH, N_MEM, D_MODEL), f32),
        "norm_mix_g": gain(ks[2], (L, D_MODEL)),
        "w_in": nrm(ks[3], (L, D_MODEL, IN_COLS), D_MODEL ** -0.5),
        "gm_v_norm_g": gain(ks[4], (L, GM_WIDTH)),
        "w_spatial": nrm(ks[5], (L, GM_GROUPS, CHUNK, CHUNK), 0.5 * CHUNK ** -0.5),
        "b_spatial": 1.0 + 0.01 * jax.random.normal(ks[6], (L, GM_GROUPS, CHUNK), f32),
        "head_norm_g": gain(ks[7], (L, D_MIX)),
        "w_out": nrm(ks[8], (L, D_MIX, D_MODEL), D_MIX ** -0.5),
        "norm_cross_g": gain(ks[9], (L, D_MODEL)),
        "norm_mem_g": gain(ks[10], (L, D_MODEL)),
        "w_cq": nrm(ks[11], (L, D_MODEL, D_MODEL), D_MODEL ** -0.5),
        "w_ckv": nrm(ks[12], (L, D_MODEL, 2 * D_MODEL), D_MODEL ** -0.5),
        "w_co": nrm(ks[13], (L, D_MODEL, D_MODEL), D_MODEL ** -0.5),
        "norm_ffn_g": gain(ks[14], (L, D_MODEL)),
        "w_ff1": nrm(ks[15], (L, D_MODEL, D_FF), D_MODEL ** -0.5),
        "w_ff2": nrm(ks[16], (L, D_FF, D_MODEL), D_FF ** -0.5),
        "norm_final_g": gain(ks[17], (D_MODEL,)),
    }

def reference(x, mem, norm_mix_g, w_in, gm_v_norm_g, w_spatial, b_spatial, head_norm_g, w_out,
              norm_cross_g, norm_mem_g, w_cq, w_ckv, w_co, norm_ffn_g, w_ff1, w_ff2, norm_final_g):
    h = x
    for l in range(DEPTH):
        xn = rms_norm(h, norm_mix_g[l])
        h = h + mixer(xn, w_in[l], gm_v_norm_g[l], w_spatial[l], b_spatial[l], head_norm_g[l], w_out[l])
        hn = rms_norm(h, norm_cross_g[l])
        mem_n = rms_norm(mem, norm_mem_g[l])
        h = h + cross_attention(hn, mem_n, w_cq[l], w_ckv[l], w_co[l])
        hn = rms_norm(h, norm_ffn_g[l])
        h = h + sq_relu_mlp(hn, w_ff1[l], w_ff2[l])
    return rms_norm(h, norm_final_g)


_drawn_inputs = setup_inputs


def setup_inputs(seed=0):
    import zlib

    import numpy as np

    out = dict(_drawn_inputs(seed))
    spreads = {}
    factors = {'norm_mix_g': 3.179,
     'gm_v_norm_g': 8.0,
     'b_spatial': 8.0,
     'head_norm_g': 3.79,
     'norm_cross_g': 8.0,
     'norm_mem_g': 8.0,
     'norm_ffn_g': 3.796,
     'norm_final_g': 2.864}
    for name, (base, spread) in spreads.items():
        noise = np.random.default_rng([zlib.crc32(name.encode()), seed]).standard_normal(out[name].shape)
        drawn = base * np.exp(spread * noise) if base else spread * noise
        out[name] = __import__('jax').numpy.asarray(drawn.astype(out[name].dtype))
    for name, factor in factors.items():
        out[name] = (out[name] * factor).astype(out[name].dtype)
    return out
```

```python
import concourse.bass as bass
from concourse import mybir
from concourse.alu_op_type import AluOpType as ALU
import numpy as np

F32 = mybir.dt.float32
F32R = mybir.dt.float32r
ACT = mybir.ActivationFunctionType
AX = mybir.AxisListType

P = 128
D = 1024
SEQ = 1024
TB = SEQ // P
KC = D // P
HALF = 512
GROUPS = 4
HEADS = 8
HD = 64
PAIRS = HEADS // 2
N_MEM = 256
MB = N_MEM // P
XH = 4
XD = D // XH
DFF = 4 * D
FG = DFF // HALF
EPS = 1e-6
Z_SCALE = HD ** -0.5
X_SCALE = XD ** -0.5
NEG = -1e30

COL_U, COL_GV, COL_Q, COL_K, COL_V = 0, 512, 1024, 1536, 2048

N_V = 0
N_QK = N_V + 8
N_GV = N_QK + 4 * PAIRS
N_U = N_GV + 8
N_OUT = N_U + 8
N_CQ = N_OUT + 16
N_CK = N_CQ + 16
N_CV = N_CK + 16
N_CO = N_CV + 16
N_FF = N_CO + 16
RAW_SLOTS = 4
WS_SLOTS = 8


def lo_on_vector(n):
    return N_GV + 4 <= n < N_CQ or N_CO + 8 <= n < N_FF


def lo_count(n):
    return sum(lo_on_vector(m) == lo_on_vector(n) for m in range(n + 1))


def used_count(n):
    def counted(m):
        if N_QK <= m < N_GV or N_CQ <= m < N_CV or m >= N_FF:
            return m % 2 == 0
        return m % 8 < 7
    return sum(counted(m) for m in range(n + 1))


def groups_before(s):
    head, tb = divmod(s, TB)
    return head * 12 + (tb if tb < 4 else 4 + 2 * (tb - 4))


def build(nc, x, mem, norm_mix_g, w_in, gm_v_norm_g, w_spatial, b_spatial, head_norm_g, w_out,
          norm_cross_g, norm_mem_g, w_cq, w_ckv, w_co, norm_ffn_g, w_ff1, w_ff2, norm_final_g, y):
    KB = 1024
    base = (nc.sbuf_base + 31) // 32 * 32
    A0 = base
    B0 = A0 + 64 * KB
    H0 = B0 + 64 * KB
    WS0 = H0 + 32 * KB
    RAW0 = WS0 + 32 * KB
    MISC0 = RAW0 + 8 * KB
    misc_at = [MISC0]

    def at(name, shape, dtype, offset):
        return nc.alloc_sbuf_tensor_at(name, shape, dtype, offset=offset)

    def misc(name, shape, dtype=F32):
        t = at(name, shape, dtype, misc_at[0])
        misc_at[0] += (4 * int(np.prod(shape[1:])) + 31) // 32 * 32
        return t

    AT_ = at("actA", [P, 2, KC, SEQ], F32R, A0)
    BT_ = at("actB", [P, 2, KC, SEQ], F32R, B0)
    XSA = at("stageA", [P, KC, SEQ], F32, A0 + 32 * KB)
    XSB = at("stageB", [P, KC, SEQ], F32, B0 + 32 * KB)
    H = at("h", [P, TB, D], F32, H0)
    WS = at("w_split", [P, WS_SLOTS, 2, HALF], F32R, WS0)
    RAW = at("w_raw", [P, RAW_SLOTS, HALF], F32, RAW0)

    VHL = at("v_parts", [P, TB, HEADS, 2 * HD], F32R, B0)
    O = at("attn_out", [P, TB, HALF], F32, B0 + 32 * KB)
    M_W = [896, 1024]
    BE_W = [640, 768, 896, 1024]
    MBUF = at("one_minus_beta", [P, sum(M_W)], F32, B0 + 48 * KB)
    NEGM = at("causal_neg", [P, P], F32, B0 + 48 * KB + 4 * sum(M_W))
    ATR = at("a_T", [P, 2, 2, HALF], F32R, B0 + 56 * KB)
    BEBUF = at("beta", [P, sum(BE_W)], F32, WS0 + 16 * KB)
    QKN = at("qk_next", [P, 2, 2, SEQ], F32R, H0)
    QKC = at("qk_now", [P, 2, 2, SEQ], F32R, H0 + 16 * KB)

    VN = at("v_norm", [P, 2, TB, HALF], F32R, B0)
    U = at("u_gated", [P, TB, HALF], F32, B0 + 48 * KB)
    WT = at("w_spatial_T", [P, 2, GROUPS, P], F32R, H0 + 16 * KB)
    WSP = at("w_spatial_masked", [P, GROUPS, P], F32, H0 + 20 * KB)
    GB = at("v_gain", [P, HALF], F32, H0 + 22 * KB)
    GV = at("gelu_v", [P, 2, HALF], F32, H0 + 24 * KB)
    SQ = at("squares", [P, HALF], F32, H0 + 28 * KB)
    ST = at("stats", [P, 2, 3, TB, HEADS], F32, H0 + 30 * KB)

    XM = [at("mem_tile0", [P, KC, P], F32, A0 + 7 * 4 * KB), at("mem_tile1", [P, KC, P], F32, A0 + 32 * KB + 7 * 4 * KB)]
    MEMT = at("mem_T", [P, 2, KC, N_MEM], F32R, B0)
    K2T = at("k2_T", [P, 2, KC, N_MEM], F32R, B0 + 16 * KB)
    V2 = at("v2", [P, 2, MB, D], F32R, B0 + 32 * KB)
    PT = [at("p_T0", [P, 2, MB, HALF], F32R, B0 + 48 * KB), at("p_T1", [P, 2, MB, HALF], F32R, B0)]
    EP = at("p_exp", [P, 2, 4, N_MEM], F32, B0 + 56 * KB)
    XST = at("softmax_stats", [P, 2, 4, 4], F32, B0 + 8 * KB)

    HID = at("hid_T", [P, 2, 4, SEQ], F32R, A0)
    W2S = at("w2_split", [P, 8, 2, HALF], F32R, A0 + 32 * KB)
    JUNK = at("junk", [P, D], F32, B0)
    YT = at("y_tiles", [P, TB, D], F32, B0 + 32 * KB)
    GF = at("final_gain", [P, D], F32, WS0)

    ident = misc("identity", [P, P])
    CG = misc("gains", [P, 5, KC])
    BSP = misc("b_sp", [P, GROUPS])
    SS = misc("row_sums", [P, TB])
    RS = misc("row_rstd", [P, TB])
    NEGH = misc("minus_half", [P, 8])
    G_MIX, G_HEAD, G_CROSS, G_MEM, G_FFN = range(5)

    PS = nc.alloc_psum_tensor("ps", [P, 8, HALF], F32)

    def f32(ap):
        return ap.bitcast(F32)

    S = {}

    def sem(name):
        S[name] = nc.alloc_semaphore(name)
        return S[name]

    raw_in = [sem(f"raw_in{i}") for i in range(RAW_SLOTS)]
    w_hi = sem("w_hi")
    w_lo_pool = sem("w_lo_pool")
    w_lo_dve = sem("w_lo_dve")
    w_used = sem("w_used")
    const_in = sem("const_in")
    const_made = sem("const_made")
    x_in = [sem(f"x_in{t}") for t in range(TB)]

    class Norm:
        def __init__(self, name):
            self.squared = sem(name + "_squared")
            self.mean = sem(name + "_mean")
            self.rstd = sem(name + "_rstd")
            self.scaled = sem(name + "_scaled")
            self.turned = sem(name + "_turned")
            self.hi = sem(name + "_hi")
            self.lo = sem(name + "_lo")

    n_x, n_h1, n_mem, n_h2, n_fin = (Norm(n) for n in ("x", "h1", "mem", "h2", "fin"))

    v_done, v_hi, v_lo = sem("v_done"), sem("v_hi"), sem("v_lo")
    proj_done, qk_hi, qk_lo, qk_now = sem("proj_done"), sem("qk_hi"), sem("qk_lo"), sem("qk_now_ready")
    z_done, z_masked, sig, scanned, a_done = sem("z_done"), sem("z_masked"), sem("sig"), sem("scanned"), sem("a_done")
    t_done, at_hi, at_lo, pv_done, o_done = sem("t_done"), sem("at_hi"), sem("at_lo"), sem("pv_done"), sem("o_done")

    wsp_in, wsp_masked, wt_turned, wt_hi, wt_lo = (sem(n) for n in ("wsp_in", "wsp_masked", "wt_turned", "wt_hi", "wt_lo"))
    gb_in = sem("gb_in")
    gv_done, gv_gelu, gv_squared, gv_summed, gv_mean, gv_rstd = (sem("gv_" + n) for n in ("done", "gelu", "squared", "summed", "mean", "rstd"))
    gv_gained, gv_scaled, vn_hi, vn_lo = sem("gv_gained"), sem("gv_scaled"), sem("vn_hi"), sem("vn_lo")
    os_squared, os_summed, os_mean, os_rstd, os_scaled = (sem("o_" + n) for n in ("squared", "summed", "mean", "rstd", "scaled"))
    u_done, u_gelu, mix_done, gated = sem("u_done"), sem("u_gelu"), sem("mix_done"), sem("gated")
    a_squared, a_summed, a_mean, a_rstd, a_scaled = (sem("a_" + n) for n in ("squared", "summed", "mean", "rstd", "scaled"))
    mt_turned, mt_hi, mt_lo = sem("mt_turned"), sem("mt_hi"), sem("mt_lo")
    x2_in = [sem(f"x_again{t}") for t in range(TB)]
    wout_done, wout_added = sem("wout_done"), sem("wout_added")

    q2_done, q2_hi, q2_lo = sem("q2_done"), sem("q2_hi"), sem("q2_lo")
    mem_in = sem("mem_in")
    k2_done, k2_hi, k2_lo = sem("k2_done"), sem("k2_hi"), sem("k2_lo")
    v2_done, v2_hi, v2_lo = sem("v2_done"), sem("v2_hi"), sem("v2_lo")
    xs_done, xs_max, xs_neg, xs_exp, xs_inv, xs_prob = (sem("xs_" + n) for n in ("done", "max", "neg", "exp", "inv", "prob"))
    xt_done, xt_hi, xt_lo, xo_done, xo_hi, xo_lo = (sem(n) for n in ("xt_done", "xt_hi", "xt_lo", "xo_done", "xo_hi", "xo_lo"))
    down_done, down_added = sem("down_done"), sem("down_added")

    ff1_done, ff_relu, ff_sq, hid_hi, hid_lo = (sem(n) for n in ("ff1_done", "ff_relu", "ff_sq", "hid_hi", "hid_lo"))
    gf_in, y_made, y_out = sem("gf_in"), sem("y_made"), sem("y_out")

    def wait_lo(eng, n, more=0):
        eng.wait_ge(w_lo_dve if lo_on_vector(n) else w_lo_pool, lo_count(n) + more)

    def tok(tb, n=1):
        return slice(tb * P, (tb + n) * P)

    def xs(stage, tb):
        return stage[:, :, tok(tb)]

    def split_hi(out, src, gain=None):
        if gain is None:
            return nc.scalar.activation(out, src, ACT.Copy)
        return nc.scalar.activation(out, src, ACT.Copy, scale=gain)

    def split_lo(out, src, hi, gain=None):
        if gain is None:
            return nc.vector.tensor_tensor(out, src, f32(hi), ALU.subtract)
        return nc.vector.scalar_tensor_tensor(out, src, gain, f32(hi), ALU.mult, ALU.subtract)

    def freed(n):
        if n < N_QK:
            return (w_used, used_count(n)) if n < 7 else (v_done, TB)
        if n < N_GV:
            pair, j = divmod(n - N_QK, 4)
            return (w_used, used_count(n)) if j % 2 == 0 else (proj_done, 4 * pair + j + 1)
        for first, done in ((N_GV, gv_done), (N_U, u_done), (N_OUT, wout_done), (N_OUT + 8, wout_done), (N_CO, down_done), (N_CO + 8, down_done)):
            if first <= n < first + 8:
                second = first in (N_OUT + 8, N_CO + 8)
                return (w_used, used_count(n)) if n < first + 7 else (done, TB * (1 + second))
        if n < N_CV:
            m, kh = divmod((n - N_CQ) % 16, 2)
            if kh == 0:
                return w_used, used_count(n)
            return (q2_done, 2 * m + 2) if n < N_CK else (k2_done, m + 1)
        if n < N_CO:
            c, k = divmod(n - N_CV, 8)
            return (w_used, used_count(n)) if k < 7 else (v2_done, MB * (c + 1))
        f, kh = divmod(n - N_FF, 2)
        return (w_used, used_count(n)) if kh == 0 else (ff1_done, 2 * f + 2)

    def place_free(n):
        if n < WS_SLOTS:
            return None
        if n < N_QK + 4:
            return freed(n - 8)
        if n < N_GV + 4:
            return freed(n - 4)
        if n < N_GV + 8:
            return t_done, 24 * PAIRS
        return freed(n - 8)

    def weight_hi(act, n):
        act.wait_ge(raw_in[n % 4], 16 * (n // 4 + 1))
        free = place_free(n)
        if free:
            act.wait_ge(*free)
        split_hi(WS[:, n % 8 if not N_QK <= n < N_GV else n % 4, 0, :], RAW[:, n % 4, :]).then_inc(w_hi, 1)

    def weight_lo(eng, n):
        eng.wait_ge(w_hi, n + 1)
        place = n % 8 if not N_QK <= n < N_GV else n % 4
        return eng.tensor_tensor(WS[:, place, 1, :], RAW[:, n % 4, :], f32(WS[:, place, 0, :]), ALU.subtract).then_inc(
            w_lo_dve if lo_on_vector(n) else w_lo_pool, 1)

    def cols_of(w, k, c):
        return w[k * P:(k + 1) * P, c:c + HALF]

    def unit_of(w, kh, c):
        return w.rearrange("(k p) n -> p k n", p=P)[:, 4 * kh:4 * kh + 4, bass.ds(c, P)]

    block = nc.Block()
    with block:
        @block.sync
        def _(sp):
            def load(n, src, more=0, unit=False):
                if n >= RAW_SLOTS:
                    wait_lo(sp, n - RAW_SLOTS, more)
                dst = RAW[:, n % 4, :]
                if unit:
                    dst = dst.rearrange("p (k n) -> p k n", k=4)
                sp.dma_start(dst, src).then_inc(raw_in[n % 4], 16)

            for k in range(KC):
                load(N_V + k, cols_of(w_in, k, COL_V))
            for j in range(4):
                load(N_QK + j, unit_of(w_in, j % 2, COL_Q if j < 2 else COL_K), unit=True)
            with sp.Fori(0, PAIRS - 1) as i:
                for j in range(4):
                    load(N_QK + 4 + j, unit_of(w_in, j % 2, (COL_Q if j < 2 else COL_K) + P + P * i), 4 * i, True)
            for k in range(KC):
                load(N_GV + k, cols_of(w_in, k, COL_GV))
            for k in range(KC):
                load(N_U + k, cols_of(w_in, k, COL_U))
            for c in range(2):
                for k in range(KC):
                    load(N_OUT + 8 * c + k, cols_of(w_out, k, c * HALF))
            for j in range(4):
                load(N_CQ + j, unit_of(w_cq, j % 2, (j // 2) * P), unit=True)
            with sp.Fori(0, 3) as i:
                for j in range(4):
                    load(N_CQ + 4 + j, unit_of(w_cq, j % 2, (2 + j // 2) * P + 2 * P * i), 4 * i, True)
            with sp.Fori(0, 4) as i:
                for j in range(4):
                    load(N_CK + j, unit_of(w_ckv, j % 2, (j // 2) * P + 2 * P * i), 4 * i, True)
            for c in range(2):
                for k in range(KC):
                    load(N_CV + 8 * c + k, cols_of(w_ckv, k, D + c * HALF))
            for c in range(2):
                for k in range(KC):
                    load(N_CO + 8 * c + k, cols_of(w_co, k, c * HALF))

            def ff2_slots(g):
                for j in range(8):
                    load(N_FF + 8 + j, w_ff2[bass.ds(g * HALF + (j % 4) * P, P), (j // 4) * HALF:(j // 4 + 1) * HALF], 16 * g)

            for j in range(8):
                load(N_FF + j, unit_of(w_ff1, j % 2, (j // 2) * P), unit=True)
            with sp.Fori(0, FG - 1) as g:
                ff2_slots(g)
                for j in range(8):
                    load(N_FF + 16 + j, unit_of(w_ff1, j % 2, HALF + g * HALF + (j // 2) * P), 16 * g, True)
            ff2_slots(FG - 1)
            for tb in range(TB):
                sp.wait_ge(y_made, tb + 1)
                sp.dma_start(y[tok(tb), :], YT[:, tb, :]).then_inc(y_out, 16)
            sp.wait_ge(y_out, 16 * TB)

        @block.gpsimd
        def _(pool):
            pool.memset(ident[:, :], 0.0).then_inc(const_made, 1)
            pool.memset(NEGH[:, :], -0.5).then_inc(const_made, 1)
            pool.memset(NEGM[:, :], 0.0).then_inc(const_made, 1)
            pool.wait_ge(const_made, 3)
            pool.affine_select(out=ident[:, :], in_=ident[:, :], compare_op=ALU.not_equal, fill=1.0, base=0,
                               pattern=[[-1, P]], channel_multiplier=1).then_inc(const_made, 1)
            pool.affine_select(out=NEGM[:, :], in_=NEGM[:, :], compare_op=ALU.is_gt, fill=NEG, base=0,
                               pattern=[[-1, P]], channel_multiplier=1).then_inc(const_made, 1)

            def row_rstd(norm, tb, width=D, src=SS, dst=RS):
                pool.wait_ge(norm.squared, tb + 1)
                pool.tensor_scalar(dst[:, tb:tb + 1], src[:, tb:tb + 1], 1.0 / width, EPS, ALU.mult, ALU.add).then_inc(norm.mean, 1)
                pool.wait_ge(norm.mean, tb + 1)
                pool.tensor_tensor(dst[:, tb:tb + 1], dst[:, tb:tb + 1], NEGH[:, 0:1], ALU.pow).then_inc(norm.rstd, 1)

            row_rstd(n_x, 0)
            for k in range(KC):
                weight_lo(pool, N_V + k)
                if k in (0, 3):
                    row_rstd(n_x, 1 if k == 0 else 2)
            for tb in range(3, TB):
                row_rstd(n_x, tb)
            for j in range(4):
                weight_lo(pool, N_QK + j)

            def weigh(u, s):
                tb = s % TB
                w = (tb + 1) * P
                m0, b0 = sum(M_W[:s % 2]), sum(BE_W[:s % 4])
                pool.wait_ge(scanned, u + 1)
                pool.wait_ge(sig, 2 * u + 2)
                pool.tensor_tensor(BEBUF[:, b0:b0 + w - 1], BEBUF[:, b0:b0 + w - 1], MBUF[:, m0 + 1:m0 + w], ALU.mult).then_inc(a_done, 1)

            for u in range(1, 4):
                weigh(u - 1, u - 1)
            with pool.Fori(0, PAIRS - 1) as i:
                for t in range(16):
                    weigh(16 * i + 3 + t, (3 + t) % 16)
                    if t < 2:
                        for j in (2 * t, 2 * t + 1):
                            pool.wait_ge(w_hi, N_QK + 4 + j + 1 + 4 * i)
                            pool.tensor_tensor(WS[:, j, 1, :], RAW[:, j, :], f32(WS[:, j, 0, :]), ALU.subtract).then_inc(w_lo_pool, 1)
            for t in range(12 + 1):
                weigh(16 * (PAIRS - 1) + 3 + t, (3 + t) % 16)
                if t < 4:
                    weight_lo(pool, N_GV + t)

            pool.wait_ge(wsp_in, 16)
            pool.affine_select(out=WSP[:, :, :], in_=WSP[:, :, :], compare_op=ALU.is_ge, fill=0.0, base=0,
                               pattern=[[0, GROUPS], [-1, P]], channel_multiplier=1).then_inc(wsp_masked, 1)

            def group_rstd(which, tb, n, width, summed, mean, rstd):
                pool.wait_ge(summed, tb + 1)
                s, r = ST[:, 0, which, tb, 0:n], ST[:, 1, which, tb, 0:n]
                pool.tensor_scalar(r, s, 1.0 / width, EPS, ALU.mult, ALU.add).then_inc(mean, 1)
                pool.wait_ge(mean, tb + 1)
                pool.tensor_tensor(r, r, NEGH[:, 0:n], ALU.pow).then_inc(rstd, 1)

            for tb in range(TB):
                group_rstd(1, tb, HEADS, HD, os_summed, os_mean, os_rstd)
                group_rstd(0, tb, GROUPS, P, gv_summed, gv_mean, gv_rstd)
            for tb in range(TB):
                group_rstd(2, tb, GROUPS, P, a_summed, a_mean, a_rstd)
            for tb in range(TB):
                if tb == TB - 1:
                    for n in range(N_CQ, N_CQ + 4):
                        weight_lo(pool, n)
                row_rstd(n_h1, tb)
            for n in range(N_CQ + 4, N_CQ + 8):
                weight_lo(pool, n)
            for mt in range(MB):
                row_rstd(n_mem, mt)
            for n in range(N_CQ + 8, N_CO + 8):
                weight_lo(pool, n)
            for tb in range(TB - 1):
                row_rstd(n_h2, tb)

            def ff_lo(j, more, dst):
                pool.wait_ge(w_hi, N_FF + j + 1 + more)
                pool.tensor_tensor(dst[:, j % 8, 1, :], RAW[:, j % 4, :], f32(dst[:, j % 8, 0, :]), ALU.subtract).then_inc(w_lo_pool, 1)

            for j in range(8):
                if j == 4:
                    row_rstd(n_h2, TB - 1)
                ff_lo(j, 0, WS)
            with pool.Fori(0, FG - 1) as g:
                for j in range(8, 16):
                    ff_lo(j, 16 * g, W2S)
                for j in range(16, 24):
                    ff_lo(j, 16 * g, WS)
            for j in range(8, 16):
                ff_lo(j, 16 * (FG - 1), W2S)
            for tb in range(TB):
                row_rstd(n_fin, tb)

        @block.scalar
        def _(act):
            for tb in range(2):
                act.dma_start(xs(XSA, tb), x[tok(tb), :].rearrange("p (k n) -> p k n", k=KC)).then_inc(x_in[tb], 16)
            for g, src in enumerate((norm_mix_g, head_norm_g, norm_cross_g, norm_mem_g, norm_ffn_g)):
                act.dma_start(CG[:, g, :], src.rearrange("(k p) -> p k", p=P)).then_inc(const_in, 16)
            act.dma_start(BSP[:, :], b_spatial.rearrange("g t -> t g")).then_inc(const_in, 16)
            for tb in range(2, TB):
                act.dma_start(xs(XSA, tb), x[tok(tb), :].rearrange("p (k n) -> p k n", k=KC)).then_inc(x_in[tb], 16)

            def evac_turned(norm, tb, dst, gain, count0=0):
                for b in range(2):
                    act.wait_ge(norm.turned, 2 * tb + b + 1)
                    for k in range(4 * b, 4 * b + 4):
                        last = split_hi(dst[:, 0, k, tok(tb)], PS[:, 2 + b, tok(k % 4)], CG[:, gain, k:k + 1])
                    last.then_inc(norm.hi, 1)

            def square_x(tb):
                act.wait_ge(x_in[tb], 16)
                nc.scalar.activation(H[:, tb, :].rearrange("p (k n) -> p k n", k=KC), xs(XSA, tb), ACT.Square,
                                     accum_out=SS[:, tb:tb + 1]).then_inc(n_x.squared, 1)

            def evac_v(tb):
                act.wait_ge(v_done, tb + 1)
                split_hi(VHL[:, tb, :, 0:HD], PS[:, tb % 2, :].rearrange("p (h d) -> p h d", h=HEADS)).then_inc(v_hi, 1)

            square_x(0)
            weight_hi(act, N_V)
            act.wait_ge(const_in, 6 * 16)
            square_x(1)
            for k in range(1, KC):
                weight_hi(act, N_V + k)
                if k == 3:
                    evac_turned(n_x, 0, AT_, G_MIX)
                    square_x(2)
            for tb in range(1, TB):
                evac_turned(n_x, tb, AT_, G_MIX)
                if tb + 2 < TB:
                    square_x(tb + 2)
                evac_v(tb - 1)
            for j in range(4):
                weight_hi(act, N_QK + j)
            evac_v(TB - 1)

            def evac_proj(j, i4, now_count):
                act.wait_ge(proj_done, i4 + j + 1)
                if now_count is not None:
                    act.wait_ge(qk_now, now_count)
                split_hi(QKN[:, j // 2, 0, (j % 2) * HALF:(j % 2 + 1) * HALF], PS[:, 7, :]).then_inc(qk_hi, 1)

            for j in range(4):
                evac_proj(j, 0, None)

            def attn_a_hi(u, s, g24):
                tb = s % TB
                for g in range(1 if tb < 4 else 2):
                    n = min(4, tb + 1 - 4 * g) * P
                    count = groups_before(s) + g + 1 + g24
                    act.wait_ge(t_done, count)
                    if g == 0 and not (isinstance(u, int) and u == 0):
                        act.wait_ge(pv_done, u)
                    split_hi(ATR[:, g, 0, 0:n], PS[:, 4 + g, 0:n]).then_inc(at_hi, 1)

            def sigmoids(u, s):
                tb = s % TB
                w = (tb + 1) * P
                z0 = 2 * (s % 2)
                m0, b0 = sum(M_W[:s % 2]), sum(BE_W[:s % 4])
                zp = PS[:, z0:z0 + 2, :].rearrange("p b n -> p (b n)")[:, 0:w]
                act.wait_ge(z_masked, u + 1)
                if not (isinstance(u, int) and u < 2):
                    act.wait_ge(a_done, u - 1)
                nc.scalar.activation(MBUF[:, m0:m0 + w], zp, ACT.Sigmoid, scale=-Z_SCALE).then_inc(sig, 1)
                nc.scalar.activation(BEBUF[:, b0:b0 + w], zp, ACT.Sigmoid, scale=Z_SCALE).then_inc(sig, 1)

            act.wait_ge(v_lo, TB)
            for u in range(4):
                if u >= 3:
                    attn_a_hi(u - 3, u - 3, 0)
                sigmoids(u, u)
            with act.Fori(0, PAIRS - 1) as i:
                for t in range(16):
                    s = 1 + t
                    attn_a_hi(16 * i + s, s % 16, 24 * i + 24 * (s // 16))
                    if t < 2:
                        for j in (2 * t, 2 * t + 1):
                            act.wait_ge(raw_in[j], 16 * (N_QK // 4 + 2) + 16 * i)
                            if j % 2 == 0:
                                act.wait_ge(w_used, used_count(N_QK + j) + 2 * i)
                            else:
                                act.wait_ge(proj_done, 4 * i + j + 1)
                            split_hi(WS[:, j, 0, :], RAW[:, j, :]).then_inc(w_hi, 1)
                    if t in (2, 4, 7, 10):
                        j = (2, 4, 7, 10).index(t)
                        evac_proj(j, 4 * i + 4, i + 1)
                    sigmoids(16 * i + 4 + t, (4 + t) % 16)
            for t in range(12 + 3):
                s = 1 + t
                last = PAIRS - 1
                attn_a_hi(16 * last + s, s, 24 * last)
                if t < 4:
                    weight_hi(act, N_GV + t)
                if t < 12:
                    sigmoids(16 * last + 4 + t, 4 + t)
            act.wait_ge(z_done, 16 * PAIRS)
            act.dma_start(WSP[:, :, :], w_spatial.rearrange("g t s -> t g s")).then_inc(wsp_in, 16)
            act.dma_start(GB[:, :], gm_v_norm_g.rearrange("(a n) -> a n", a=1).to_broadcast([P, HALF])).then_inc(gb_in, 16)
            for tb in range(4):
                act.dma_start(H[:, tb, :], x[tok(tb), :]).then_inc(x2_in[tb], 16)
            for k in range(4, KC):
                weight_hi(act, N_GV + k)

            def square_o(tb):
                act.wait_ge(o_done, 16 * PAIRS)
                if tb:
                    act.wait_ge(gv_summed, tb)
                nc.scalar.activation(SQ[:, :], O[:, tb, :], ACT.Square).then_inc(os_squared, 1)

            def gelu_v(tb):
                act.wait_ge(gv_done, tb + 1)
                if tb >= 2:
                    act.wait_ge(vn_lo, tb - 1)
                nc.scalar.activation(GV[:, tb % 2, :], PS[:, tb % 2, :], ACT.Gelu_apprx_tanh).then_inc(gv_gelu, 1)

            def square_v(tb):
                act.wait_ge(gv_gelu, tb + 1)
                act.wait_ge(os_summed, tb + 1)
                nc.scalar.activation(SQ[:, :], GV[:, tb % 2, :], ACT.Square).then_inc(gv_squared, 1)

            def hi_v(tb):
                act.wait_ge(gv_scaled, tb + 1)
                split_hi(VN[:, 0, tb, :], GV[:, tb % 2, :]).then_inc(vn_hi, 1)

            for tb in range(TB):
                if tb == 2:
                    act.wait_ge(wt_turned, 1)
                    split_hi(WT[:, 0, :, :], PS[:, 2, :].rearrange("p (g t) -> p g t", g=GROUPS)).then_inc(wt_hi, 1)
                if tb == TB - 1:
                    for k in range(KC):
                        weight_hi(act, N_U + k)
                square_o(tb)
                gelu_v(tb)
                square_v(tb)
                hi_v(tb)

            def gelu_u(tb):
                act.wait_ge(u_done, tb + 1)
                nc.scalar.activation(U[:, tb, :], PS[:, tb % 2, :], ACT.Gelu_apprx_tanh).then_inc(u_gelu, 1)

            def evac_merged(i, tb, half):
                act.wait_ge(mt_turned, i + 1)
                for k in range(4):
                    last = split_hi(AT_[:, 0, 4 * half + k, tok(tb)], PS[:, 2 + i % 2, tok(k)],
                                    CG[:, G_HEAD, 4 * half + k:4 * half + k + 1])
                last.then_inc(mt_hi, 1)

            def square_a(tb):
                act.wait_ge(gated, 4 * (tb // 4 + 1))
                act.wait_ge(a_summed if tb else gv_summed, tb or TB)
                nc.scalar.activation(SQ[:, :], U[:, tb, :], ACT.Square).then_inc(a_squared, 1)

            gelu_u(0)
            gelu_u(1)
            evac_merged(0, 0, 1)
            gelu_u(2)
            evac_merged(1, 1, 1)
            gelu_u(3)
            evac_merged(2, 2, 1)
            gelu_u(4)
            evac_merged(3, 3, 1)
            for tb in range(4):
                square_a(tb)
            gelu_u(5)
            evac_merged(4, 4, 1)
            evac_merged(5, 0, 0)
            gelu_u(6)
            evac_merged(6, 5, 1)
            evac_merged(7, 1, 0)
            for k in range(KC):
                weight_hi(act, N_OUT + k)
            gelu_u(7)
            evac_merged(8, 6, 1)
            evac_merged(9, 2, 0)
            evac_merged(10, 7, 1)
            evac_merged(11, 3, 0)
            for tb in range(4, TB):
                square_a(tb)
            act.wait_ge(a_scaled, TB)
            for tb in range(4, TB):
                act.dma_start(H[:, tb, :], x[tok(tb), :]).then_inc(x2_in[tb], 16)
            for tb in range(4, TB):
                evac_merged(8 + tb, tb, 0)
            for k in range(KC):
                weight_hi(act, N_OUT + 8 + k)

            def square_h(norm, tb, added, count):
                act.wait_ge(added, count)
                nc.scalar.activation(xs(XSB, tb), H[:, tb, :].rearrange("p (k n) -> p k n", k=KC), ACT.Square,
                                     accum_out=SS[:, tb:tb + 1]).then_inc(norm.squared, 1)

            act.wait_ge(mt_lo, 16)
            for tb in range(TB):
                if tb >= 3:
                    evac_turned(n_h1, tb - 3, BT_, G_CROSS)
                square_h(n_h1, tb, wout_added, TB + tb + 1)
                if tb == TB - 2:
                    for k in range(KC):
                        weight_hi(act, N_CQ + k)
            for tb in range(TB - 3, TB):
                evac_turned(n_h1, tb, BT_, G_CROSS)

            act.wait_ge(wout_done, 2 * TB)
            for mt in range(MB):
                act.dma_start(XM[mt][:, :, :], mem[tok(mt), :].rearrange("p (k n) -> p k n", k=KC)).then_inc(mem_in, 16)
            act.wait_ge(mem_in, 16 * MB)
            act.wait_ge(n_h1.scaled, TB)
            for mt in range(MB):
                act.wait_ge(wout_added, 2 * TB)
                if mt:
                    act.wait_ge(n_mem.squared, mt)
                nc.scalar.activation(PS[:, 0:2, :].rearrange("p b (k n) -> p (b k) n", k=4), XM[mt][:, :, :], ACT.Square,
                                     accum_out=SS[:, mt:mt + 1]).then_inc(n_mem.squared, 1)

            def evac_q2(m, j, i8):
                for f in range(2):
                    act.wait_ge(q2_done, 2 * j + f + 1 + i8)
                    split_hi(AT_[:, 0, m, f * HALF:(f + 1) * HALF], PS[:, 4 + 2 * (j % 2) + f, :]).then_inc(q2_hi, 1)

            for j in range(4):
                evac_q2(j, j, 0)
                for k in (2 * j, 2 * j + 1):
                    weight_hi(act, N_CQ + 8 + k)
            for j in range(4):
                if j == 3:
                    act.wait_ge(n_mem.turned, 2 * MB)
                    for mt in range(MB):
                        for b in range(2):
                            for k in range(4 * b, 4 * b + 4):
                                last = split_hi(MEMT[:, 0, k, tok(mt)], PS[:, 2 * mt + b, tok(k % 4)], CG[:, G_MEM, k:k + 1])
                            last.then_inc(n_mem.hi, 1)
                evac_q2(4 + j, j, 8)
                for k in (2 * j, 2 * j + 1):
                    weight_hi(act, N_CK + k)

            for m in range(KC):
                act.wait_ge(k2_done, m + 1)
                split_hi(K2T[:, 0, m, :], PS[:, 4 + m % 4, 0:N_MEM]).then_inc(k2_hi, 1)
                for k in (2 * m, 2 * m + 1):
                    weight_hi(act, N_CK + 8 + k)
            for c in range(2):
                for mb in range(MB):
                    if mb == MB - 1:
                        for k in range(KC):
                            weight_hi(act, (N_CV + 8 if c == 0 else N_CO) + k)
                    act.wait_ge(v2_done, MB * c + mb + 1)
                    split_hi(V2[:, 0, mb, c * HALF:(c + 1) * HALF], PS[:, mb, :]).then_inc(v2_hi, 1)

            def x_exp(v):
                act.wait_ge(xs_neg, v + 1)
                if v >= 2:
                    act.wait_ge(xt_done, 2 * (v - 1))
                for q in range(4):
                    nc.scalar.activation(EP[:, v % 2, q, :], PS[:, 2 * (v % 2) + q // 2, (q % 2) * N_MEM:(q % 2 + 1) * N_MEM], ACT.Exp,
                                         bias=XST[:, v % 2, 1, q:q + 1], scale=X_SCALE,
                                         accum_out=XST[:, v % 2, 2, q:q + 1]).then_inc(xs_exp, 1)

            def x_t_hi(v):
                for mb in range(MB):
                    act.wait_ge(xt_done, 2 * v + mb + 1)
                    if v >= 2:
                        act.wait_ge(xo_done, 2 * (v - 1))
                    split_hi(PT[v % 2][:, 0, mb, :], PS[:, 4 + mb, :]).then_inc(xt_hi, 1)

            def x_o_hi(v):
                h, f = divmod(v, 2)
                for d in range(2):
                    act.wait_ge(xo_done, 2 * v + d + 1)
                    split_hi(AT_[:, 0, 2 * h + d, f * HALF:(f + 1) * HALF], PS[:, 6 + d, :]).then_inc(xo_hi, 1)

            for v in range(2 * XH + 3):
                if v >= 3:
                    x_o_hi(v - 3)
                if 2 <= v < 2 * XH + 2:
                    x_t_hi(v - 2)
                if v < 2 * XH:
                    x_exp(v)

            act.wait_ge(xo_lo, 4 * XH)
            for tb in range(TB):
                if tb >= 3:
                    evac_turned(n_h2, tb - 3, BT_, G_FFN)
                if tb == 0:
                    for k in range(KC):
                        weight_hi(act, N_CO + 8 + k)
                square_h(n_h2, tb, down_added, TB + tb + 1)
                if tb == TB - 2:
                    for k in range(KC):
                        weight_hi(act, N_FF + k)
            for tb in range(TB - 3, TB):
                evac_turned(n_h2, tb, BT_, G_FFN)

            def ff_hi(j, more, dst):
                act.wait_ge(raw_in[j % 4], 16 * ((N_FF + j) // 4 + 1) + more)
                split_hi(dst[:, j % 8, 0, :], RAW[:, j % 4, :]).then_inc(w_hi, 1)

            def relu_square(g8, f):
                for half in range(2):
                    b = 4 + 2 * (f % 2) + half
                    act.wait_ge(ff_relu, g8 + 2 * f + half + 1)
                    nc.scalar.activation(PS[:, b, :], PS[:, b, :], ACT.Square).then_inc(ff_sq, 1)
                    act.wait_ge(ff_sq, g8 + 2 * f + half + 1)
                    split_hi(HID[:, 0, f, half * HALF:(half + 1) * HALF], PS[:, b, :]).then_inc(hid_hi, 1)

            def ff_group(g):
                for f in range(4):
                    for j in (8 + 2 * f, 9 + 2 * f):
                        if j == 8:
                            act.wait_ge(down_done, 2 * TB + 2 * TB * g)
                        ff_hi(j, 64 * g, W2S)
                    relu_square(8 * g, f)

            act.wait_ge(down_done, 2 * TB)
            with act.Fori(0, FG - 1) as g:
                ff_group(g)
                for j in range(16, 24):
                    sem_free, count = freed(N_FF + j - 16)
                    act.wait_ge(sem_free, count + (4 * g if j % 2 == 0 else 8 * g))
                    ff_hi(j, 64 * g, WS)
            ff_group(FG - 1)
            act.wait_ge(ff1_done, 8 * FG)
            act.dma_start(GF[:, :], norm_final_g.rearrange("(a n) -> a n", a=1).to_broadcast([P, D])).then_inc(gf_in, 16)
            for tb in range(TB):
                act.wait_ge(down_added, 2 * TB * FG + 2 * tb + 2)
                if tb:
                    act.wait_ge(n_fin.squared, tb)
                nc.scalar.activation(JUNK[:, :], H[:, tb, :], ACT.Square, accum_out=SS[:, tb:tb + 1]).then_inc(n_fin.squared, 1)

        @block.vector
        def _(dve):
            def scale_rows(norm, tb, dst, src):
                dve.wait_ge(norm.rstd, tb + 1)
                nc.vector.tensor_scalar(dst, src, RS[:, tb:tb + 1], None, ALU.mult).then_inc(norm.scaled, 1)

            def lo_turned(norm, tb, dst, gain):
                for b in range(2):
                    dve.wait_ge(norm.hi, 2 * tb + b + 1)
                    for k in range(4 * b, 4 * b + 4):
                        last = split_lo(dst[:, 1, k, tok(tb)], PS[:, 2 + b, tok(k % 4)], dst[:, 0, k, tok(tb)], CG[:, gain, k:k + 1])
                    last.then_inc(norm.lo, 1)

            def lo_v(tb):
                dve.wait_ge(v_hi, tb + 1)
                nc.vector.tensor_tensor(VHL[:, tb, :, HD:2 * HD], PS[:, tb % 2, :].rearrange("p (h d) -> p h d", h=HEADS),
                                        f32(VHL[:, tb, :, 0:HD]), ALU.subtract).then_inc(v_lo, 1)

            for tb in range(2):
                scale_rows(n_x, tb, xs(XSA, tb), xs(XSA, tb))
            dve.wait_ge(const_in, 6 * 16)
            for tb in range(TB):
                lo_turned(n_x, tb, AT_, G_MIX)
                if tb + 2 < TB:
                    scale_rows(n_x, tb + 2, xs(XSA, tb + 2), xs(XSA, tb + 2))
                if tb:
                    lo_v(tb - 1)
            lo_v(TB - 1)

            def lo_proj(j, i4):
                dve.wait_ge(qk_hi, i4 + j + 1)
                half = slice((j % 2) * HALF, (j % 2 + 1) * HALF)
                split_lo(QKN[:, j // 2, 1, half], PS[:, 7, :], QKN[:, j // 2, 0, half]).then_inc(qk_lo, 1)

            def take_qk(i, first=False):
                if not first:
                    dve.wait_ge(z_done, 16 * i)
                dve.wait_ge(qk_lo, 4 * i + 4)
                nc.vector.tensor_copy(QKC[:, :, :, :], QKN[:, :, :, :]).then_inc(qk_now, 1)

            for j in range(4):
                lo_proj(j, 0)
            take_qk(0, first=True)

            def scan(u, s):
                w = (s % TB + 1) * P
                m0 = sum(M_W[:s % 2])
                dve.wait_ge(sig, 2 * u + 1)
                m = MBUF[:, m0:m0 + w][:, ::-1]
                nc.vector.tensor_tensor_scan(m, m, m, 1.0, ALU.mult, ALU.bypass).then_inc(scanned, 1)

            def sum_o(u, s, head):
                dve.wait_ge(pv_done, u + 1)
                nc.vector.tensor_reduce(O[:, s % TB, bass.ds(head * HD, HD)], PS[:, 6, 0:2 * HD].rearrange("p (a d) -> p d a", a=2),
                                        AX.X, ALU.add).then_inc(o_done, 1)

            def lo_a(s, g24):
                tb = s % TB
                for g in range(1 if tb < 4 else 2):
                    n = min(4, tb + 1 - 4 * g) * P
                    dve.wait_ge(at_hi, groups_before(s) + g + 1 + g24)
                    split_lo(ATR[:, g, 1, 0:n], PS[:, 4 + g, 0:n], ATR[:, g, 0, 0:n]).then_inc(at_lo, 1)

            def mask(u, s):
                tb = s % TB
                b, c = 2 * (s % 2) + tb // 4, (tb % 4) * P
                dve.wait_ge(z_done, u + 1)
                nc.vector.tensor_tensor(PS[:, b, c:c + P], PS[:, b, c:c + P], NEGM[:, :], ALU.add).then_inc(z_masked, 1)

            dve.wait_ge(const_made, 5)
            for u in range(4):
                if u >= 1:
                    scan(u - 1, u - 1)
                if u >= 3:
                    lo_a(u - 3, 0)
                mask(u, u)
            with dve.Fori(0, PAIRS - 1) as i:
                for t in range(16):
                    scan(16 * i + 3 + t, (3 + t) % 16)
                    sum_o(16 * i + t, t, 2 * i + t // 8)
                    s = 1 + t
                    lo_a(s % 16, 24 * i + 24 * (s // 16))
                    if t in (2, 4, 7, 10):
                        lo_proj((2, 4, 7, 10).index(t), 4 * i + 4)
                    mask(16 * i + 4 + t, (4 + t) % 16)
                    if t == 11:
                        take_qk(i + 1)
            last_pair = PAIRS - 1
            for t in range(16):
                u = 16 * last_pair + t
                if t < 13:
                    scan(u + 3, (3 + t) % 16)
                sum_o(u, t, 2 * last_pair + t // 8)
                if t < 15:
                    lo_a(1 + t, 24 * last_pair)
                if t < 12:
                    mask(u + 4, 4 + t)

            for k in range(4, KC):
                weight_lo(dve, N_GV + k)

            def group_sum(src_sem, which, tb, n, done):
                dve.wait_ge(src_sem, tb + 1)
                nc.vector.tensor_reduce(ST[:, 0, which, tb, 0:n], SQ[:, :].rearrange("p (g d) -> p g d", g=n), AX.X, ALU.add).then_inc(done, 1)

            def group_scale(which, tb, n, rstd, tile, done):
                dve.wait_ge(rstd, tb + 1)
                v = tile.rearrange("p (g d) -> p g d", g=n)
                r = ST[:, 1, which, tb, 0:n].rearrange("p (g a) -> p g a", a=1).to_broadcast([P, n, HALF // n])
                nc.vector.tensor_tensor(v, v, r, ALU.mult).then_inc(done, 1)

            dve.wait_ge(gb_in, 16)
            for tb in range(TB):
                if tb == 2:
                    dve.wait_ge(wt_hi, 1)
                    split_lo(WT[:, 1, :, :], PS[:, 2, :].rearrange("p (g t) -> p g t", g=GROUPS), WT[:, 0, :, :]).then_inc(wt_lo, 1)
                if tb == TB - 1:
                    for k in range(KC):
                        weight_lo(dve, N_U + k)
                group_sum(os_squared, 1, tb, HEADS, os_summed)
                group_sum(gv_squared, 0, tb, GROUPS, gv_summed)
                group_scale(1, tb, HEADS, os_rstd, O[:, tb, :], os_scaled)
                nc.vector.tensor_tensor(GV[:, tb % 2, :], GV[:, tb % 2, :], GB[:, :], ALU.mult).then_inc(gv_gained, 1)
                dve.wait_ge(gv_gained, tb + 1)
                group_scale(0, tb, GROUPS, gv_rstd, GV[:, tb % 2, :], gv_scaled)
                dve.wait_ge(vn_hi, tb + 1)
                split_lo(VN[:, 1, tb, :], GV[:, tb % 2, :], VN[:, 0, tb, :]).then_inc(vn_lo, 1)

            def lo_merged(i, tb, half):
                dve.wait_ge(mt_hi, i + 1)
                for k in range(4):
                    c = 4 * half + k
                    last = split_lo(AT_[:, 1, c, tok(tb)], PS[:, 2 + i % 2, tok(k)], AT_[:, 0, c, tok(tb)], CG[:, G_HEAD, c:c + 1])
                last.then_inc(mt_lo, 1)

            def gate(half, g):
                dve.wait_ge(mix_done, 4 * half + g + 1)
                dve.wait_ge(u_gelu, 4 * half + 4)
                u = U[:, 4 * half:4 * half + 4, tok(g)]
                nc.vector.scalar_tensor_tensor(u, PS[:, 4 + g, :].rearrange("p (c d) -> p c d", c=4), BSP[:, g:g + 1], u,
                                               ALU.add, ALU.mult).then_inc(gated, 1)

            def finish_a(half):
                for tb in range(4 * half, 4 * half + 4):
                    group_sum(a_squared, 2, tb, GROUPS, a_summed)
                    if tb > 4 * half:
                        group_scale(2, tb - 1, GROUPS, a_rstd, U[:, tb - 1, :], a_scaled)
                group_scale(2, 4 * half + 3, GROUPS, a_rstd, U[:, 4 * half + 3, :], a_scaled)

            for i in range(4):
                lo_merged(i, i, 1)
            for g in range(GROUPS):
                gate(0, g)
            finish_a(0)
            lo_merged(4, 4, 1)
            lo_merged(5, 0, 0)
            lo_merged(6, 5, 1)
            lo_merged(7, 1, 0)
            for k in range(KC):
                weight_lo(dve, N_OUT + k)
            lo_merged(8, 6, 1)
            lo_merged(9, 2, 0)
            lo_merged(10, 7, 1)
            lo_merged(11, 3, 0)
            for g in range(GROUPS):
                gate(1, g)
            finish_a(1)

            def add_block(done, i, added, tb, c):
                dve.wait_ge(done, i + 1)
                hc = H[:, tb, c * HALF:(c + 1) * HALF]
                nc.vector.tensor_tensor(hc, PS[:, i % 2, :], hc, ALU.add).then_inc(added, 1)

            for tb in range(TB):
                if tb >= 2 and tb < 6:
                    lo_merged(10 + tb, tb + 2, 0)
                dve.wait_ge(x2_in[tb], 16)
                if tb == TB - 1:
                    for k in range(KC):
                        weight_lo(dve, N_OUT + 8 + k)
                add_block(wout_done, tb, wout_added, tb, 0)
            for tb in range(TB):
                if tb >= 3:
                    lo_turned(n_h1, tb - 3, BT_, G_CROSS)
                add_block(wout_done, TB + tb, wout_added, tb, 1)
                if tb:
                    scale_rows(n_h1, tb - 1, xs(XSB, tb - 1), H[:, tb - 1, :].rearrange("p (k n) -> p k n", k=KC))
            scale_rows(n_h1, TB - 1, xs(XSB, TB - 1), H[:, TB - 1, :].rearrange("p (k n) -> p k n", k=KC))
            for tb in range(TB - 3, TB):
                lo_turned(n_h1, tb, BT_, G_CROSS)

            def lo_q2(m, j, i8):
                for f in range(2):
                    dve.wait_ge(q2_hi, 2 * j + f + 1 + i8)
                    c = slice(f * HALF, (f + 1) * HALF)
                    split_lo(AT_[:, 1, m, c], PS[:, 4 + 2 * (j % 2) + f, :], AT_[:, 0, m, c]).then_inc(q2_lo, 1)

            for j in range(4):
                if j == 1:
                    for mt in range(MB):
                        scale_rows(n_mem, mt, XM[mt][:, :, :], XM[mt][:, :, :])
                lo_q2(j, j, 0)
            for j in range(4):
                if j == 3:
                    for mt in range(MB):
                        for b in range(2):
                            dve.wait_ge(n_mem.hi, 2 * mt + b + 1)
                            for k in range(4 * b, 4 * b + 4):
                                last = split_lo(MEMT[:, 1, k, tok(mt)], PS[:, 2 * mt + b, tok(k % 4)], MEMT[:, 0, k, tok(mt)],
                                                CG[:, G_MEM, k:k + 1])
                            last.then_inc(n_mem.lo, 1)
                lo_q2(4 + j, j, 8)
            for m in range(KC):
                dve.wait_ge(k2_hi, m + 1)
                split_lo(K2T[:, 1, m, :], PS[:, 4 + m % 4, 0:N_MEM], K2T[:, 0, m, :]).then_inc(k2_lo, 1)
            for c in range(2):
                for mb in range(MB):
                    dve.wait_ge(v2_hi, MB * c + mb + 1)
                    cc = slice(c * HALF, (c + 1) * HALF)
                    split_lo(V2[:, 1, mb, cc], PS[:, mb, :], V2[:, 0, mb, cc]).then_inc(v2_lo, 1)

            def x_max(v):
                if v == 0:
                    dve.wait_ge(v2_done, 2 * MB)
                if v >= 2:
                    dve.wait_ge(xs_exp, 4 * (v - 1))
                for b in range(2):
                    dve.wait_ge(xs_done, 2 * v + b + 1)
                    nc.vector.tensor_reduce(XST[:, v % 2, 0, 2 * b:2 * b + 2], PS[:, 2 * (v % 2) + b, :].rearrange("p (q m) -> p q m", q=2),
                                            AX.X, ALU.max).then_inc(xs_max, 1)
                dve.wait_ge(xs_max, 2 * v + 2)
                nc.vector.tensor_scalar(XST[:, v % 2, 1, :], XST[:, v % 2, 0, :], -X_SCALE, None, ALU.mult).then_inc(xs_neg, 1)

            def x_prob(v):
                dve.wait_ge(xs_exp, 4 * v + 4)
                nc.vector.reciprocal(XST[:, v % 2, 3, :], XST[:, v % 2, 2, :]).then_inc(xs_inv, 1)
                dve.wait_ge(xs_inv, v + 1)
                e = EP[:, v % 2, :, :]
                r = XST[:, v % 2, 3, :].rearrange("p (q a) -> p q a", a=1).to_broadcast([P, 4, N_MEM])
                nc.vector.tensor_tensor(e, e, r, ALU.mult).then_inc(xs_prob, 1)

            def x_t_lo(v):
                for mb in range(MB):
                    dve.wait_ge(xt_hi, 2 * v + mb + 1)
                    split_lo(PT[v % 2][:, 1, mb, :], PS[:, 4 + mb, :], PT[v % 2][:, 0, mb, :]).then_inc(xt_lo, 1)

            def x_o_lo(v):
                h, f = divmod(v, 2)
                for d in range(2):
                    dve.wait_ge(xo_hi, 2 * v + d + 1)
                    c = slice(f * HALF, (f + 1) * HALF)
                    split_lo(AT_[:, 1, 2 * h + d, c], PS[:, 6 + d, :], AT_[:, 0, 2 * h + d, c]).then_inc(xo_lo, 1)

            for v in range(2 * XH + 3):
                if 1 <= v < 2 * XH + 1:
                    x_prob(v - 1)
                if v >= 3:
                    x_o_lo(v - 3)
                if 2 <= v < 2 * XH + 2:
                    x_t_lo(v - 2)
                if v < 2 * XH:
                    x_max(v)

            for tb in range(TB):
                if tb == TB - 1:
                    for k in range(KC):
                        weight_lo(dve, N_CO + 8 + k)
                add_block(down_done, tb, down_added, tb, 0)
            for tb in range(TB):
                if tb >= 3:
                    lo_turned(n_h2, tb - 3, BT_, G_FFN)
                add_block(down_done, TB + tb, down_added, tb, 1)
                if tb:
                    scale_rows(n_h2, tb - 1, xs(XSB, tb - 1), H[:, tb - 1, :].rearrange("p (k n) -> p k n", k=KC))
            scale_rows(n_h2, TB - 1, xs(XSB, TB - 1), H[:, TB - 1, :].rearrange("p (k n) -> p k n", k=KC))
            for tb in range(TB - 3, TB):
                lo_turned(n_h2, tb, BT_, G_FFN)

            with dve.Fori(0, FG) as g:
                for i in range(9):
                    if i < 8:
                        b = 4 + 2 * ((i // 2) % 2) + i % 2
                        dve.wait_ge(ff1_done, 8 * g + i + 1)
                        nc.vector.tensor_scalar(PS[:, b, :], PS[:, b, :], 0.0, None, ALU.max).then_inc(ff_relu, 1)
                    if i >= 1:
                        f, half = divmod(i - 1, 2)
                        b = 4 + 2 * (f % 2) + half
                        c = slice(half * HALF, (half + 1) * HALF)
                        dve.wait_ge(hid_hi, 8 * g + i)
                        split_lo(HID[:, 1, f, c], PS[:, b, :], HID[:, 0, f, c]).then_inc(hid_lo, 1)
                for i in range(2 * TB):
                    tb, nh = divmod(i, 2)
                    dve.wait_ge(down_done, 2 * TB + 2 * TB * g + i + 1)
                    hc = H[:, tb, nh * HALF:(nh + 1) * HALF]
                    nc.vector.tensor_tensor(hc, PS[:, i % 4, :], hc, ALU.add).then_inc(down_added, 1)
            dve.wait_ge(gf_in, 16)
            for tb in range(TB):
                dve.wait_ge(n_fin.rstd, tb + 1)
                nc.vector.scalar_tensor_tensor(YT[:, tb, :], H[:, tb, :], RS[:, tb:tb + 1], GF[:, :], ALU.mult, ALU.mult).then_inc(y_made, 1)

        @block.tensor
        def _(pe):
            mm = nc.tensor.matmul

            def three(out, w_hi_, w_lo_, m_hi, m_lo, first, last):
                mm(out, w_hi_, m_hi, start=first, stop=False)
                mm(out, w_hi_, m_lo, start=False, stop=False)
                return mm(out, w_lo_, m_hi, start=False, stop=last)

            def turn(chunk, bank, ks):
                for q, k in enumerate(ks):
                    last = nc.tensor.transpose(PS[:, bank, tok(q)], chunk(k), ident[:, :])
                return last

            def turn_block(norm, tb, stage):
                pe.wait_ge(norm.scaled, tb + 1)
                for b in range(2):
                    if tb:
                        pe.wait_ge(norm.lo, 2 * (tb - 1) + b + 1)
                    turn(lambda k: stage[:, k, tok(tb)], 2 + b, range(4 * b, 4 * b + 4)).then_inc(norm.turned, 1)

            def token_major(src, tb, bank, n0, done, last_block):
                for k in range(KC):
                    if tb == 0:
                        wait_lo(pe, n0 + k)
                    last = three(PS[:, bank, :], src[:, 0, k, tok(tb)], src[:, 1, k, tok(tb)], WS[:, k, 0, :], WS[:, k, 1, :],
                                 k == 0, k == KC - 1)
                    if last_block and k < KC - 1:
                        last.then_inc(w_used, 1)
                last.then_inc(done, 1)

            def feature_major(src, bank, place, n0, more, cols, done, first_half, last_half):
                for k in range(KC):
                    if first_half and k % 4 == 0:
                        wait_lo(pe, n0 + k // 4, more)
                    w = WS[:, place + k // 4, :, tok(k % 4)]
                    width = cols.stop - cols.start
                    last = three(PS[:, bank, 0:width], w[:, 0, :], w[:, 1, :], src[:, 0, k, cols], src[:, 1, k, cols], k == 0, k == KC - 1)
                    if last_half and k == 3:
                        last.then_inc(w_used, 1)
                last.then_inc(done, 1)

            halves = (slice(0, HALF), slice(HALF, SEQ))

            pe.wait_ge(const_made, 5)
            turn_block(n_x, 0, XSA)
            turn_block(n_x, 1, XSA)
            for tb in range(TB):
                pe.wait_ge(n_x.lo, 2 * tb + 2)
                if tb >= 2:
                    pe.wait_ge(v_lo, tb - 1)
                token_major(AT_, tb, tb % 2, N_V, v_done, tb == TB - 1)
                if tb + 2 < TB:
                    turn_block(n_x, tb + 2, XSA)

            def project(j, ks, pair):
                for k in ks:
                    place = 2 * (j // 2) + k // 4
                    if k == 0 and not (isinstance(pair, int) and pair == 0 and j == 0):
                        pe.wait_ge(qk_lo, 4 * pair + j)
                    if j % 2 == 0 and k % 4 == 0:
                        wait_lo(pe, N_QK + place, 4 * pair)
                    w = WS[:, place, :, tok(k % 4)]
                    last = three(PS[:, 7, :], w[:, 0, :], w[:, 1, :], AT_[:, 0, k, halves[j % 2]], AT_[:, 1, k, halves[j % 2]],
                                 k == 0, k == KC - 1)
                    if j % 2 == 1 and k == 3:
                        last.then_inc(w_used, 1)
                    if k == KC - 1:
                        last.then_inc(proj_done, 1)

            for j in range(4):
                project(j, range(KC), 0)

            def logits(u, s, pair):
                hh, tb = divmod(s, TB)
                if s == 0:
                    pe.wait_ge(qk_now, pair + 1)
                if not (isinstance(u, int) and u < 2):
                    pe.wait_ge(sig, 2 * u - 2)
                rows = slice(HD * hh, HD * hh + HD)
                w = (tb + 1) * P
                for b in range(1 if w <= HALF else 2):
                    keys = slice(b * HALF, min(w, (b + 1) * HALF))
                    last = three(PS[:, 2 * (s % 2) + b, 0:keys.stop - keys.start],
                                 QKC[rows, 0, 0, tok(tb)], QKC[rows, 0, 1, tok(tb)], QKC[rows, 1, 0, keys], QKC[rows, 1, 1, keys], True, True)
                last.then_inc(z_done, 1)

            def turn_a(u, s):
                tb = s % TB
                b0 = sum(BE_W[:s % 4])
                pe.wait_ge(a_done, u + 1)
                for g in range(1 if tb < 4 else 2):
                    turn(lambda k: BEBUF[:, b0 + k * P:b0 + (k + 1) * P], 4 + g, range(4 * g, min(4 * g + 4, tb + 1))).then_inc(t_done, 1)

            def values(u, s, g24, head):
                tb = s % TB
                pe.wait_ge(at_lo, groups_before(s) + (1 if tb < 4 else 2) + g24)
                if s:
                    pe.wait_ge(o_done, u)
                for sb in range(tb + 1):
                    for part in range(2):
                        last = mm(PS[:, 6, 0:2 * HD], ATR[:, sb // 4, part, tok(sb % 4)], VHL[:, sb, head, :],
                                  start=sb == 0 and part == 0, stop=sb == tb and part == 1)
                last.then_inc(pv_done, 1)

            pe.wait_ge(v_lo, TB)
            for u in range(4):
                if u >= 3:
                    turn_a(u - 3, u - 3)
                logits(u, u, 0)
            PARTS = {1: (0, range(4)), 2: (0, range(4, 8)), 3: (1, range(4)), 4: (1, range(4, 8)),
                     5: (2, range(3)), 6: (2, range(3, 6)), 7: (2, range(6, 8)), 8: (3, range(3)), 9: (3, range(3, 6)), 10: (3, range(6, 8))}
            with pe.Fori(0, PAIRS - 1) as i:
                for t in range(16):
                    values(16 * i + t, t, 24 * i, 2 * i + t // TB)
                    turn_a(16 * i + 1 + t, (1 + t) % 16)
                    if t in PARTS:
                        project(*PARTS[t], i + 1)
                    logits(16 * i + 4 + t, (4 + t) % 16, i + (4 + t) // 16)
                pe.wait_ge(o_done, 16 * i + 16)
            for t in range(16):
                u = 16 * (PAIRS - 1) + t
                values(u, t, 24 * (PAIRS - 1), 2 * (PAIRS - 1) + t // TB)
                if t < 15:
                    turn_a(u + 1, 1 + t)
                if t < 12:
                    logits(u + 4, 4 + t, PAIRS - 1)

            pe.wait_ge(sig, 2 * 16 * PAIRS)
            for tb in range(TB):
                if tb >= 2:
                    pe.wait_ge(gv_gelu, tb - 1)
                token_major(AT_, tb, tb % 2, N_GV, gv_done, tb == TB - 1)
                if tb == 1:
                    pe.wait_ge(wsp_masked, 1)
                    turn(lambda g: WSP[:, g, :], 2, range(GROUPS)).then_inc(wt_turned, 1)

            merged_at = {}

            def turn_merged(tb, half):
                i = len(merged_at)
                merged_at[tb, half] = i
                if half == 1:
                    pe.wait_ge(os_scaled, tb + 1)
                else:
                    pe.wait_ge(a_scaled, tb + 1)
                if i >= 2:
                    pe.wait_ge(mt_lo, i - 1)
                else:
                    pe.wait_ge(wt_lo, 1)
                turn(lambda k: (O if half else U)[:, tb, tok(k)], 2 + i % 2, range(4)).then_inc(mt_turned, 1)

            def mix(half):
                pe.wait_ge(vn_lo, TB)
                for g in range(GROUPS):
                    if half == 0:
                        pe.wait_ge((at_lo, at_lo, o_done, qk_lo)[g], (24 * PAIRS, 24 * PAIRS, 16 * PAIRS, 4 * PAIRS)[g])
                    else:
                        pe.wait_ge(gated, g + 1)
                    v = VN[:, :, 4 * half:4 * half + 4, tok(g)]
                    three(PS[:, 4 + g, :], WT[:, 0, g, :], WT[:, 1, g, :], v[:, 0], v[:, 1], True, True).then_inc(mix_done, 1)

            AFTER_U = {1: [(0, 1)], 2: [(1, 1)], 3: [(2, 1)], 4: [(3, 1)], 5: [(4, 1), (0, 0)], 6: [(5, 1), (1, 0)],
                       7: [(6, 1), (2, 0)]}
            for tb in range(TB):
                pe.wait_ge(u_gelu if tb >= 2 else gv_gelu, tb - 1 if tb >= 2 else TB)
                token_major(AT_, tb, tb % 2, N_U, u_done, tb == TB - 1)
                for at_tb, half in AFTER_U.get(tb, ()):
                    turn_merged(at_tb, half)
                if tb == 4:
                    mix(0)
            mix(1)
            turn_merged(7, 1)
            turn_merged(3, 0)

            pe.wait_ge(u_gelu, TB)
            for tb in range(TB):
                if 2 <= tb < 6:
                    turn_merged(tb + 2, 0)
                pe.wait_ge(mt_lo, max(merged_at[tb, 0], merged_at[tb, 1]) + 1)
                if tb >= 2:
                    pe.wait_ge(wout_added, tb - 1)
                token_major(AT_, tb, tb % 2, N_OUT, wout_done, tb == TB - 1)
            for tb in range(TB):
                pe.wait_ge(wout_added, TB + tb - 1)
                token_major(AT_, tb, tb % 2, N_OUT + 8, wout_done, tb == TB - 1)
                if tb >= 2:
                    turn_block(n_h1, tb - 2, XSB)
            turn_block(n_h1, TB - 2, XSB)
            turn_block(n_h1, TB - 1, XSB)

            pe.wait_ge(n_h1.lo, 2 * TB)
            with pe.Fori(0, 2) as i:
                for j in range(4):
                    for f in range(2):
                        if j >= 2:
                            pe.wait_ge(q2_lo, 8 * i + 2 * j + f - 3)
                        elif j == 1 and f == 0:
                            pe.wait_ge(q2_lo, 8 * i + 1)
                        feature_major(BT_, 4 + 2 * (j % 2) + f, 2 * j, N_CQ + 2 * j, 8 * i, halves[f], q2_done, f == 0, f == 1)
                pe.wait_ge(q2_lo, 8 * i + 6)
            for mt in range(MB):
                pe.wait_ge(n_mem.scaled, mt + 1)
                for b in range(2):
                    turn(lambda k: XM[mt][:, k, :], 2 * mt + b, range(4 * b, 4 * b + 4)).then_inc(n_mem.turned, 1)
            pe.wait_ge(n_mem.lo, 2 * MB)
            pe.wait_ge(q2_lo, 2 * KC)
            with pe.Fori(0, 2) as i:
                for j in range(4):
                    if j >= 2:
                        pe.wait_ge(k2_lo, 4 * i + j - 1)
                    feature_major(MEMT, 4 + j, 2 * j, N_CK + 2 * j, 8 * i, slice(0, N_MEM), k2_done, True, True)
            for c in range(2):
                for mb in range(MB):
                    if c:
                        pe.wait_ge(v2_lo, mb + 1)
                    if mb == 0:
                        token_major(MEMT, 0, mb, N_CV + 8 * c, v2_done, False)
                    else:
                        token_major(MEMT, mb, mb, N_CV + 8 * c, v2_done, True)

            def x_logits(v):
                h, f = divmod(v, 2)
                if v >= 2:
                    pe.wait_ge(xs_exp, 4 * (v - 1))
                for q in range(4):
                    out = PS[:, 2 * (v % 2) + q // 2, (q % 2) * N_MEM:(q % 2 + 1) * N_MEM]
                    for c in (2 * h, 2 * h + 1):
                        t = tok(4 * f + q)
                        last = three(out, AT_[:, 0, c, t], AT_[:, 1, c, t], K2T[:, 0, c, :], K2T[:, 1, c, :], c == 2 * h, c == 2 * h + 1)
                    if q % 2:
                        last.then_inc(xs_done, 1)

            def x_turn(v):
                pe.wait_ge(xs_prob, v + 1)
                for mb in range(MB):
                    if v:
                        pe.wait_ge(xt_lo, 2 * (v - 1) + mb + 1)
                    turn(lambda q: EP[:, v % 2, q, tok(mb)], 4 + mb, range(4)).then_inc(xt_done, 1)

            def x_values(v):
                h = v // 2
                pe.wait_ge(xt_lo, 2 * v + 2)
                for d in range(2):
                    if v:
                        pe.wait_ge(xo_lo, 2 * (v - 1) + d + 1)
                    c = slice(h * XD + d * P, h * XD + (d + 1) * P)
                    for mb in range(MB):
                        last = three(PS[:, 6 + d, :], V2[:, 0, mb, c], V2[:, 1, mb, c], PT[v % 2][:, 0, mb, :], PT[v % 2][:, 1, mb, :],
                                     mb == 0, mb == MB - 1)
                    last.then_inc(xo_done, 1)

            pe.wait_ge(k2_lo, KC)
            pe.wait_ge(v2_lo, 2 * MB)
            for v in range(2 * XH + 3):
                if v >= 3:
                    x_values(v - 3)
                if 2 <= v < 2 * XH + 2:
                    x_turn(v - 2)
                if v < 2 * XH:
                    x_logits(v)

            pe.wait_ge(xo_lo, 4 * XH)
            pe.wait_ge(xs_exp, 8 * XH)
            for c in range(2):
                for tb in range(TB):
                    i = TB * c + tb
                    if i >= 2:
                        pe.wait_ge(down_added, i - 1)
                    token_major(AT_, tb, tb % 2, N_CO + 8 * c, down_done, tb == TB - 1)
                    if c and tb >= 2:
                        turn_block(n_h2, tb - 2, XSB)
            turn_block(n_h2, TB - 2, XSB)
            turn_block(n_h2, TB - 1, XSB)

            pe.wait_ge(n_h2.lo, 2 * TB)
            pe.wait_ge(down_added, 2 * TB)
            with pe.Fori(0, FG) as g:
                for f in range(4):
                    for half in range(2):
                        if f >= 2:
                            pe.wait_ge(hid_lo, 8 * g + 2 * f + half - 3)
                        feature_major(BT_, 4 + 2 * (f % 2) + half, 2 * f, N_FF + 2 * f, 16 * g, halves[half], ff1_done, half == 0, half == 1)

                def down(i, k):
                    tb, nh = divmod(i, 2)
                    last = three(PS[:, i % 4, :], HID[:, 0, k, tok(tb)], HID[:, 1, k, tok(tb)],
                                 W2S[:, 4 * nh + k, 0, :], W2S[:, 4 * nh + k, 1, :], k == 0, k == 3)
                    if k == 3:
                        last.then_inc(down_done, 1)

                pe.wait_ge(down_added, 2 * TB + 2 * TB * g)
                for k in range(4):
                    pe.wait_ge(hid_lo, 8 * g + 2 * k + 1)
                    for i in range(4):
                        if i < 2:
                            wait_lo(pe, N_FF + 8 + 4 * i + k, 16 * g)
                        down(i, k)
                pe.wait_ge(hid_lo, 8 * g + 8)
                for i in range(4, 2 * TB):
                    pe.wait_ge(down_added, 2 * TB + 2 * TB * g + i - 3)
                    for k in range(4):
                        down(i, k)


_INS = ["x", "mem", "norm_mix_g", "w_in", "gm_v_norm_g", "w_spatial", "b_spatial", "head_norm_g", "w_out", "norm_cross_g",
        "norm_mem_g", "w_cq", "w_ckv", "w_co", "norm_ffn_g", "w_ff1", "w_ff2", "norm_final_g"]


def kernel(**inputs):
    import numpy as _np
    import concourse.bacc as _bacc
    from concourse import mybir as _mybir
    from concourse.bass_utils import run_bass_kernel_spmd as _run

    nc = _bacc.Bacc("TRN2", target_bir_lowering=False, num_devices=1)
    arrays, args = {}, []
    for name in _INS:
        a = _np.ascontiguousarray(inputs[name])
        if name != "norm_final_g":
            a = a.reshape(a.shape[1:])
        arrays[f"in_{name}"] = a
        args.append(nc.dram_tensor(f"in_{name}", a.shape, _mybir.dt.from_np(a.dtype), kind="ExternalInput").ap())
    out = nc.dram_tensor("out_y", (SEQ, D), F32, kind="ExternalOutput").ap()
    with nc.allow_non_contiguous_dma(reason="gains and biases go one feature to a partition"):
        build(nc, *args, out)
    r = _run(nc, [arrays], core_ids=[0])
    return r.results[0]["out_y"].reshape(1, SEQ, D)
```

```python
import concourse.bass as bass
from concourse import mybir
from concourse.alu_op_type import AluOpType as ALU
import numpy as np

F32 = mybir.dt.float32
F32R = mybir.dt.float32r
ACT = mybir.ActivationFunctionType
AX = mybir.AxisListType

P = 128
D = 1024
SEQ = 1024
TB = SEQ // P
KC = D // P
HALF = 512
GROUPS = 4
HEADS = 8
HD = 64
PAIRS = HEADS // 2
N_MEM = 256
MB = N_MEM // P
XH = 4
XD = D // XH
DFF = 4 * D
FG = DFF // HALF
EPS = 1e-6
Z_SCALE = HD ** -0.5
X_SCALE = XD ** -0.5
NEG = -1e30

COL_U, COL_GV, COL_Q, COL_K, COL_V = 0, 512, 1024, 1536, 2048

N_V = 0
N_QK = N_V + 8
N_GV = N_QK + 4 * PAIRS
N_U = N_GV + 8
N_OUT = N_U + 8
N_CQ = N_OUT + 16
N_CK = N_CQ + 16
N_CV = N_CK + 16
N_CO = N_CV + 16
N_FF = N_CO + 16
RAW_SLOTS = 4
WS_SLOTS = 8


def lo_on_vector(n):
    return N_GV + 4 <= n < N_CQ or N_CO + 8 <= n < N_FF or N_CK + 8 <= n < N_CO and n % 2 == 1


def lo_count(n):
    return sum(lo_on_vector(m) == lo_on_vector(n) for m in range(n + 1))


def used_count(n):
    def counted(m):
        if N_QK <= m < N_GV or N_CQ <= m < N_CV or m >= N_FF:
            return m % 2 == 0
        return m % 8 < 7
    return sum(counted(m) for m in range(n + 1))


def groups_before(s):
    head, tb = divmod(s, TB)
    return head * 12 + (tb if tb < 4 else 4 + 2 * (tb - 4))


def build(nc, x, mem, norm_mix_g, w_in, gm_v_norm_g, w_spatial, b_spatial, head_norm_g, w_out,
          norm_cross_g, norm_mem_g, w_cq, w_ckv, w_co, norm_ffn_g, w_ff1, w_ff2, norm_final_g, y):
    KB = 1024
    base = (nc.sbuf_base + 31) // 32 * 32
    A0 = base
    B0 = A0 + 64 * KB
    H0 = B0 + 64 * KB
    WS0 = H0 + 32 * KB
    RAW0 = WS0 + 32 * KB
    MISC0 = RAW0 + 8 * KB
    misc_at = [MISC0]

    def at(name, shape, dtype, offset):
        return nc.alloc_sbuf_tensor_at(name, shape, dtype, offset=offset)

    def misc(name, shape, dtype=F32):
        t = at(name, shape, dtype, misc_at[0])
        misc_at[0] += (4 * int(np.prod(shape[1:])) + 31) // 32 * 32
        return t

    AT_ = at("actA", [P, 2, KC, SEQ], F32R, A0)
    BT_ = at("actB", [P, 2, KC, SEQ], F32R, B0)
    XSA = at("stageA", [P, KC, SEQ], F32, A0 + 32 * KB)
    XSB = at("stageB", [P, KC, SEQ], F32, B0 + 32 * KB)
    H = at("h", [P, TB, D], F32, H0)
    WS = at("w_split", [P, WS_SLOTS, 2, HALF], F32R, WS0)
    RAW = at("w_raw", [P, RAW_SLOTS, HALF], F32, RAW0)

    VHL = at("v_parts", [P, TB, HEADS, 2 * HD], F32R, B0)
    O = at("attn_out", [P, TB, HALF], F32, B0 + 32 * KB)
    M_W = [896, 1024]
    BE_W = [640, 768, 896, 1024]
    MBUF = at("one_minus_beta", [P, sum(M_W)], F32, B0 + 48 * KB)
    NEGM = at("causal_neg", [P, P], F32, B0 + 48 * KB + 4 * sum(M_W))
    A_T_EVEN = misc_at[0]
    ATR = [misc("a_T_even", [P, 2, 7 * P], F32R), at("a_T_odd", [P, 2, SEQ], F32R, B0 + 56 * KB)]
    BEBUF = at("beta", [P, sum(BE_W)], F32, WS0 + 16 * KB)
    QKN = at("qk_next", [P, 2, 2, SEQ], F32R, H0)
    QKC = at("qk_now", [P, 2, 2, SEQ], F32R, H0 + 16 * KB)

    VN = at("v_norm", [P, 2, TB, HALF], F32R, B0)
    U = at("u_gated", [P, TB, HALF], F32, B0 + 48 * KB)
    WT = at("w_spatial_T", [P, 2, GROUPS, P], F32R, H0 + 16 * KB)
    WSP = at("w_spatial_masked", [P, GROUPS, P], F32, H0 + 20 * KB)
    GB = at("v_gain", [P, HALF], F32, H0 + 22 * KB)
    GV = at("gelu_v", [P, 2, HALF], F32, H0 + 24 * KB)
    SQ = at("squares", [P, HALF], F32, H0 + 28 * KB)
    ST = at("stats", [P, 2, 3, TB, HEADS], F32, H0 + 30 * KB)

    XM = [at("mem_tile0", [P, KC, P], F32, A0 + 7 * 4 * KB), at("mem_tile1", [P, KC, P], F32, A0 + 32 * KB + 7 * 4 * KB)]
    MEMT = BT_[:, :, :, 0:N_MEM]
    K2T = BT_[:, :, :, N_MEM:2 * N_MEM]
    BF = at("actB_f32", [P, 2, KC, SEQ], F32, B0)

    def v2_at(part, mb, c):
        return BT_[:, part, 2 * mb + c, HALF:SEQ]

    def pt_at(v, part, mb):
        return BT_[:, part, 4 + 2 * (v % 2) + mb, HALF:SEQ]


    HID = at("hid_T", [P, 2, 4, SEQ], F32R, A0)
    W2S = at("w2_split", [P, 8, 2, HALF], F32R, A0 + 32 * KB)
    JUNK = at("junk", [P, D], F32, B0)
    YT = at("y_tiles", [P, TB, D], F32, B0 + 32 * KB)
    GF = at("final_gain", [P, D], F32, WS0)

    EP = [at("p_exp_even", [P, 4, N_MEM], F32, A_T_EVEN), BF[:, 0, 0:4, 0:N_MEM]]
    XST = at("softmax_stats", [P, 2, 4, 4], F32, A_T_EVEN + 4 * KB)

    ident = misc("identity", [P, P])
    CG = misc("gains", [P, 5, KC])
    BSP = misc("b_sp", [P, GROUPS])
    SS = misc("row_sums", [P, TB])
    RS = misc("row_rstd", [P, TB])
    NEGH = misc("minus_half", [P, 8])
    G_MIX, G_HEAD, G_CROSS, G_MEM, G_FFN = range(5)

    PS = nc.alloc_psum_tensor("ps", [P, 8, HALF], F32)

    def f32(ap):
        return ap.bitcast(F32)

    S = {}

    def sem(name):
        S[name] = nc.alloc_semaphore(name)
        return S[name]

    raw_in = [sem(f"raw_in{i}") for i in range(RAW_SLOTS)]
    w_hi = sem("w_hi")
    w_lo_pool = sem("w_lo_pool")
    w_lo_dve = sem("w_lo_dve")
    w_used = sem("w_used")
    const_in = sem("const_in")
    const_made = sem("const_made")
    x_in = [sem(f"x_in{t}") for t in range(TB)]

    class Norm:
        def __init__(self, name):
            self.squared = sem(name + "_squared")
            self.mean = sem(name + "_mean")
            self.rstd = sem(name + "_rstd")
            self.scaled = sem(name + "_scaled")
            self.turned = sem(name + "_turned")
            self.hi = sem(name + "_hi")
            self.lo = sem(name + "_lo")

    n_x, n_h1, n_mem, n_h2, n_fin = (Norm(n) for n in ("x", "h1", "mem", "h2", "fin"))

    v_done, v_hi, v_lo = sem("v_done"), sem("v_hi"), sem("v_lo")
    proj_done, qk_hi, qk_lo, qk_now = sem("proj_done"), sem("qk_hi"), sem("qk_lo"), sem("qk_now_ready")
    z_done, z_masked, sig, scanned, a_done = sem("z_done"), sem("z_masked"), sem("sig"), sem("scanned"), sem("a_done")
    t_done, at_hi, at_lo, pv_done, o_done = sem("t_done"), sem("at_hi"), sem("at_lo"), sem("pv_done"), sem("o_done")

    wsp_in, wsp_masked, wt_turned, wt_hi, wt_lo = (sem(n) for n in ("wsp_in", "wsp_masked", "wt_turned", "wt_hi", "wt_lo"))
    gb_in = sem("gb_in")
    gv_done, gv_gelu, gv_squared, gv_summed, gv_mean, gv_rstd = (sem("gv_" + n) for n in ("done", "gelu", "squared", "summed", "mean", "rstd"))
    gv_gained, gv_scaled, vn_hi, vn_lo = sem("gv_gained"), sem("gv_scaled"), sem("vn_hi"), sem("vn_lo")
    os_squared, os_summed, os_mean, os_rstd, os_scaled = (sem("o_" + n) for n in ("squared", "summed", "mean", "rstd", "scaled"))
    u_done, u_gelu, mix_done, gated = sem("u_done"), sem("u_gelu"), sem("mix_done"), sem("gated")
    a_squared, a_summed, a_mean, a_rstd, a_scaled = (sem("a_" + n) for n in ("squared", "summed", "mean", "rstd", "scaled"))
    mt_turned, mt_hi, mt_lo = sem("mt_turned"), sem("mt_hi"), sem("mt_lo")
    x2_in = [sem(f"x_again{t}") for t in range(TB)]
    wout_done, wout_added = sem("wout_done"), sem("wout_added")

    q2_done, q2_hi, q2_lo = sem("q2_done"), sem("q2_hi"), sem("q2_lo")
    mem_in = sem("mem_in")
    k2_done, k2_hi, k2_lo = sem("k2_done"), sem("k2_hi"), sem("k2_lo")
    v2_done, v2_hi, v2_lo = sem("v2_done"), sem("v2_hi"), sem("v2_lo")
    xs_done, xs_max, xs_neg, xs_exp, xs_inv, xs_prob = (sem("xs_" + n) for n in ("done", "max", "neg", "exp", "inv", "prob"))
    xt_done, xt_hi, xt_lo, xo_done, xo_hi, xo_lo = (sem(n) for n in ("xt_done", "xt_hi", "xt_lo", "xo_done", "xo_hi", "xo_lo"))
    down_done, down_added = sem("down_done"), sem("down_added")

    ff1_done, ff_relu, ff_sq, hid_hi, hid_lo = (sem(n) for n in ("ff1_done", "ff_relu", "ff_sq", "hid_hi", "hid_lo"))
    gf_in, y_made, y_out = sem("gf_in"), sem("y_made"), sem("y_out")

    def wait_lo(eng, n, more=0):
        eng.wait_ge(w_lo_dve if lo_on_vector(n) else w_lo_pool, lo_count(n) + more)

    def tok(tb, n=1):
        return slice(tb * P, (tb + n) * P)

    def xs(stage, tb):
        return stage[:, :, tok(tb)]

    def split_hi(out, src, gain=None):
        if gain is None:
            return nc.scalar.activation(out, src, ACT.Copy)
        return nc.scalar.activation(out, src, ACT.Copy, scale=gain)

    def split_lo(out, src, hi, gain=None):
        if gain is None:
            return nc.vector.tensor_tensor(out, src, f32(hi), ALU.subtract)
        return nc.vector.scalar_tensor_tensor(out, src, gain, f32(hi), ALU.mult, ALU.subtract)

    def freed(n):
        if n < N_QK:
            return (w_used, used_count(n)) if n < 7 else (v_done, TB)
        if n < N_GV:
            pair, j = divmod(n - N_QK, 4)
            return (w_used, used_count(n)) if j % 2 == 0 else (proj_done, 4 * pair + j + 1)
        for first, done in ((N_GV, gv_done), (N_U, u_done), (N_OUT, wout_done), (N_OUT + 8, wout_done), (N_CO, down_done), (N_CO + 8, down_done)):
            if first <= n < first + 8:
                second = first in (N_OUT + 8, N_CO + 8)
                return (w_used, used_count(n)) if n < first + 7 else (done, TB * (1 + second))
        if n < N_CV:
            m, kh = divmod((n - N_CQ) % 16, 2)
            if kh == 0:
                return w_used, used_count(n)
            return (q2_done, 8 * (m // 4) + m % 4 + 5) if n < N_CK else (k2_done, m + 1)
        if n < N_CO:
            c, k = divmod(n - N_CV, 8)
            return (w_used, used_count(n)) if k < 7 else (v2_done, MB * (c + 1))
        f, kh = divmod(n - N_FF, 2)
        return (w_used, used_count(n)) if kh == 0 else (ff1_done, 4 + f + 1)

    def place_free(n):
        if n < WS_SLOTS:
            return None
        if n < N_QK + 4:
            return freed(n - 8)
        if n < N_GV + 4:
            return freed(n - 4)
        if n < N_GV + 8:
            return t_done, 24 * PAIRS
        return freed(n - 8)

    def weight_hi(act, n):
        act.wait_ge(raw_in[n % 4], 16 * (n // 4 + 1))
        free = place_free(n)
        if free:
            act.wait_ge(*free)
        split_hi(WS[:, n % 8 if not N_QK <= n < N_GV else n % 4, 0, :], RAW[:, n % 4, :]).then_inc(w_hi, 1)

    def weight_lo(eng, n):
        eng.wait_ge(w_hi, n + 1)
        place = n % 8 if not N_QK <= n < N_GV else n % 4
        return eng.tensor_tensor(WS[:, place, 1, :], RAW[:, n % 4, :], f32(WS[:, place, 0, :]), ALU.subtract).then_inc(
            w_lo_dve if lo_on_vector(n) else w_lo_pool, 1)

    def cols_of(w, k, c):
        return w[k * P:(k + 1) * P, c:c + HALF]

    def unit_of(w, kh, c):
        return w.rearrange("(k p) n -> p k n", p=P)[:, 4 * kh:4 * kh + 4, bass.ds(c, P)]

    block = nc.Block()
    with block:
        @block.sync
        def _(sp):
            def load(n, src, more=0, unit=False):
                if n >= RAW_SLOTS:
                    wait_lo(sp, n - RAW_SLOTS, more)
                dst = RAW[:, n % 4, :]
                if unit:
                    dst = dst.rearrange("p (k n) -> p k n", k=4)
                sp.dma_start(dst, src).then_inc(raw_in[n % 4], 16)

            for k in range(KC):
                load(N_V + k, cols_of(w_in, k, COL_V))
            for j in range(4):
                load(N_QK + j, unit_of(w_in, j % 2, COL_Q if j < 2 else COL_K), unit=True)
            with sp.Fori(0, PAIRS - 1) as i:
                for j in range(4):
                    load(N_QK + 4 + j, unit_of(w_in, j % 2, (COL_Q if j < 2 else COL_K) + P + P * i), 4 * i, True)
            for k in range(KC):
                load(N_GV + k, cols_of(w_in, k, COL_GV))
            for k in range(KC):
                load(N_U + k, cols_of(w_in, k, COL_U))
            for c in range(2):
                for k in range(KC):
                    load(N_OUT + 8 * c + k, cols_of(w_out, k, c * HALF))
            for m in range(KC):
                for kh in range(2):
                    load(N_CQ + 2 * m + kh, unit_of(w_cq, kh, m * P), unit=True)
            for m in range(KC):
                for kh in range(2):
                    load(N_CK + 2 * m + kh, unit_of(w_ckv, kh, m * P), unit=True)
            for c in range(2):
                for k in range(KC):
                    load(N_CV + 8 * c + k, cols_of(w_ckv, k, D + c * HALF))
            for c in range(2):
                for k in range(KC):
                    load(N_CO + 8 * c + k, cols_of(w_co, k, c * HALF))

            def ff2_slots(g):
                for j in range(8):
                    load(N_FF + 8 + j, w_ff2[bass.ds(g * HALF + (j % 4) * P, P), (j // 4) * HALF:(j // 4 + 1) * HALF], 16 * g)

            for j in range(8):
                load(N_FF + j, unit_of(w_ff1, j % 2, (j // 2) * P), unit=True)
            with sp.Fori(0, FG - 1) as g:
                ff2_slots(g)
                for j in range(8):
                    load(N_FF + 16 + j, unit_of(w_ff1, j % 2, HALF + g * HALF + (j // 2) * P), 16 * g, True)
            ff2_slots(FG - 1)
            for tb in range(TB):
                sp.wait_ge(y_made, tb + 1)
                sp.dma_start(y[tok(tb), :], YT[:, tb, :]).then_inc(y_out, 16)
            sp.wait_ge(y_out, 16 * TB)

        @block.gpsimd
        def _(pool):
            pool.memset(ident[:, :], 0.0).then_inc(const_made, 1)
            pool.memset(NEGH[:, :], -0.5).then_inc(const_made, 1)
            pool.memset(NEGM[:, :], 0.0).then_inc(const_made, 1)
            pool.wait_ge(const_made, 3)
            pool.affine_select(out=ident[:, :], in_=ident[:, :], compare_op=ALU.not_equal, fill=1.0, base=0,
                               pattern=[[-1, P]], channel_multiplier=1).then_inc(const_made, 1)
            pool.affine_select(out=NEGM[:, :], in_=NEGM[:, :], compare_op=ALU.is_gt, fill=NEG, base=0,
                               pattern=[[-1, P]], channel_multiplier=1).then_inc(const_made, 1)

            def row_rstd(norm, tb, width=D, src=SS, dst=RS):
                pool.wait_ge(norm.squared, tb + 1)
                pool.tensor_scalar(dst[:, tb:tb + 1], src[:, tb:tb + 1], 1.0 / width, EPS, ALU.mult, ALU.add).then_inc(norm.mean, 1)
                pool.wait_ge(norm.mean, tb + 1)
                pool.tensor_tensor(dst[:, tb:tb + 1], dst[:, tb:tb + 1], NEGH[:, 0:1], ALU.pow).then_inc(norm.rstd, 1)

            row_rstd(n_x, 0)
            for k in range(KC):
                weight_lo(pool, N_V + k)
                if k in (0, 3):
                    row_rstd(n_x, 1 if k == 0 else 2)
            for tb in range(3, TB):
                row_rstd(n_x, tb)
            for j in range(4):
                weight_lo(pool, N_QK + j)

            def weigh(u, s):
                tb = s % TB
                w = (tb + 1) * P
                m0, b0 = sum(M_W[:s % 2]), sum(BE_W[:s % 4])
                pool.wait_ge(scanned, u + 1)
                pool.tensor_tensor(BEBUF[:, b0:b0 + w - 1], BEBUF[:, b0:b0 + w - 1], MBUF[:, m0 + 1:m0 + w], ALU.mult).then_inc(a_done, 1)

            for u in range(1, 4):
                weigh(u - 1, u - 1)
            with pool.Fori(0, PAIRS - 1) as i:
                for t in range(16):
                    weigh(16 * i + 3 + t, (3 + t) % 16)
                    if t < 2:
                        for j in (2 * t, 2 * t + 1):
                            pool.wait_ge(w_hi, N_QK + 4 + j + 1 + 4 * i)
                            pool.tensor_tensor(WS[:, j, 1, :], RAW[:, j, :], f32(WS[:, j, 0, :]), ALU.subtract).then_inc(w_lo_pool, 1)
            for t in range(12 + 1):
                weigh(16 * (PAIRS - 1) + 3 + t, (3 + t) % 16)
                if t < 4:
                    weight_lo(pool, N_GV + t)

            pool.wait_ge(wsp_in, 16)
            pool.affine_select(out=WSP[:, :, :], in_=WSP[:, :, :], compare_op=ALU.is_ge, fill=0.0, base=0,
                               pattern=[[0, GROUPS], [-1, P]], channel_multiplier=1).then_inc(wsp_masked, 1)

            def group_rstd(which, tb, n, width, summed, mean, rstd):
                pool.wait_ge(summed, tb + 1)
                s, r = ST[:, 0, which, tb, 0:n], ST[:, 1, which, tb, 0:n]
                pool.tensor_scalar(r, s, 1.0 / width, EPS, ALU.mult, ALU.add).then_inc(mean, 1)
                pool.wait_ge(mean, tb + 1)
                pool.tensor_tensor(r, r, NEGH[:, 0:n], ALU.pow).then_inc(rstd, 1)

            for tb in range(TB):
                group_rstd(1, tb, HEADS, HD, os_summed, os_mean, os_rstd)
                group_rstd(0, tb, GROUPS, P, gv_summed, gv_mean, gv_rstd)
            for tb in range(TB):
                group_rstd(2, tb, GROUPS, P, a_summed, a_mean, a_rstd)
            for tb in range(TB):
                if tb == TB - 1:
                    for n in range(N_CQ, N_CQ + 2):
                        weight_lo(pool, n)
                row_rstd(n_h1, tb)
            for n in range(N_CQ + 2, N_CQ + 8):
                weight_lo(pool, n)
            for mt in range(MB):
                row_rstd(n_mem, mt)
            for n in range(N_CQ + 8, N_CO):
                if not lo_on_vector(n):
                    weight_lo(pool, n)

            for v in range(2 * XH):
                pool.wait_ge(xs_inv, v + 1)
                r = XST[:, v % 2, 3, :].rearrange("p (q a) -> p q a", a=1).to_broadcast([P, 4, N_MEM])
                pool.tensor_tensor(EP[v % 2][:, :, :], EP[v % 2][:, :, :], r, ALU.mult).then_inc(xs_prob, 1)
                if 1 <= v < 5:
                    for n in (N_CO + 2 * v - 2, N_CO + 2 * v - 1):
                        weight_lo(pool, n)
            for tb in range(TB - 1):
                row_rstd(n_h2, tb)

            def ff_lo(j, more, dst):
                pool.wait_ge(w_hi, N_FF + j + 1 + more)
                pool.tensor_tensor(dst[:, j % 8, 1, :], RAW[:, j % 4, :], f32(dst[:, j % 8, 0, :]), ALU.subtract).then_inc(w_lo_pool, 1)

            for j in range(8):
                if j == 2:
                    row_rstd(n_h2, TB - 1)
                ff_lo(j, 0, WS)
            with pool.Fori(0, FG - 1) as g:
                for j in range(8, 16):
                    ff_lo(j, 16 * g, W2S)
                for j in range(16, 24):
                    ff_lo(j, 16 * g, WS)
            for j in range(8, 16):
                ff_lo(j, 16 * (FG - 1), W2S)
            for tb in range(TB):
                row_rstd(n_fin, tb)

        @block.scalar
        def _(act):
            for tb in range(2):
                act.dma_start(xs(XSA, tb), x[tok(tb), :].rearrange("p (k n) -> p k n", k=KC)).then_inc(x_in[tb], 16)
            for g, src in enumerate((norm_mix_g, head_norm_g, norm_cross_g, norm_mem_g, norm_ffn_g)):
                act.dma_start(CG[:, g, :], src.rearrange("(k p) -> p k", p=P)).then_inc(const_in, 16)
            act.dma_start(BSP[:, :], b_spatial.rearrange("g t -> t g")).then_inc(const_in, 16)
            for tb in range(2, TB):
                act.dma_start(xs(XSA, tb), x[tok(tb), :].rearrange("p (k n) -> p k n", k=KC)).then_inc(x_in[tb], 16)

            def evac_turned(norm, tb, dst, gain, count0=0):
                for b in range(2):
                    act.wait_ge(norm.turned, 2 * tb + b + 1)
                    for k in range(4 * b, 4 * b + 4):
                        last = split_hi(dst[:, 0, k, tok(tb)], PS[:, 2 + b, tok(k % 4)], CG[:, gain, k:k + 1])
                    last.then_inc(norm.hi, 1)

            def square_x(tb):
                act.wait_ge(x_in[tb], 16)
                nc.scalar.activation(H[:, tb, :].rearrange("p (k n) -> p k n", k=KC), xs(XSA, tb), ACT.Square,
                                     accum_out=SS[:, tb:tb + 1]).then_inc(n_x.squared, 1)

            def evac_v(tb):
                act.wait_ge(v_done, tb + 1)
                split_hi(VHL[:, tb, :, 0:HD], PS[:, tb % 2, :].rearrange("p (h d) -> p h d", h=HEADS)).then_inc(v_hi, 1)

            square_x(0)
            weight_hi(act, N_V)
            act.wait_ge(const_in, 6 * 16)
            square_x(1)
            for k in range(1, KC):
                weight_hi(act, N_V + k)
                if k == 3:
                    evac_turned(n_x, 0, AT_, G_MIX)
                    square_x(2)
            for tb in range(1, TB):
                evac_turned(n_x, tb, AT_, G_MIX)
                if tb + 2 < TB:
                    square_x(tb + 2)
                evac_v(tb - 1)
            for j in range(4):
                weight_hi(act, N_QK + j)
            evac_v(TB - 1)

            def evac_proj(j, i4, dst, bank):
                act.wait_ge(proj_done, i4 + j + 1)
                split_hi(dst[:, j // 2, 0, (j % 2) * HALF:(j % 2 + 1) * HALF], PS[:, bank, :]).then_inc(qk_hi, 1)

            for j in range(4):
                evac_proj(j, 0, QKC, 4 + j)

            def attn_a_hi(u, s, g24):
                tb = s % TB
                for g in range(1 if tb < 4 else 2):
                    n = min(4, tb + 1 - 4 * g) * P
                    count = groups_before(s) + g + 1 + g24
                    act.wait_ge(t_done, count)
                    if g == 0 and not (isinstance(u, int) and u < 2):
                        act.wait_ge(pv_done, u - 1)
                    split_hi(ATR[tb % 2][:, 0, g * HALF:g * HALF + n], PS[:, 4 + g, 0:n]).then_inc(at_hi, 1)

            def sigmoids(u, s):
                tb = s % TB
                w = (tb + 1) * P
                z0 = 2 * (s % 2)
                m0, b0 = sum(M_W[:s % 2]), sum(BE_W[:s % 4])
                zp = PS[:, z0:z0 + 2, :].rearrange("p b n -> p (b n)")[:, 0:w]
                act.wait_ge(z_masked, u + 1)
                nc.scalar.activation(BEBUF[:, b0:b0 + w], zp, ACT.Sigmoid, scale=Z_SCALE).then_inc(sig, 1)
                if not (isinstance(u, int) and u < 2):
                    act.wait_ge(a_done, u - 1)
                nc.scalar.activation(MBUF[:, m0:m0 + w], zp, ACT.Sigmoid, scale=-Z_SCALE).then_inc(sig, 1)

            act.wait_ge(v_lo, TB)
            for u in range(4):
                if u >= 3:
                    attn_a_hi(u - 3, u - 3, 0)
                sigmoids(u, u)
            with act.Fori(0, PAIRS - 1) as i:
                for t in range(16):
                    s = 1 + t
                    attn_a_hi(16 * i + s, s % 16, 24 * i + 24 * (s // 16))
                    if t < 2:
                        for j in (2 * t, 2 * t + 1):
                            act.wait_ge(raw_in[j], 16 * (N_QK // 4 + 2) + 16 * i)
                            if j % 2 == 0:
                                act.wait_ge(w_used, used_count(N_QK + j) + 2 * i)
                            else:
                                act.wait_ge(proj_done, 4 * i + j + 1)
                            split_hi(WS[:, j, 0, :], RAW[:, j, :]).then_inc(w_hi, 1)
                    if t in (2, 4, 7, 10):
                        j = (2, 4, 7, 10).index(t)
                        evac_proj(j, 4 * i + 4, QKN, 7)
                    sigmoids(16 * i + 4 + t, (4 + t) % 16)
            for t in range(12 + 3):
                s = 1 + t
                last = PAIRS - 1
                attn_a_hi(16 * last + s, s, 24 * last)
                if t < 4:
                    weight_hi(act, N_GV + t)
                if t < 12:
                    sigmoids(16 * last + 4 + t, 4 + t)
            act.wait_ge(z_done, 16 * PAIRS)
            act.dma_start(WSP[:, :, :], w_spatial.rearrange("g t s -> t g s")).then_inc(wsp_in, 16)
            act.dma_start(GB[:, :], gm_v_norm_g.rearrange("(a n) -> a n", a=1).to_broadcast([P, HALF])).then_inc(gb_in, 16)
            for tb in range(4):
                act.dma_start(H[:, tb, :], x[tok(tb), :]).then_inc(x2_in[tb], 16)
            for k in range(4, KC):
                weight_hi(act, N_GV + k)

            def square_o(tb):
                act.wait_ge(o_done, 16 * PAIRS)
                if tb:
                    act.wait_ge(gv_summed, tb)
                nc.scalar.activation(SQ[:, :], O[:, tb, :], ACT.Square).then_inc(os_squared, 1)

            def gelu_v(tb):
                act.wait_ge(gv_done, tb + 1)
                if tb >= 2:
                    act.wait_ge(vn_lo, tb - 1)
                nc.scalar.activation(GV[:, tb % 2, :], PS[:, tb % 2, :], ACT.Gelu_apprx_tanh).then_inc(gv_gelu, 1)

            def square_v(tb):
                act.wait_ge(gv_gelu, tb + 1)
                act.wait_ge(os_summed, tb + 1)
                nc.scalar.activation(SQ[:, :], GV[:, tb % 2, :], ACT.Square).then_inc(gv_squared, 1)

            def hi_v(tb):
                act.wait_ge(gv_scaled, tb + 1)
                split_hi(VN[:, 0, tb, :], GV[:, tb % 2, :]).then_inc(vn_hi, 1)

            for tb in range(TB):
                if tb == 2:
                    act.wait_ge(wt_turned, 1)
                    split_hi(WT[:, 0, :, :], PS[:, 2, :].rearrange("p (g t) -> p g t", g=GROUPS)).then_inc(wt_hi, 1)
                if tb < TB - 2:
                    square_o(tb)
                    gelu_v(tb)
                    square_v(tb)
                    hi_v(tb)
            gelu_v(TB - 2)
            for k in range(KC):
                weight_hi(act, N_U + k)
            gelu_v(TB - 1)
            for tb in range(TB - 2, TB):
                square_o(tb)
                square_v(tb)
                hi_v(tb)

            def gelu_u(tb):
                act.wait_ge(u_done, tb + 1)
                nc.scalar.activation(U[:, tb, :], PS[:, tb % 2, :], ACT.Gelu_apprx_tanh).then_inc(u_gelu, 1)

            def evac_merged(i, tb, half):
                act.wait_ge(mt_turned, i + 1)
                for k in range(4):
                    last = split_hi(AT_[:, 0, 4 * half + k, tok(tb)], PS[:, 2 + i % 2, tok(k)],
                                    CG[:, G_HEAD, 4 * half + k:4 * half + k + 1])
                last.then_inc(mt_hi, 1)

            def square_a(tb):
                act.wait_ge(gated, 4 * (tb // 4 + 1))
                act.wait_ge(a_summed if tb else gv_summed, tb or TB)
                nc.scalar.activation(SQ[:, :], U[:, tb, :], ACT.Square).then_inc(a_squared, 1)

            gelu_u(0)
            gelu_u(1)
            evac_merged(0, 0, 1)
            gelu_u(2)
            evac_merged(1, 1, 1)
            gelu_u(3)
            evac_merged(2, 2, 1)
            gelu_u(4)
            evac_merged(3, 3, 1)
            for tb in range(4):
                square_a(tb)
            gelu_u(5)
            evac_merged(4, 4, 1)
            evac_merged(5, 0, 0)
            gelu_u(6)
            evac_merged(6, 5, 1)
            evac_merged(7, 1, 0)
            for k in range(KC):
                weight_hi(act, N_OUT + k)
            gelu_u(7)
            evac_merged(8, 6, 1)
            evac_merged(9, 2, 0)
            evac_merged(10, 7, 1)
            evac_merged(11, 3, 0)
            for tb in range(4, TB):
                square_a(tb)
            act.wait_ge(a_scaled, TB)
            for tb in range(4, TB):
                act.dma_start(H[:, tb, :], x[tok(tb), :]).then_inc(x2_in[tb], 16)
            for tb in range(4, TB):
                evac_merged(8 + tb, tb, 0)
            for k in range(KC):
                weight_hi(act, N_OUT + 8 + k)

            def square_h(norm, tb, added, count):
                act.wait_ge(added, count)
                nc.scalar.activation(xs(XSB, tb), H[:, tb, :].rearrange("p (k n) -> p k n", k=KC), ACT.Square,
                                     accum_out=SS[:, tb:tb + 1]).then_inc(norm.squared, 1)

            act.wait_ge(mt_lo, 16)
            for tb in range(TB):
                if tb >= 3:
                    evac_turned(n_h1, tb - 3, BT_, G_CROSS)
                square_h(n_h1, tb, wout_added, TB + tb + 1)
                if tb == TB - 2:
                    for k in range(4):
                        weight_hi(act, N_CQ + k)
            evac_turned(n_h1, TB - 3, BT_, G_CROSS)
            for k in range(4, 8):
                weight_hi(act, N_CQ + k)
            act.wait_ge(wout_done, 2 * TB)
            for mt in range(MB):
                act.dma_start(XM[mt][:, :, :], mem[tok(mt), :].rearrange("p (k n) -> p k n", k=KC)).then_inc(mem_in, 16)

            def evac_q2(i, m, f):
                act.wait_ge(q2_done, i + 1)
                if m == KC - 1:
                    act.wait_ge(n_mem.turned, 2 * MB)
                split_hi(AT_[:, 0, m, f * HALF:(f + 1) * HALF], PS[:, 4 + i % 4, :]).then_inc(q2_hi, 1)

            for i in range(4):
                evac_q2(i, i, 0)
                if i < 2:
                    evac_turned(n_h1, TB - 2 + i, BT_, G_CROSS)
            act.wait_ge(mem_in, 16 * MB)
            act.wait_ge(n_h1.scaled, TB)
            for mt in range(MB):
                act.wait_ge(wout_added, 2 * TB)
                if mt:
                    act.wait_ge(n_mem.squared, mt)
                nc.scalar.activation(PS[:, 0:2, :].rearrange("p b (k n) -> p (b k) n", k=4), XM[mt][:, :, :], ACT.Square,
                                     accum_out=SS[:, mt:mt + 1]).then_inc(n_mem.squared, 1)
            for i in range(4, 8):
                evac_q2(i, i - 4, 1)
                for k in (2 * i - 8, 2 * i - 7):
                    weight_hi(act, N_CQ + 8 + k)
            for i in range(8, 12):
                evac_q2(i, i - 4, 0)
            for mt in range(MB):
                for b in range(2):
                    for k in range(4 * b, 4 * b + 4):
                        last = split_hi(MEMT[:, 0, k, tok(mt)], PS[:, 2 * mt + b, tok(k % 4)], CG[:, G_MEM, k:k + 1])
                    last.then_inc(n_mem.hi, 1)
            for i in range(12, 16):
                evac_q2(i, i - 8, 1)
                for k in (2 * i - 24, 2 * i - 23):
                    weight_hi(act, N_CK + k)

            for m in range(KC):
                act.wait_ge(k2_done, m + 1)
                split_hi(K2T[:, 0, m, :], PS[:, 4 + m % 4, 0:N_MEM]).then_inc(k2_hi, 1)
                for k in (2 * m, 2 * m + 1):
                    weight_hi(act, N_CK + 8 + k)

            def x_exp(v):
                act.wait_ge(xs_neg, v + 1)
                if v >= 2:
                    act.wait_ge(xt_done, 2 * (v - 1))
                for q in range(4):
                    nc.scalar.activation(EP[v % 2][:, q, :], PS[:, 2 * (v % 2) + q // 2, (q % 2) * N_MEM:(q % 2 + 1) * N_MEM], ACT.Exp,
                                         bias=XST[:, v % 2, 1, q:q + 1], scale=X_SCALE,
                                         accum_out=XST[:, v % 2, 2, q:q + 1]).then_inc(xs_exp, 1)

            x_exp(0)
            for c in range(2):
                for mb in range(MB):
                    if mb == MB - 1 and c == 0:
                        for k in range(KC):
                            weight_hi(act, N_CV + 8 + k)
                    act.wait_ge(v2_done, MB * c + mb + 1)
                    split_hi(v2_at(0, mb, c), PS[:, 6 + mb, :]).then_inc(v2_hi, 1)

            def x_t_hi(v):
                for mb in range(MB):
                    act.wait_ge(xt_done, 2 * v + mb + 1)
                    if v >= 2:
                        act.wait_ge(xo_done, 2 * (v - 1))
                    split_hi(pt_at(v, 0, mb), PS[:, 4 + mb, :]).then_inc(xt_hi, 1)

            def x_o_hi(v):
                h, f = divmod(v, 2)
                for d in range(2):
                    act.wait_ge(xo_done, 2 * v + d + 1)
                    split_hi(AT_[:, 0, 2 * h + d, f * HALF:(f + 1) * HALF], PS[:, 6 + d, :]).then_inc(xo_hi, 1)

            for v in range(1, 2 * XH + 3):
                if v >= 3:
                    x_o_hi(v - 3)
                if 2 <= v < 2 * XH + 2:
                    x_t_hi(v - 2)
                if v < 2 * XH:
                    x_exp(v)
                if v < 5:
                    for k in (2 * v - 2, 2 * v - 1):
                        weight_hi(act, N_CO + k)

            act.wait_ge(xo_lo, 4 * XH)
            for tb in range(TB):
                if tb >= 3:
                    evac_turned(n_h2, tb - 3, BT_, G_FFN)
                if tb == 0:
                    for k in range(KC):
                        weight_hi(act, N_CO + 8 + k)
                square_h(n_h2, tb, down_added, TB + tb + 1)
                if tb == TB - 2:
                    for k in range(4):
                        weight_hi(act, N_FF + k)
            evac_turned(n_h2, TB - 3, BT_, G_FFN)
            for k in range(4, 8):
                weight_hi(act, N_FF + k)

            def ff_hi(j, more, dst):
                act.wait_ge(raw_in[j % 4], 16 * ((N_FF + j) // 4 + 1) + more)
                split_hi(dst[:, j % 8, 0, :], RAW[:, j % 4, :]).then_inc(w_hi, 1)

            def relu_square(g8, i):
                f, half = i % 4, i // 4
                act.wait_ge(ff_relu, g8 + i + 1)
                nc.scalar.activation(PS[:, 4 + f, :], PS[:, 4 + f, :], ACT.Square).then_inc(ff_sq, 1)
                act.wait_ge(ff_sq, g8 + i + 1)
                split_hi(HID[:, 0, f, half * HALF:(half + 1) * HALF], PS[:, 4 + f, :]).then_inc(hid_hi, 1)

            def ff_group(g, first=False):
                act.wait_ge(down_done, 2 * TB + 2 * TB * g)
                for i in range(8):
                    relu_square(8 * g, i)
                    if first and i < 2:
                        evac_turned(n_h2, TB - 2 + i, BT_, G_FFN)
                    ff_hi(8 + i, 64 * g, W2S)

            def next_ff1(g):
                for j in range(16, 24):
                    sem_free, count = freed(N_FF + j - 16)
                    act.wait_ge(sem_free, count + (4 * g if j % 2 == 0 else 8 * g))
                    ff_hi(j, 64 * g, WS)

            ff_group(0, first=True)
            next_ff1(0)
            with act.Fori(1, FG - 1) as g:
                ff_group(g)
                next_ff1(g)
            ff_group(FG - 1)
            act.wait_ge(ff1_done, 8 * FG)
            act.dma_start(GF[:, :], norm_final_g.rearrange("(a n) -> a n", a=1).to_broadcast([P, D])).then_inc(gf_in, 16)
            for tb in range(TB):
                act.wait_ge(down_added, 2 * TB * FG + 2 * tb + 2)
                if tb:
                    act.wait_ge(n_fin.squared, tb)
                nc.scalar.activation(JUNK[:, :], H[:, tb, :], ACT.Square, accum_out=SS[:, tb:tb + 1]).then_inc(n_fin.squared, 1)

        @block.vector
        def _(dve):
            def scale_rows(norm, tb, dst, src):
                dve.wait_ge(norm.rstd, tb + 1)
                nc.vector.tensor_scalar(dst, src, RS[:, tb:tb + 1], None, ALU.mult).then_inc(norm.scaled, 1)

            def lo_turned(norm, tb, dst, gain):
                for b in range(2):
                    dve.wait_ge(norm.hi, 2 * tb + b + 1)
                    for k in range(4 * b, 4 * b + 4):
                        last = split_lo(dst[:, 1, k, tok(tb)], PS[:, 2 + b, tok(k % 4)], dst[:, 0, k, tok(tb)], CG[:, gain, k:k + 1])
                    last.then_inc(norm.lo, 1)

            def lo_v(tb):
                dve.wait_ge(v_hi, tb + 1)
                nc.vector.tensor_tensor(VHL[:, tb, :, HD:2 * HD], PS[:, tb % 2, :].rearrange("p (h d) -> p h d", h=HEADS),
                                        f32(VHL[:, tb, :, 0:HD]), ALU.subtract).then_inc(v_lo, 1)

            for tb in range(2):
                scale_rows(n_x, tb, xs(XSA, tb), xs(XSA, tb))
            dve.wait_ge(const_in, 6 * 16)
            for tb in range(TB):
                lo_turned(n_x, tb, AT_, G_MIX)
                if tb + 2 < TB:
                    scale_rows(n_x, tb + 2, xs(XSA, tb + 2), xs(XSA, tb + 2))
                if tb:
                    lo_v(tb - 1)
            lo_v(TB - 1)

            def lo_proj(j, i4, dst, bank):
                dve.wait_ge(qk_hi, i4 + j + 1)
                half = slice((j % 2) * HALF, (j % 2 + 1) * HALF)
                split_lo(dst[:, j // 2, 1, half], PS[:, bank, :], dst[:, j // 2, 0, half]).then_inc(qk_lo, 1)

            def take_qk(i, half):
                dve.wait_ge(z_done, 16 * i)
                dve.wait_ge(qk_lo, 4 * i + 4)
                t = slice(half * HALF, (half + 1) * HALF)
                nc.vector.tensor_copy(QKC[:, :, :, t], QKN[:, :, :, t]).then_inc(qk_now, 1)

            for j in range(4):
                lo_proj(j, 0, QKC, 4 + j)

            def scan(u, s):
                w = (s % TB + 1) * P
                m0 = sum(M_W[:s % 2])
                dve.wait_ge(sig, 2 * u + 2)
                m = MBUF[:, m0:m0 + w][:, ::-1]
                nc.vector.tensor_tensor_scan(m, m, m, 1.0, ALU.mult, ALU.bypass).then_inc(scanned, 1)

            def sum_o(u, s, head):
                dve.wait_ge(pv_done, u + 1)
                nc.vector.tensor_reduce(O[:, s % TB, bass.ds(head * HD, HD)], PS[:, 6, 0:2 * HD].rearrange("p (a d) -> p d a", a=2),
                                        AX.X, ALU.add).then_inc(o_done, 1)

            def lo_a(s, g24):
                tb = s % TB
                for g in range(1 if tb < 4 else 2):
                    n = min(4, tb + 1 - 4 * g) * P
                    dve.wait_ge(at_hi, groups_before(s) + g + 1 + g24)
                    keys = slice(g * HALF, g * HALF + n)
                    split_lo(ATR[tb % 2][:, 1, keys], PS[:, 4 + g, 0:n], ATR[tb % 2][:, 0, keys]).then_inc(at_lo, 1)

            def mask(u, s):
                tb = s % TB
                b, c = 2 * (s % 2) + tb // 4, (tb % 4) * P
                dve.wait_ge(z_done, u + 1)
                nc.vector.tensor_tensor(PS[:, b, c:c + P], PS[:, b, c:c + P], NEGM[:, :], ALU.add).then_inc(z_masked, 1)

            dve.wait_ge(const_made, 5)
            for u in range(5):
                if u >= 4:
                    lo_a(u - 4, 0)
                mask(u, u)
                if u >= 1:
                    scan(u - 1, u - 1)
            with dve.Fori(0, PAIRS - 1) as i:
                for t in range(16):
                    sum_o(16 * i + t, t, 2 * i + t // 8)
                    lo_a((t + 1) % 16, 24 * i + 24 * ((t + 1) // 16))
                    if t in (2, 4, 7, 10):
                        lo_proj((2, 4, 7, 10).index(t), 4 * i + 4, QKN, 7)
                    mask(16 * i + 5 + t, (5 + t) % 16)
                    scan(16 * i + 4 + t, (4 + t) % 16)
                    if t == 10:
                        take_qk(i + 1, 0)
                    if t == 11:
                        take_qk(i + 1, 1)
            last_pair = PAIRS - 1
            for t in range(16):
                u = 16 * last_pair + t
                sum_o(u, t, 2 * last_pair + t // 8)
                if t < 15:
                    lo_a(1 + t, 24 * last_pair)
                if t < 11:
                    mask(u + 5, 5 + t)
                if t < 12:
                    scan(u + 4, 4 + t)

            for k in range(4, KC):
                weight_lo(dve, N_GV + k)

            def group_sum(src_sem, which, tb, n, done):
                dve.wait_ge(src_sem, tb + 1)
                nc.vector.tensor_reduce(ST[:, 0, which, tb, 0:n], SQ[:, :].rearrange("p (g d) -> p g d", g=n), AX.X, ALU.add).then_inc(done, 1)

            def group_scale(which, tb, n, rstd, tile, done):
                dve.wait_ge(rstd, tb + 1)
                v = tile.rearrange("p (g d) -> p g d", g=n)
                r = ST[:, 1, which, tb, 0:n].rearrange("p (g a) -> p g a", a=1).to_broadcast([P, n, HALF // n])
                nc.vector.tensor_tensor(v, v, r, ALU.mult).then_inc(done, 1)

            dve.wait_ge(gb_in, 16)
            for tb in range(TB):
                if tb == 2:
                    dve.wait_ge(wt_hi, 1)
                    split_lo(WT[:, 1, :, :], PS[:, 2, :].rearrange("p (g t) -> p g t", g=GROUPS), WT[:, 0, :, :]).then_inc(wt_lo, 1)
                if tb == TB - 2:
                    for k in range(KC):
                        weight_lo(dve, N_U + k)
                group_sum(os_squared, 1, tb, HEADS, os_summed)
                group_sum(gv_squared, 0, tb, GROUPS, gv_summed)
                group_scale(1, tb, HEADS, os_rstd, O[:, tb, :], os_scaled)
                nc.vector.tensor_tensor(GV[:, tb % 2, :], GV[:, tb % 2, :], GB[:, :], ALU.mult).then_inc(gv_gained, 1)
                dve.wait_ge(gv_gained, tb + 1)
                group_scale(0, tb, GROUPS, gv_rstd, GV[:, tb % 2, :], gv_scaled)
                dve.wait_ge(vn_hi, tb + 1)
                split_lo(VN[:, 1, tb, :], GV[:, tb % 2, :], VN[:, 0, tb, :]).then_inc(vn_lo, 1)

            def lo_merged(i, tb, half):
                dve.wait_ge(mt_hi, i + 1)
                for k in range(4):
                    c = 4 * half + k
                    last = split_lo(AT_[:, 1, c, tok(tb)], PS[:, 2 + i % 2, tok(k)], AT_[:, 0, c, tok(tb)], CG[:, G_HEAD, c:c + 1])
                last.then_inc(mt_lo, 1)

            def gate(half, g):
                dve.wait_ge(mix_done, 4 * half + g + 1)
                dve.wait_ge(u_gelu, 4 * half + 4)
                u = U[:, 4 * half:4 * half + 4, tok(g)]
                nc.vector.scalar_tensor_tensor(u, PS[:, 4 + g, :].rearrange("p (c d) -> p c d", c=4), BSP[:, g:g + 1], u,
                                               ALU.add, ALU.mult).then_inc(gated, 1)

            def finish_a(half):
                for tb in range(4 * half, 4 * half + 4):
                    group_sum(a_squared, 2, tb, GROUPS, a_summed)
                    if tb > 4 * half:
                        group_scale(2, tb - 1, GROUPS, a_rstd, U[:, tb - 1, :], a_scaled)
                group_scale(2, 4 * half + 3, GROUPS, a_rstd, U[:, 4 * half + 3, :], a_scaled)

            for i in range(4):
                lo_merged(i, i, 1)
            for g in range(GROUPS):
                gate(0, g)
            finish_a(0)
            lo_merged(4, 4, 1)
            lo_merged(5, 0, 0)
            lo_merged(6, 5, 1)
            lo_merged(7, 1, 0)
            for k in range(KC):
                weight_lo(dve, N_OUT + k)
            lo_merged(8, 6, 1)
            lo_merged(9, 2, 0)
            lo_merged(10, 7, 1)
            lo_merged(11, 3, 0)
            for g in range(GROUPS):
                gate(1, g)
            finish_a(1)

            def add_block(done, i, added, tb, c):
                dve.wait_ge(done, i + 1)
                hc = H[:, tb, c * HALF:(c + 1) * HALF]
                nc.vector.tensor_tensor(hc, PS[:, i % 2, :], hc, ALU.add).then_inc(added, 1)

            for tb in range(TB):
                if tb >= 2 and tb < 6:
                    lo_merged(10 + tb, tb + 2, 0)
                dve.wait_ge(x2_in[tb], 16)
                if tb == TB - 1:
                    for k in range(KC):
                        weight_lo(dve, N_OUT + 8 + k)
                add_block(wout_done, tb, wout_added, tb, 0)
            for tb in range(TB):
                if tb >= 3:
                    lo_turned(n_h1, tb - 3, BT_, G_CROSS)
                add_block(wout_done, TB + tb, wout_added, tb, 1)
                if tb:
                    scale_rows(n_h1, tb - 1, xs(XSB, tb - 1), H[:, tb - 1, :].rearrange("p (k n) -> p k n", k=KC))
            scale_rows(n_h1, TB - 1, xs(XSB, TB - 1), H[:, TB - 1, :].rearrange("p (k n) -> p k n", k=KC))
            lo_turned(n_h1, TB - 3, BT_, G_CROSS)

            def lo_q2(i, m, f):
                dve.wait_ge(q2_hi, i + 1)
                c = slice(f * HALF, (f + 1) * HALF)
                split_lo(AT_[:, 1, m, c], PS[:, 4 + i % 4, :], AT_[:, 0, m, c]).then_inc(q2_lo, 1)

            for i in range(4):
                lo_q2(i, i, 0)
                if i < 2:
                    lo_turned(n_h1, TB - 2 + i, BT_, G_CROSS)
            for mt in range(MB):
                scale_rows(n_mem, mt, XM[mt][:, :, :], XM[mt][:, :, :])
            for i in range(4, 8):
                lo_q2(i, i - 4, 1)
            for i in range(8, 12):
                lo_q2(i, i - 4, 0)
            for mt in range(MB):
                for b in range(2):
                    dve.wait_ge(n_mem.hi, 2 * mt + b + 1)
                    for k in range(4 * b, 4 * b + 4):
                        last = split_lo(MEMT[:, 1, k, tok(mt)], PS[:, 2 * mt + b, tok(k % 4)], MEMT[:, 0, k, tok(mt)],
                                        CG[:, G_MEM, k:k + 1])
                    last.then_inc(n_mem.lo, 1)
            for i in range(12, 16):
                lo_q2(i, i - 8, 1)
            for m in range(KC):
                dve.wait_ge(k2_hi, m + 1)
                split_lo(K2T[:, 1, m, :], PS[:, 4 + m % 4, 0:N_MEM], K2T[:, 0, m, :]).then_inc(k2_lo, 1)
                weight_lo(dve, N_CK + 8 + 2 * m + 1)

            def x_max(v):
                if v >= 2:
                    dve.wait_ge(xs_exp, 4 * (v - 1))
                for b in range(2):
                    dve.wait_ge(xs_done, 2 * v + b + 1)
                    nc.vector.tensor_reduce(XST[:, v % 2, 0, 2 * b:2 * b + 2], PS[:, 2 * (v % 2) + b, :].rearrange("p (q m) -> p q m", q=2),
                                            AX.X, ALU.max).then_inc(xs_max, 1)
                dve.wait_ge(xs_max, 2 * v + 2)
                nc.vector.tensor_scalar(XST[:, v % 2, 1, :], XST[:, v % 2, 0, :], -X_SCALE, None, ALU.mult).then_inc(xs_neg, 1)

            def x_inv(v):
                dve.wait_ge(xs_exp, 4 * v + 4)
                nc.vector.reciprocal(XST[:, v % 2, 3, :], XST[:, v % 2, 2, :]).then_inc(xs_inv, 1)

            def x_t_lo(v):
                for mb in range(MB):
                    dve.wait_ge(xt_hi, 2 * v + mb + 1)
                    split_lo(pt_at(v, 1, mb), PS[:, 4 + mb, :], pt_at(v, 0, mb)).then_inc(xt_lo, 1)

            def x_o_lo(v):
                h, f = divmod(v, 2)
                for d in range(2):
                    dve.wait_ge(xo_hi, 2 * v + d + 1)
                    c = slice(f * HALF, (f + 1) * HALF)
                    split_lo(AT_[:, 1, 2 * h + d, c], PS[:, 6 + d, :], AT_[:, 0, 2 * h + d, c]).then_inc(xo_lo, 1)

            x_max(0)
            for c in range(2):
                for mb in range(MB):
                    if mb == MB - 1 and c == 0:
                        for k in range(1, KC, 2):
                            weight_lo(dve, N_CV + 8 + k)
                    dve.wait_ge(v2_hi, MB * c + mb + 1)
                    split_lo(v2_at(1, mb, c), PS[:, 6 + mb, :], v2_at(0, mb, c)).then_inc(v2_lo, 1)

            for v in range(1, 2 * XH + 3):
                if v < 2 * XH + 1:
                    x_inv(v - 1)
                if v >= 3:
                    x_o_lo(v - 3)
                if 2 <= v < 2 * XH + 2:
                    x_t_lo(v - 2)
                if v < 2 * XH:
                    x_max(v)

            for tb in range(TB):
                if tb == TB - 1:
                    for k in range(KC):
                        weight_lo(dve, N_CO + 8 + k)
                add_block(down_done, tb, down_added, tb, 0)
            for tb in range(TB):
                if tb >= 3:
                    lo_turned(n_h2, tb - 3, BT_, G_FFN)
                add_block(down_done, TB + tb, down_added, tb, 1)
                if tb:
                    scale_rows(n_h2, tb - 1, xs(XSB, tb - 1), H[:, tb - 1, :].rearrange("p (k n) -> p k n", k=KC))
            scale_rows(n_h2, TB - 1, xs(XSB, TB - 1), H[:, TB - 1, :].rearrange("p (k n) -> p k n", k=KC))
            lo_turned(n_h2, TB - 3, BT_, G_FFN)

            def ff_hidden(g, first=False):
                for i in range(9):
                    if i < 8:
                        dve.wait_ge(ff1_done, 8 * g + i + 1)
                        nc.vector.tensor_scalar(PS[:, 4 + i % 4, :], PS[:, 4 + i % 4, :], 0.0, None, ALU.max).then_inc(ff_relu, 1)
                    if i >= 1:
                        f, half = (i - 1) % 4, (i - 1) // 4
                        c = slice(half * HALF, (half + 1) * HALF)
                        dve.wait_ge(hid_hi, 8 * g + i)
                        split_lo(HID[:, 1, f, c], PS[:, 4 + f, :], HID[:, 0, f, c]).then_inc(hid_lo, 1)
                    if first and i < 2:
                        lo_turned(n_h2, TB - 2 + i, BT_, G_FFN)

            def ff_add(g, i):
                tb, nh = divmod(i, 2)
                dve.wait_ge(down_done, 2 * TB + 2 * TB * g + i + 1)
                hc = H[:, tb, nh * HALF:(nh + 1) * HALF]
                nc.vector.tensor_tensor(hc, PS[:, i % 4, :], hc, ALU.add).then_inc(down_added, 1)

            def make_y(tb):
                dve.wait_ge(n_fin.rstd, tb + 1)
                nc.vector.scalar_tensor_tensor(YT[:, tb, :], H[:, tb, :], RS[:, tb:tb + 1], GF[:, :], ALU.mult, ALU.mult).then_inc(y_made, 1)

            ff_hidden(0, first=True)
            for i in range(2 * TB):
                ff_add(0, i)
            with dve.Fori(1, FG - 1) as g:
                ff_hidden(g)
                for i in range(2 * TB):
                    ff_add(g, i)
            ff_hidden(FG - 1)
            dve.wait_ge(gf_in, 16)
            for i in range(2 * TB):
                ff_add(FG - 1, i)
                if i % 2 and i > 1:
                    make_y(i // 2 - 1)
            make_y(TB - 1)

        @block.tensor
        def _(pe):
            mm = nc.tensor.matmul

            def three(out, w_hi_, w_lo_, m_hi, m_lo, first, last, between=iter(())):
                mm(out, w_hi_, m_hi, start=first, stop=False)
                next(between, None)
                mm(out, w_hi_, m_lo, start=False, stop=False)
                next(between, None)
                return mm(out, w_lo_, m_hi, start=False, stop=last)

            def turn(chunk, bank, ks):
                for q, k in enumerate(ks):
                    last = nc.tensor.transpose(PS[:, bank, tok(q)], chunk(k), ident[:, :])
                return last

            def turn_block(norm, tb, stage):
                pe.wait_ge(norm.scaled, tb + 1)
                for b in range(2):
                    if tb:
                        pe.wait_ge(norm.lo, 2 * (tb - 1) + b + 1)
                    turn(lambda k: stage[:, k, tok(tb)], 2 + b, range(4 * b, 4 * b + 4)).then_inc(norm.turned, 1)

            def token_major(src, tb, bank, n0, done, last_block):
                for k in range(KC):
                    if tb == 0:
                        wait_lo(pe, n0 + k)
                    last = three(PS[:, bank, :], src[:, 0, k, tok(tb)], src[:, 1, k, tok(tb)], WS[:, k, 0, :], WS[:, k, 1, :],
                                 k == 0, k == KC - 1)
                    if last_block and k < KC - 1:
                        last.then_inc(w_used, 1)
                last.then_inc(done, 1)

            def feature_major(src, bank, place, n0, more, cols, done, first_half, last_half):
                for k in range(KC):
                    if first_half and k % 4 == 0:
                        wait_lo(pe, n0 + k // 4, more)
                    w = WS[:, place + k // 4, :, tok(k % 4)]
                    width = cols.stop - cols.start
                    last = three(PS[:, bank, 0:width], w[:, 0, :], w[:, 1, :], src[:, 0, k, cols], src[:, 1, k, cols], k == 0, k == KC - 1)
                    if last_half and k == 3:
                        last.then_inc(w_used, 1)
                last.then_inc(done, 1)

            halves = (slice(0, HALF), slice(HALF, SEQ))

            pe.wait_ge(const_made, 5)
            turn_block(n_x, 0, XSA)
            turn_block(n_x, 1, XSA)
            for tb in range(TB):
                pe.wait_ge(n_x.lo, 2 * tb + 2)
                if tb >= 2:
                    pe.wait_ge(v_lo, tb - 1)
                token_major(AT_, tb, tb % 2, N_V, v_done, tb == TB - 1)
                if tb + 2 < TB:
                    turn_block(n_x, tb + 2, XSA)

            def project(j, ks, pair, bank, between=iter(())):
                for k in ks:
                    place = 2 * (j // 2) + k // 4
                    if k == 0 and not (isinstance(pair, int) and pair == 0):
                        pe.wait_ge(qk_lo, 4 * pair + j)
                    if j % 2 == 0 and k % 4 == 0:
                        wait_lo(pe, N_QK + place, 4 * pair)
                    w = WS[:, place, :, tok(k % 4)]
                    last = three(PS[:, bank, :], w[:, 0, :], w[:, 1, :], AT_[:, 0, k, halves[j % 2]], AT_[:, 1, k, halves[j % 2]],
                                 k == 0, k == KC - 1, between)
                    if j % 2 == 1 and k == 3:
                        last.then_inc(w_used, 1)
                    if k == KC - 1:
                        last.then_inc(proj_done, 1)

            for j in range(4):
                project(j, range(KC), 0, 4 + j)

            def logits(u, s, pair, between=iter(())):
                hh, tb = divmod(s, TB)
                if isinstance(u, int) and u == 0:
                    pe.wait_ge(qk_lo, 4)
                elif s in (0, TB // 2 - 1) and not isinstance(u, int):
                    pe.wait_ge(qk_now, 2 * pair - 1 + (s > 0))
                if not (isinstance(u, int) and u < 2):
                    pe.wait_ge(sig, 2 * u - 2)
                rows = slice(HD * hh, HD * hh + HD)
                w = (tb + 1) * P
                for b in range(1 if w <= HALF else 2):
                    keys = slice(b * HALF, min(w, (b + 1) * HALF))
                    last = three(PS[:, 2 * (s % 2) + b, 0:keys.stop - keys.start],
                                 QKC[rows, 0, 0, tok(tb)], QKC[rows, 0, 1, tok(tb)], QKC[rows, 1, 0, keys], QKC[rows, 1, 1, keys], True, True, between)
                last.then_inc(z_done, 1)

            def turn_a(u, s, g24, between=iter(())):
                tb = s % TB
                b0 = sum(BE_W[:s % 4])
                pe.wait_ge(a_done, u + 1)
                for g in range(1 if tb < 4 else 2):
                    if not (isinstance(u, int) and u == 0) and g <= (s - 1) % TB // 4:
                        pe.wait_ge(at_lo, groups_before(s - 1) + g + 1 + g24)
                    for k in range(4 * g, min(4 * g + 4, tb + 1)):
                        next(between, None)
                        last = nc.tensor.transpose(PS[:, 4 + g, tok(k % 4)], BEBUF[:, b0 + k * P:b0 + (k + 1) * P], ident[:, :])
                    last.then_inc(t_done, 1)

            def values(u, s, g24, head):
                tb = s % TB
                if s:
                    pe.wait_ge(o_done, u)
                for sb in range(tb + 1):
                    if sb % 4 == 0:
                        pe.wait_ge(at_lo, groups_before(s) + sb // 4 + 1 + g24)
                    for part in range(2):
                        last = mm(PS[:, 6, 0:2 * HD], ATR[tb % 2][:, part, tok(sb)], VHL[:, sb, head, :],
                                  start=sb == 0 and part == 0, stop=sb == tb and part == 1)
                        if sb == tb and part == 1:
                            last.then_inc(pv_done, 1)
                        yield

            pe.wait_ge(v_lo, TB)
            for u in range(4):
                logits(u, u, 0)
                if u >= 3:
                    turn_a(u - 3, u - 3, 0)
            PARTS = {1: (0, range(4)), 2: (0, range(4, 8)), 3: (1, range(4)), 4: (1, range(4, 8)),
                     5: (2, range(3)), 6: (2, range(3, 6)), 7: (2, range(6, 8)), 8: (3, range(3)), 9: (3, range(3, 6)), 10: (3, range(6, 8))}
            with pe.Fori(0, PAIRS - 1) as i:
                for t in range(16):
                    value_steps = values(16 * i + t, t, 24 * i, 2 * i + t // TB)
                    logits(16 * i + 4 + t, (4 + t) % 16, i + (4 + t) // 16)
                    turn_a(16 * i + 1 + t, (1 + t) % 16, 24 * i + 24 * (t // 15), value_steps)
                    if t in PARTS:
                        project(*PARTS[t], i + 1, 7, value_steps)
                    for _ in value_steps:
                        pass
                pe.wait_ge(o_done, 16 * i + 16)
            for t in range(16):
                u = 16 * (PAIRS - 1) + t
                value_steps = values(u, t, 24 * (PAIRS - 1), 2 * (PAIRS - 1) + t // TB)
                if t < 12:
                    logits(u + 4, 4 + t, PAIRS - 1)
                if t < 15:
                    turn_a(u + 1, 1 + t, 24 * (PAIRS - 1), value_steps)
                for _ in value_steps:
                    pass

            pe.wait_ge(sig, 2 * 16 * PAIRS)
            for tb in range(TB):
                if tb >= 2:
                    pe.wait_ge(gv_gelu, tb - 1)
                token_major(AT_, tb, tb % 2, N_GV, gv_done, tb == TB - 1)
                if tb == 1:
                    pe.wait_ge(wsp_masked, 1)
                    turn(lambda g: WSP[:, g, :], 2, range(GROUPS)).then_inc(wt_turned, 1)

            merged_at = {}

            def turn_merged(tb, half):
                i = len(merged_at)
                merged_at[tb, half] = i
                if half == 1:
                    pe.wait_ge(os_scaled, tb + 1)
                else:
                    pe.wait_ge(a_scaled, tb + 1)
                if i >= 2:
                    pe.wait_ge(mt_lo, i - 1)
                else:
                    pe.wait_ge(wt_lo, 1)
                turn(lambda k: (O if half else U)[:, tb, tok(k)], 2 + i % 2, range(4)).then_inc(mt_turned, 1)

            def mix(half):
                pe.wait_ge(vn_lo, TB)
                for g in range(GROUPS):
                    if half == 0:
                        pe.wait_ge((at_lo, at_lo, o_done, qk_lo)[g], (24 * PAIRS, 24 * PAIRS, 16 * PAIRS, 4 * PAIRS)[g])
                    else:
                        pe.wait_ge(gated, g + 1)
                    v = VN[:, :, 4 * half:4 * half + 4, tok(g)]
                    three(PS[:, 4 + g, :], WT[:, 0, g, :], WT[:, 1, g, :], v[:, 0], v[:, 1], True, True).then_inc(mix_done, 1)

            AFTER_U = {1: [(0, 1)], 2: [(1, 1)], 3: [(2, 1)], 4: [(3, 1)], 5: [(4, 1), (0, 0)], 6: [(5, 1), (1, 0)],
                       7: [(6, 1), (2, 0)]}
            for tb in range(TB):
                pe.wait_ge(u_gelu if tb >= 2 else gv_gelu, tb - 1 if tb >= 2 else TB)
                token_major(AT_, tb, tb % 2, N_U, u_done, tb == TB - 1)
                for at_tb, half in AFTER_U.get(tb, ()):
                    turn_merged(at_tb, half)
                if tb == 4:
                    mix(0)
            mix(1)
            turn_merged(7, 1)
            turn_merged(3, 0)

            pe.wait_ge(u_gelu, TB)
            for tb in range(TB):
                if 2 <= tb < 6:
                    turn_merged(tb + 2, 0)
                pe.wait_ge(mt_lo, max(merged_at[tb, 0], merged_at[tb, 1]) + 1)
                if tb >= 2:
                    pe.wait_ge(wout_added, tb - 1)
                token_major(AT_, tb, tb % 2, N_OUT, wout_done, tb == TB - 1)
            for tb in range(TB):
                pe.wait_ge(wout_added, TB + tb - 1)
                token_major(AT_, tb, tb % 2, N_OUT + 8, wout_done, tb == TB - 1)
                if tb >= 2:
                    turn_block(n_h1, tb - 2, XSB)

            def q2(i, m, f):
                if i >= 4:
                    pe.wait_ge(q2_lo, i - 3)
                feature_major(BT_, 4 + i % 4, 2 * (m % 4), N_CQ + 2 * m, 0, halves[f], q2_done, f == 0, f == 1)

            pe.wait_ge(n_h1.lo, TB)
            for i in range(4):
                q2(i, i, 0)
                if i < 2:
                    turn_block(n_h1, TB - 2 + i, XSB)
            pe.wait_ge(n_h1.lo, 2 * TB)
            for i in range(4, 8):
                q2(i, i - 4, 1)
            for i in range(8, 12):
                if i == 9:
                    for mt in range(MB):
                        pe.wait_ge(n_mem.scaled, mt + 1)
                        for b in range(2):
                            turn(lambda k: XM[mt][:, k, :], 2 * mt + b, range(4 * b, 4 * b + 4)).then_inc(n_mem.turned, 1)
                q2(i, i - 4, 0)
            for i in range(12, 16):
                q2(i, i - 8, 1)
            pe.wait_ge(n_mem.lo, 2 * MB)
            for m in range(KC):
                if m < 4:
                    pe.wait_ge(q2_lo, 12 + m + 1)
                else:
                    pe.wait_ge(k2_lo, m - 3)
                feature_major(MEMT, 4 + m % 4, 2 * (m % 4), N_CK + 2 * m, 0, slice(0, N_MEM), k2_done, True, True)

            def x_logits(v):
                h, f = divmod(v, 2)
                if v >= 2:
                    pe.wait_ge(xs_exp, 4 * (v - 1))
                for q in range(4):
                    out = PS[:, 2 * (v % 2) + q // 2, (q % 2) * N_MEM:(q % 2 + 1) * N_MEM]
                    for c in (2 * h, 2 * h + 1):
                        t = tok(4 * f + q)
                        last = three(out, AT_[:, 0, c, t], AT_[:, 1, c, t], K2T[:, 0, c, :], K2T[:, 1, c, :], c == 2 * h, c == 2 * h + 1)
                    if q % 2:
                        last.then_inc(xs_done, 1)

            def x_turn(v):
                pe.wait_ge(xs_prob, v + 1)
                for mb in range(MB):
                    if v:
                        pe.wait_ge(xt_lo, 2 * (v - 1) + mb + 1)
                    turn(lambda q: EP[v % 2][:, q, tok(mb)], 4 + mb, range(4)).then_inc(xt_done, 1)

            def x_values(v):
                h = v // 2
                pe.wait_ge(xt_lo, 2 * v + 2)
                if v == 0:
                    pe.wait_ge(v2_lo, 2 * MB)
                for d in range(2):
                    if v:
                        pe.wait_ge(xo_lo, 2 * (v - 1) + d + 1)
                    c, part = divmod(h * XD + d * P, HALF)
                    cols = slice(part, part + P)
                    for mb in range(MB):
                        last = three(PS[:, 6 + d, :], v2_at(0, mb, c)[:, cols], v2_at(1, mb, c)[:, cols], pt_at(v, 0, mb), pt_at(v, 1, mb),
                                     mb == 0, mb == MB - 1)
                    last.then_inc(xo_done, 1)

            pe.wait_ge(k2_lo, KC)
            x_logits(0)
            for c in range(2):
                for mb in range(MB):
                    if c:
                        pe.wait_ge(v2_lo, mb + 1)
                    token_major(MEMT, mb, 6 + mb, N_CV + 8 * c, v2_done, mb == MB - 1)
            for v in range(1, 2 * XH + 2):
                if v >= 3:
                    x_values(v - 3)
                if 2 <= v:
                    x_turn(v - 2)
                if v < 2 * XH:
                    x_logits(v)

            def co(i):
                c, tb = divmod(i, TB)
                if i >= 2:
                    pe.wait_ge(down_added, i - 1)
                token_major(AT_, tb, tb % 2, N_CO + 8 * c, down_done, tb == TB - 1)
                if c and tb >= 2:
                    turn_block(n_h2, tb - 2, XSB)

            pe.wait_ge(xo_lo, 4 * XH - 2)
            pe.wait_ge(xs_exp, 8 * XH)
            co(0)
            x_values(2 * XH - 1)
            for i in range(1, 2 * TB):
                if i == TB // 2:
                    pe.wait_ge(xo_lo, 4 * XH)
                co(i)

            def ff1(g, i):
                f, half = i % 4, i // 4
                if i >= 4:
                    pe.wait_ge(hid_lo, 8 * g + i - 3)
                feature_major(BT_, 4 + f, 2 * f, N_FF + 2 * f, 16 * g, halves[half], ff1_done, half == 0, half == 1)

            def down(g):
                for i in range(2 * TB):
                    tb, nh = divmod(i, 2)
                    if i == 0 or i >= 4:
                        pe.wait_ge(down_added, 2 * TB + 2 * TB * g + max(i - 3, 0))
                    if tb in (0, TB // 2) and nh == 0:
                        pe.wait_ge(hid_lo, 8 * g + 4 + tb)
                    for k in range(4):
                        if tb == 0:
                            wait_lo(pe, N_FF + 8 + 4 * nh + k, 16 * g)
                        last = three(PS[:, i % 4, :], HID[:, 0, k, tok(tb)], HID[:, 1, k, tok(tb)],
                                     W2S[:, 4 * nh + k, 0, :], W2S[:, 4 * nh + k, 1, :], k == 0, k == 3)
                    last.then_inc(down_done, 1)

            pe.wait_ge(n_h2.lo, TB)
            for i in range(8):
                if i == 4:
                    pe.wait_ge(n_h2.lo, 2 * TB)
                ff1(0, i)
                if i < 2:
                    turn_block(n_h2, TB - 2 + i, XSB)
            down(0)
            with pe.Fori(1, FG) as g:
                for i in range(8):
                    ff1(g, i)
                down(g)


_INS = ["x", "mem", "norm_mix_g", "w_in", "gm_v_norm_g", "w_spatial", "b_spatial", "head_norm_g", "w_out", "norm_cross_g",
        "norm_mem_g", "w_cq", "w_ckv", "w_co", "norm_ffn_g", "w_ff1", "w_ff2", "norm_final_g"]


def kernel(**inputs):
    import numpy as _np
    import concourse.bacc as _bacc
    from concourse import mybir as _mybir
    from concourse.bass_utils import run_bass_kernel_spmd as _run

    nc = _bacc.Bacc("TRN2", target_bir_lowering=False, num_devices=1)
    arrays, args = {}, []
    for name in _INS:
        a = _np.ascontiguousarray(inputs[name])
        if name != "norm_final_g":
            a = a.reshape(a.shape[1:])
        arrays[f"in_{name}"] = a
        args.append(nc.dram_tensor(f"in_{name}", a.shape, _mybir.dt.from_np(a.dtype), kind="ExternalInput").ap())
    out = nc.dram_tensor("out_y", (SEQ, D), F32, kind="ExternalOutput").ap()
    with nc.allow_non_contiguous_dma(reason="gains and biases go one feature to a partition"):
        build(nc, *args, out)
    r = _run(nc, [arrays], core_ids=[0])
    return r.results[0]["out_y"].reshape(1, SEQ, D)
```

```python
import concourse.bass as bass
from concourse import mybir
from concourse.alu_op_type import AluOpType as ALU
import numpy as np

F32 = mybir.dt.float32
F32R = mybir.dt.float32r
ACT = mybir.ActivationFunctionType
AX = mybir.AxisListType

P = 128
D = 1024
SEQ = 1024
TB = SEQ // P
KC = D // P
HALF = 512
GROUPS = 4
HEADS = 8
HD = 64
PAIRS = HEADS // 2
N_MEM = 256
MB = N_MEM // P
XH = 4
XD = D // XH
DFF = 4 * D
FG = DFF // HALF
EPS = 1e-6
Z_SCALE = HD ** -0.5
X_SCALE = XD ** -0.5
NEG = -1e30

COL_U, COL_GV, COL_Q, COL_K, COL_V = 0, 512, 1024, 1536, 2048

N_V = 0
N_QK = N_V + 8
N_GV = N_QK + 4 * PAIRS
N_U = N_GV + 8
N_OUT = N_U + 8
N_CQ = N_OUT + 16
N_CK = N_CQ + 16
N_CV = N_CK + 16
N_CO = N_CV + 16
N_FF = N_CO + 16
RAW_SLOTS = 4
WS_SLOTS = 8


def lo_on_vector(n):
    return N_U <= n < N_CQ or N_CO + 8 <= n < N_FF or (n < N_QK or N_CK + 8 <= n < N_CO) and n % 2 == 1


def lo_count(n):
    return sum(lo_on_vector(m) == lo_on_vector(n) for m in range(n + 1))


def used_count(n):
    def counted(m):
        if N_QK <= m < N_GV or N_CQ <= m < N_CV or m >= N_FF:
            return m % 2 == 0
        return m % 8 < 7
    return sum(counted(m) for m in range(n + 1))


def groups_before(s):
    head, tb = divmod(s, TB)
    return head * 12 + (tb if tb < 4 else 4 + 2 * (tb - 4))


PARTS = {0: ((1, 3), (1, 4)), 1: ((1, 5), (1, 6)), 2: ((1, 7),),
         3: ((2, 0), (2, 1)), 4: ((2, 2), (2, 3)), 5: ((2, 4), (2, 5)), 6: ((2, 6), (2, 7)),
         7: ((3, 0), (3, 1), (3, 2)), 8: ((3, 3), (3, 4), (3, 5)), 9: ((3, 6), (3, 7)),
         11: ((0, 0), (0, 1)), 12: ((0, 2), (0, 3)), 13: ((0, 4), (0, 5)), 14: ((0, 6), (0, 7)), 15: ((1, 0), (1, 1), (1, 2))}
EVACUATE = {2: 1, 6: 2, 9: 3, 14: 0}
O_STEPS = {PAIRS - 2: {0: 0, 2: 1, 4: 2, 6: 3}, PAIRS - 1: {0: 4, 3: 5, 9: 6}}
OUT_BANKS = (0, 1, 4, 5, 6, 7, 0, 1)
V_STEPS = (3, 3, 3, 3, 2, 2, 2, 1)
V_BANKS = (7, 7, 7, 7, 7, 7, 7, 1)
V_START = 13


def v_chunks(pair, t):
    step = 16 * (pair - (PAIRS - 2)) + t - V_START
    for tb, n in enumerate(V_STEPS):
        if 0 <= step < n:
            each = -(-KC // n)
            return [(tb, k) for k in range(each * step, min(KC, each * (step + 1)))]
        step -= n
    return []


def build(nc, x, mem, norm_mix_g, w_in, gm_v_norm_g, w_spatial, b_spatial, head_norm_g, w_out,
          norm_cross_g, norm_mem_g, w_cq, w_ckv, w_co, norm_ffn_g, w_ff1, w_ff2, norm_final_g, y):
    KB = 1024
    base = (nc.sbuf_base + 31) // 32 * 32
    A0 = base
    B0 = A0 + 64 * KB
    H0 = B0 + 64 * KB
    WS0 = H0 + 32 * KB
    RAW0 = WS0 + 32 * KB
    MISC0 = RAW0 + 8 * KB
    misc_at = [MISC0]

    def at(name, shape, dtype, offset):
        return nc.alloc_sbuf_tensor_at(name, shape, dtype, offset=offset)

    def misc(name, shape, dtype=F32):
        t = at(name, shape, dtype, misc_at[0])
        misc_at[0] += (4 * int(np.prod(shape[1:])) + 31) // 32 * 32
        return t

    AT_ = at("actA", [P, 2, KC, SEQ], F32R, A0)
    BT_ = at("actB", [P, 2, KC, SEQ], F32R, B0)
    XSA = at("stageA", [P, KC, SEQ], F32, A0 + 32 * KB)
    XSB = at("stageB", [P, KC, SEQ], F32, B0 + 32 * KB)
    H = at("h", [P, TB, D], F32, H0)
    WS = at("w_split", [P, WS_SLOTS, 2, HALF], F32R, WS0)
    WGV = at("w_split_gv", [P, 4, 2, HALF], F32R, H0)
    RAW = at("w_raw", [P, RAW_SLOTS, HALF], F32, RAW0)

    VHL = at("v_parts", [P, TB, HEADS, 2 * HD], F32R, B0)
    VF = at("v_columns", [P, TB, HEADS, 2 * HD], F32, B0)
    O = at("attn_out", [P, TB, HALF], F32, B0 + 32 * KB)
    M_W = [896, 1024]
    BE_W = [640, 768, 896, 1024]
    MBUF = at("one_minus_beta", [P, sum(M_W)], F32, B0 + 48 * KB)
    NEGM = at("causal_neg", [P, P], F32, B0 + 48 * KB + 4 * sum(M_W))
    A_T_EVEN = misc_at[0]
    ATR = [misc("a_T_even", [P, 2, 7 * P], F32R), at("a_T_odd", [P, 2, SEQ], F32R, B0 + 56 * KB)]
    BEBUF = at("beta", [P, sum(BE_W)], F32, WS0 + 16 * KB)
    QKN = at("qk_next", [P, 2, 2, SEQ], F32R, H0)
    QKC = at("qk_now", [P, 2, 2, SEQ], F32R, H0 + 16 * KB)

    VN = at("v_norm", [P, TB, 2, HALF], F32R, B0)
    GV = at("v_gelu", [P, TB, 2, HALF], F32, B0)[:, :, 0, :]
    U = at("u_gated", [P, TB, HALF], F32, B0 + 48 * KB)
    WT = at("w_spatial_T", [P, 2, GROUPS, P], F32R, H0 + 16 * KB)
    WSP = at("w_spatial_masked", [P, GROUPS, P], F32, H0 + 20 * KB)
    GB = at("v_gain", [P, HALF], F32, H0 + 22 * KB)
    SQ = at("squares", [P, 2, HALF], F32, H0 + 26 * KB)
    ST = at("stats", [P, 2, 2, TB, GROUPS], F32, H0 + 30 * KB)

    XM = [at("mem_tile0", [P, KC, P], F32, A0 + 7 * 4 * KB), at("mem_tile1", [P, KC, P], F32, A0 + 32 * KB + 7 * 4 * KB)]
    MEMT = BT_[:, :, :, 0:N_MEM]
    K2T = BT_[:, :, :, N_MEM:2 * N_MEM]
    BF = at("actB_f32", [P, 2, KC, SEQ], F32, B0)

    def v2_at(part, mb, c):
        return BT_[:, part, 2 * mb + c, HALF:SEQ]

    def pt_at(v, part, mb):
        return BT_[:, part, 4 + 2 * (v % 2) + mb, HALF:SEQ]


    HID = at("hid_T", [P, 2, 4, SEQ], F32R, A0)
    W2S = at("w2_split", [P, 8, 2, HALF], F32R, A0 + 32 * KB)
    JUNK = at("junk", [P, D], F32, B0)
    YT = at("y_tiles", [P, TB, D], F32, B0 + 32 * KB)
    GF = at("final_gain", [P, D], F32, WS0)

    EP = [at("p_exp_even", [P, 4, N_MEM], F32, A_T_EVEN), BF[:, 0, 0:4, 0:N_MEM]]
    XST = at("softmax_stats", [P, 2, 4, 4], F32, A_T_EVEN + 4 * KB)

    ident = misc("identity", [P, P])
    CG = misc("gains", [P, 5, KC])
    BSP = misc("b_sp", [P, GROUPS])
    SS = misc("row_sums", [P, TB])
    RS = misc("row_rstd", [P, TB])
    NEGH = misc("minus_half", [P, 8])
    G_MIX, G_HEAD, G_CROSS, G_MEM, G_FFN = range(5)

    PS = nc.alloc_psum_tensor("ps", [P, 8, HALF], F32)

    def f32(ap):
        return ap.bitcast(F32)

    S = {}

    def sem(name):
        S[name] = nc.alloc_semaphore(name)
        return S[name]

    raw_in = [sem(f"raw_in{i}") for i in range(RAW_SLOTS)]
    w_hi = sem("w_hi")
    w_lo_pool = sem("w_lo_pool")
    w_lo_dve = sem("w_lo_dve")
    w_used = sem("w_used")
    mix_gain_in = sem("mix_gain_in")
    const_in = sem("const_in")
    const_made = sem("const_made")
    x_in = [sem(f"x_in{t}") for t in range(TB)]

    class Norm:
        def __init__(self, name):
            self.squared = sem(name + "_squared")
            self.mean = sem(name + "_mean")
            self.rstd = sem(name + "_rstd")
            self.scaled = sem(name + "_scaled")
            self.turned = sem(name + "_turned")
            self.hi = sem(name + "_hi")
            self.lo = sem(name + "_lo")

    n_x, n_h1, n_mem, n_h2, n_fin = (Norm(n) for n in ("x", "h1", "mem", "h2", "fin"))

    v_done, v_hi, v_lo = sem("v_done"), sem("v_hi"), sem("v_lo")
    proj_done, qk_hi, qk_lo, qk_now = sem("proj_done"), sem("qk_hi"), sem("qk_lo"), sem("qk_now_ready")
    z_done, z_masked, sig, scanned, a_done = sem("z_done"), sem("z_masked"), sem("sig"), sem("scanned"), sem("a_done")
    t_done, at_hi, at_lo, pv_done, o_done = sem("t_done"), sem("at_hi"), sem("at_lo"), sem("pv_done"), sem("o_done")

    wsp_in, wsp_masked, wt_turned, wt_hi, wt_lo = (sem(n) for n in ("wsp_in", "wsp_masked", "wt_turned", "wt_hi", "wt_lo"))
    gb_in = sem("gb_in")
    gv_done, gv_copied, gv_gelu, gv_squared, gv_summed, gv_mean, gv_rstd = (sem("gv_" + n) for n in ("done", "copied", "gelu", "squared", "summed", "mean", "rstd"))
    gv_gained, gv_scaled, vn_hi, vn_lo = sem("gv_gained"), sem("gv_scaled"), sem("vn_hi"), sem("vn_lo")
    os_squared, os_summed, os_mean, os_rstd, os_scaled = (sem("o_" + n) for n in ("squared", "summed", "mean", "rstd", "scaled"))
    u_done, u_gelu, mix_done, gated = sem("u_done"), sem("u_gelu"), sem("mix_done"), sem("gated")
    a_squared, a_summed, a_mean, a_rstd, a_scaled = (sem("a_" + n) for n in ("squared", "summed", "mean", "rstd", "scaled"))
    mt_turned, mt_hi, mt_lo = sem("mt_turned"), sem("mt_hi"), sem("mt_lo")
    x2_in = [sem(f"x_again{t}") for t in range(TB)]
    wout_done, wout_added = sem("wout_done"), sem("wout_added")

    q2_done, q2_hi, q2_lo = sem("q2_done"), sem("q2_hi"), sem("q2_lo")
    mem_in = sem("mem_in")
    k2_done, k2_hi, k2_lo = sem("k2_done"), sem("k2_hi"), sem("k2_lo")
    v2_done, v2_hi, v2_lo = sem("v2_done"), sem("v2_hi"), sem("v2_lo")
    xs_done, xs_max, xs_neg, xs_exp, xs_inv, xs_prob = (sem("xs_" + n) for n in ("done", "max", "neg", "exp", "inv", "prob"))
    xt_done, xt_hi, xt_lo, xo_done, xo_hi, xo_lo = (sem(n) for n in ("xt_done", "xt_hi", "xt_lo", "xo_done", "xo_hi", "xo_lo"))
    down_done, down_added = sem("down_done"), sem("down_added")

    ff1_done, ff_relu, ff_sq, hid_hi, hid_lo = (sem(n) for n in ("ff1_done", "ff_relu", "ff_sq", "hid_hi", "hid_lo"))
    gf_in, y_made, y_out = sem("gf_in"), sem("y_made"), sem("y_out")

    def wait_lo(eng, n, more=0):
        eng.wait_ge(w_lo_dve if lo_on_vector(n) else w_lo_pool, lo_count(n) + more)

    def tok(tb, n=1):
        return slice(tb * P, (tb + n) * P)

    halves = (slice(0, HALF), slice(HALF, SEQ))

    def xs(stage, tb):
        return stage[:, :, tok(tb)]

    def split_hi(out, src, gain=None):
        if gain is None:
            return nc.scalar.activation(out, src, ACT.Copy)
        return nc.scalar.activation(out, src, ACT.Copy, scale=gain)

    def split_lo(out, src, hi, gain=None):
        if gain is None:
            return nc.vector.tensor_tensor(out, src, f32(hi), ALU.subtract)
        return nc.vector.scalar_tensor_tensor(out, src, gain, f32(hi), ALU.mult, ALU.subtract)

    def freed(n):
        if n < N_QK:
            return (w_used, used_count(n)) if n < 7 else (v_done, TB)
        if n < N_GV:
            pair, j = divmod(n - N_QK, 4)
            return (w_used, used_count(n)) if j % 2 == 0 else (proj_done, 4 * pair + j + 1)
        for first, done in ((N_GV, gv_done), (N_U, u_done), (N_OUT, wout_done), (N_OUT + 8, wout_done), (N_CO, down_done), (N_CO + 8, down_done)):
            if first <= n < first + 8:
                second = first in (N_OUT + 8, N_CO + 8)
                return (w_used, used_count(n)) if n < first + 7 else (done, TB * (1 + second))
        if n < N_CV:
            m, kh = divmod((n - N_CQ) % 16, 2)
            if kh == 0:
                return w_used, used_count(n)
            return (q2_done, 8 * (m // 4) + m % 4 + 5) if n < N_CK else (k2_done, m + 1)
        if n < N_CO:
            c, k = divmod(n - N_CV, 8)
            return (w_used, used_count(n)) if k < 7 else (v2_done, MB * (c + 1))
        f, kh = divmod(n - N_FF, 2)
        return (w_used, used_count(n)) if kh == 0 else (ff1_done, 4 + f + 1)

    def place_free(n):
        if n < WS_SLOTS:
            return None
        if n < N_QK + 4:
            return freed(n - 8)
        if n < N_GV + 4:
            return freed(n - 4)
        if n < N_GV + 8:
            return qk_now, 2 * (PAIRS - 1)
        if N_U + 4 <= n < N_U + 8:
            return t_done, 24 * PAIRS
        return freed(n - 8)

    def place_of(n):
        if N_GV + 4 <= n < N_GV + 8:
            return WGV[:, n - N_GV - 4]
        return WS[:, n % 4 if N_QK <= n < N_GV else n % 8]

    def weight_hi(act, n):
        act.wait_ge(raw_in[n % 4], 16 * (n // 4 + 1))
        free = place_free(n)
        if free:
            act.wait_ge(*free)
        split_hi(place_of(n)[:, 0, :], RAW[:, n % 4, :]).then_inc(w_hi, 1)

    def weight_lo(eng, n):
        eng.wait_ge(w_hi, n + 1)
        return eng.tensor_tensor(place_of(n)[:, 1, :], RAW[:, n % 4, :], f32(place_of(n)[:, 0, :]), ALU.subtract).then_inc(
            w_lo_dve if lo_on_vector(n) else w_lo_pool, 1)

    def cols_of(w, k, c):
        return w[k * P:(k + 1) * P, c:c + HALF]

    def unit_of(w, kh, c):
        return w.rearrange("(k p) n -> p k n", p=P)[:, 4 * kh:4 * kh + 4, bass.ds(c, P)]

    block = nc.Block()
    with block:
        @block.sync
        def _(sp):
            def load(n, src, more=0, unit=False):
                if n >= RAW_SLOTS:
                    wait_lo(sp, n - RAW_SLOTS, more)
                dst = RAW[:, n % 4, :]
                if unit:
                    dst = dst.rearrange("p (k n) -> p k n", k=4)
                sp.dma_start(dst, src).then_inc(raw_in[n % 4], 16)

            gains = (norm_mix_g, head_norm_g, norm_cross_g, norm_mem_g, norm_ffn_g)

            def load_gain(g, done):
                sp.dma_start(CG[:, g, :], gains[g].rearrange("(k p) -> p k", p=P)).then_inc(done, 16)

            def load_x(tb):
                sp.dma_start(xs(XSA, tb), x[tok(tb), :].rearrange("p (k n) -> p k n", k=KC)).then_inc(x_in[tb], 16)

            for k in range(KC):
                load(N_V + k, cols_of(w_in, k, COL_V))
                if k == 1:
                    load_gain(G_MIX, mix_gain_in)
                if k in (5, 7):
                    load_x(k // 2)
            for tb in range(4, TB):
                load_x(tb)
            for g in range(1, 5):
                load_gain(g, const_in)
            sp.dma_start(BSP[:, :], b_spatial.rearrange("g t -> t g")).then_inc(const_in, 16)
            for j in range(4):
                load(N_QK + j, unit_of(w_in, j % 2, COL_Q if j < 2 else COL_K), unit=True)
            with sp.Fori(0, PAIRS - 1) as i:
                for j in range(4):
                    load(N_QK + 4 + j, unit_of(w_in, j % 2, (COL_Q if j < 2 else COL_K) + P + P * i), 4 * i, True)
            for k in range(KC):
                load(N_GV + k, cols_of(w_in, k, COL_GV))
            for k in range(KC):
                load(N_U + k, cols_of(w_in, k, COL_U))
            for c in range(2):
                for k in range(KC):
                    load(N_OUT + 8 * c + k, cols_of(w_out, k, c * HALF))
            for m in range(KC):
                for kh in range(2):
                    load(N_CQ + 2 * m + kh, unit_of(w_cq, kh, m * P), unit=True)
            for m in range(KC):
                for kh in range(2):
                    load(N_CK + 2 * m + kh, unit_of(w_ckv, kh, m * P), unit=True)
            for c in range(2):
                for k in range(KC):
                    load(N_CV + 8 * c + k, cols_of(w_ckv, k, D + c * HALF))
            for c in range(2):
                for k in range(KC):
                    load(N_CO + 8 * c + k, cols_of(w_co, k, c * HALF))

            def ff2_slots(g):
                for j in range(8):
                    load(N_FF + 8 + j, w_ff2[bass.ds(g * HALF + (j % 4) * P, P), (j // 4) * HALF:(j // 4 + 1) * HALF], 16 * g)

            for j in range(8):
                load(N_FF + j, unit_of(w_ff1, j % 2, (j // 2) * P), unit=True)
            with sp.Fori(0, FG - 1) as g:
                ff2_slots(g)
                for j in range(8):
                    load(N_FF + 16 + j, unit_of(w_ff1, j % 2, HALF + g * HALF + (j // 2) * P), 16 * g, True)
            ff2_slots(FG - 1)
            for i in range(TB + 1):
                tb = min(i, TB - 1)
                cols = slice(0, D) if i < TB - 1 else halves[i - (TB - 1)]
                sp.wait_ge(y_made, i + 1)
                sp.dma_start(y[tok(tb), cols], YT[:, tb, cols]).then_inc(y_out, 16)
            sp.wait_ge(y_out, 16 * (TB + 1))

        @block.gpsimd
        def _(pool):
            pool.memset(ident[:, :], 0.0).then_inc(const_made, 1)
            pool.memset(NEGH[:, :], -0.5).then_inc(const_made, 1)
            pool.memset(NEGM[:, :], 0.0).then_inc(const_made, 1)
            pool.wait_ge(const_made, 3)
            pool.affine_select(out=ident[:, :], in_=ident[:, :], compare_op=ALU.not_equal, fill=1.0, base=0,
                               pattern=[[-1, P]], channel_multiplier=1).then_inc(const_made, 1)
            pool.affine_select(out=NEGM[:, :], in_=NEGM[:, :], compare_op=ALU.is_gt, fill=NEG, base=0,
                               pattern=[[-1, P]], channel_multiplier=1).then_inc(const_made, 1)

            def row_rstd(norm, tb, width=D, src=SS, dst=RS):
                pool.wait_ge(norm.squared, tb + 1)
                pool.tensor_scalar(dst[:, tb:tb + 1], src[:, tb:tb + 1], 1.0 / width, EPS, ALU.mult, ALU.add).then_inc(norm.mean, 1)
                pool.wait_ge(norm.mean, tb + 1)
                pool.tensor_tensor(dst[:, tb:tb + 1], dst[:, tb:tb + 1], NEGH[:, 0:1], ALU.pow).then_inc(norm.rstd, 1)

            row_rstd(n_x, 0)
            for k in range(0, KC, 2):
                weight_lo(pool, N_V + k)
                if k in (0, 2):
                    row_rstd(n_x, 1 if k == 0 else 2)
            for tb in range(3, TB):
                row_rstd(n_x, tb)
            for j in range(4):
                weight_lo(pool, N_QK + j)

            def weigh(u, s):
                tb = s % TB
                w = (tb + 1) * P
                m0, b0 = sum(M_W[:s % 2]), sum(BE_W[:s % 4])
                pool.wait_ge(scanned, u + 1)
                pool.tensor_tensor(BEBUF[:, b0:b0 + w - 1], BEBUF[:, b0:b0 + w - 1], MBUF[:, m0 + 1:m0 + w], ALU.mult).then_inc(a_done, 1)

            for j in range(4):
                weight_lo(pool, N_QK + 4 + j)
            def o_rstd(head):
                sums, r = VF[:, 0, head, HD:HD + TB], VF[:, 0, head, HD + TB:HD + 2 * TB]
                pool.wait_ge(os_summed, head + 1)
                pool.tensor_scalar(r, sums, 1.0 / HD, EPS, ALU.mult, ALU.add).then_inc(os_mean, 1)
                pool.wait_ge(os_mean, head + 1)
                pool.tensor_tensor(r, r, NEGH[:, 0:TB], ALU.pow).then_inc(os_rstd, 1)

            for u in range(1, 4):
                weigh(u - 1, u - 1)
            with pool.Fori(0, PAIRS - 2) as i:
                for t in range(16):
                    weigh(16 * i + 3 + t, (3 + t) % 16)
                    if t in (5, 12):
                        for j in ((0, 1) if t == 5 else (2, 3)):
                            pool.wait_ge(w_hi, N_QK + 8 + j + 1 + 4 * i)
                            pool.tensor_tensor(WS[:, j, 1, :], RAW[:, j, :], f32(WS[:, j, 0, :]), ALU.subtract).then_inc(w_lo_pool, 1)
            for t in range(16 + 12 + 1):
                weigh(16 * (PAIRS - 2) + 3 + t, (3 + t) % 16)
                head = O_STEPS[PAIRS - 2 + t // 16].get(t % 16 - 2)
                if head is not None:
                    o_rstd(head)
                for k in {5: (0, 1), 11: (2, 3), 13: (4, 5), 14: (6, 7)}.get(t, ()):
                    weight_lo(pool, N_GV + k)

            pool.wait_ge(wsp_in, 16)
            pool.affine_select(out=WSP[:, :, :], in_=WSP[:, :, :], compare_op=ALU.is_ge, fill=0.0, base=0,
                               pattern=[[0, GROUPS], [-1, P]], channel_multiplier=1).then_inc(wsp_masked, 1)

            def group_rstd(which, tb, n, width, summed, mean, rstd):
                pool.wait_ge(summed, tb + 1)
                s, r = ST[:, 0, which, tb, 0:n], ST[:, 1, which, tb, 0:n]
                pool.tensor_scalar(r, s, 1.0 / width, EPS, ALU.mult, ALU.add).then_inc(mean, 1)
                pool.wait_ge(mean, tb + 1)
                pool.tensor_tensor(r, r, NEGH[:, 0:n], ALU.pow).then_inc(rstd, 1)

            o_rstd(HEADS - 1)
            for tb in range(TB):
                group_rstd(0, tb, GROUPS, P, gv_summed, gv_mean, gv_rstd)
            for tb in range(TB):
                group_rstd(1, tb, GROUPS, P, a_summed, a_mean, a_rstd)
            for tb in range(TB):
                if tb == TB - 1:
                    for n in range(N_CQ, N_CQ + 2):
                        weight_lo(pool, n)
                row_rstd(n_h1, tb)
            for n in range(N_CQ + 2, N_CQ + 8):
                weight_lo(pool, n)
            for mt in range(MB):
                row_rstd(n_mem, mt)
            for n in range(N_CQ + 8, N_CO):
                if not lo_on_vector(n):
                    weight_lo(pool, n)

            for v in range(2 * XH):
                pool.wait_ge(xs_inv, v + 1)
                r = XST[:, v % 2, 3, :].rearrange("p (q a) -> p q a", a=1).to_broadcast([P, 4, N_MEM])
                pool.tensor_tensor(EP[v % 2][:, :, :], EP[v % 2][:, :, :], r, ALU.mult).then_inc(xs_prob, 1)
                if 1 <= v < 5:
                    for n in (N_CO + 2 * v - 2, N_CO + 2 * v - 1):
                        weight_lo(pool, n)
            for tb in range(TB - 1):
                row_rstd(n_h2, tb)

            def ff_lo(j, more, dst):
                pool.wait_ge(w_hi, N_FF + j + 1 + more)
                pool.tensor_tensor(dst[:, j % 8, 1, :], RAW[:, j % 4, :], f32(dst[:, j % 8, 0, :]), ALU.subtract).then_inc(w_lo_pool, 1)

            for j in range(8):
                if j == 2:
                    row_rstd(n_h2, TB - 1)
                ff_lo(j, 0, WS)
            with pool.Fori(0, FG - 1) as g:
                for j in range(8, 16):
                    ff_lo(j, 16 * g, W2S)
                for j in range(16, 24):
                    ff_lo(j, 16 * g, WS)
            for j in range(8, 16):
                ff_lo(j, 16 * (FG - 1), W2S)
            for tb in range(TB):
                row_rstd(n_fin, tb)

        @block.scalar
        def _(act):
            for tb in range(2):
                act.dma_start(xs(XSA, tb), x[tok(tb), :].rearrange("p (k n) -> p k n", k=KC)).then_inc(x_in[tb], 16)

            def evac_turned(norm, tb, dst, gain, count0=0):
                for b in range(2):
                    act.wait_ge(norm.turned, 2 * tb + b + 1)
                    for k in range(4 * b, 4 * b + 4):
                        last = split_hi(dst[:, 0, k, tok(tb)], PS[:, 2 + b, tok(k % 4)], CG[:, gain, k:k + 1])
                    last.then_inc(norm.hi, 1)

            def square_x(tb):
                act.wait_ge(x_in[tb], 16)
                nc.scalar.activation(H[:, tb, :].rearrange("p (k n) -> p k n", k=KC), xs(XSA, tb), ACT.Square,
                                     accum_out=SS[:, tb:tb + 1]).then_inc(n_x.squared, 1)

            def evac_v(tb):
                act.wait_ge(v_done, tb + 1)
                split_hi(VHL[:, tb, :, 0:HD], PS[:, tb % 2, :].rearrange("p (h d) -> p h d", h=HEADS)).then_inc(v_hi, 1)

            square_x(0)
            weight_hi(act, N_V)
            square_x(1)
            for k in range(1, KC):
                weight_hi(act, N_V + k)
                if k == 1:
                    act.wait_ge(mix_gain_in, 16)
                    evac_turned(n_x, 0, AT_, G_MIX)
                if k == 3:
                    square_x(2)
            for tb in range(1, TB):
                evac_turned(n_x, tb, AT_, G_MIX)
                if tb + 2 < TB:
                    square_x(tb + 2)
                evac_v(tb - 1)
            for j in range(4):
                weight_hi(act, N_QK + j)
            evac_v(TB - 1)

            def evac_proj(j, i4, dst, bank):
                act.wait_ge(proj_done, i4 + j + 1)
                split_hi(dst[:, j // 2, 0, (j % 2) * HALF:(j % 2 + 1) * HALF], PS[:, bank, :]).then_inc(qk_hi, 1)

            for j in range(4):
                evac_proj(j, 0, QKC, 4 + j)
            for j in range(4):
                weight_hi(act, N_QK + 4 + j)

            def attn_a_hi(u, s, g24):
                tb = s % TB
                for g in range(1 if tb < 4 else 2):
                    n = min(4, tb + 1 - 4 * g) * P
                    count = groups_before(s) + g + 1 + g24
                    act.wait_ge(t_done, count)
                    if g == 0 and not (isinstance(u, int) and u < 2):
                        act.wait_ge(pv_done, u - 1)
                    split_hi(ATR[tb % 2][:, 0, g * HALF:g * HALF + n], PS[:, 4 + g, 0:n]).then_inc(at_hi, 1)

            def sigmoids(u, s):
                tb = s % TB
                w = (tb + 1) * P
                z0 = 2 * (s % 2)
                m0, b0 = sum(M_W[:s % 2]), sum(BE_W[:s % 4])
                zp = PS[:, z0:z0 + 2, :].rearrange("p b n -> p (b n)")[:, 0:w]
                act.wait_ge(z_masked, u + 1)
                nc.scalar.activation(BEBUF[:, b0:b0 + w], zp, ACT.Sigmoid, scale=Z_SCALE).then_inc(sig, 1)
                if not (isinstance(u, int) and u < 2):
                    act.wait_ge(a_done, u - 1)
                nc.scalar.activation(MBUF[:, m0:m0 + w], zp, ACT.Sigmoid, scale=-Z_SCALE).then_inc(sig, 1)

            act.wait_ge(const_in, 5 * 16)
            act.wait_ge(v_lo, TB)
            for u in range(4):
                if u >= 3:
                    attn_a_hi(u - 3, u - 3, 0)
                sigmoids(u, u)
                if u == 2:
                    evac_proj(0, 4, QKN, 7)
            def square_o(head):
                act.wait_ge(o_done, TB * (head + 1))
                nc.scalar.activation(VF[:, :, head, 0:HD], O[:, :, head * HD:(head + 1) * HD], ACT.Square).then_inc(os_squared, 1)

            with act.Fori(0, PAIRS - 2) as i:
                for t in range(16):
                    s = 1 + t
                    attn_a_hi(16 * i + s, s % 16, 24 * i + 24 * (s // 16))
                    if t in (4, 11):
                        for j in ((0, 1) if t == 4 else (2, 3)):
                            act.wait_ge(raw_in[j], 16 * (N_QK // 4 + 3) + 16 * i)
                            if j % 2 == 0:
                                act.wait_ge(w_used, used_count(N_QK + 4 + j) + 2 * i)
                            else:
                                act.wait_ge(proj_done, 4 * i + 4 + j + 1)
                            split_hi(WS[:, j, 0, :], RAW[:, j, :]).then_inc(w_hi, 1)
                    sigmoids(16 * i + 4 + t, (4 + t) % 16)
                    if t == 14:
                        act.wait_ge(qk_now, 2 * i + 2)
                    if t in EVACUATE:
                        evac_proj(EVACUATE[t], 4 * i + (8 if t > 10 else 4), QKN, 7)
            for pair in range(PAIRS - 2, PAIRS):
                last = pair == PAIRS - 1
                for t in range(15 if last else 16):
                    s = 1 + t
                    attn_a_hi(16 * pair + s, s % 16, 24 * pair + 24 * (s // 16))
                    if not last:
                        for k in {4: (0, 1), 10: (2, 3), 13: (4, 5, 6, 7)}.get(t, ()):
                            weight_hi(act, N_GV + k)
                    if not last or t < 12:
                        sigmoids(16 * pair + 4 + t, (4 + t) % 16)
                    if t in O_STEPS[pair]:
                        square_o(O_STEPS[pair][t])
                    if not last and t in EVACUATE and t < 10:
                        evac_proj(EVACUATE[t], 4 * pair + 4, QKN, 7)
                    if last and t == 13:
                        act.wait_ge(z_done, 16 * PAIRS)
                        act.dma_start(WSP[:, :, :], w_spatial.rearrange("g t s -> t g s")).then_inc(wsp_in, 16)
                        act.dma_start(GB[:, :], gm_v_norm_g.rearrange("(a n) -> a n", a=1).to_broadcast([P, HALF])).then_inc(gb_in, 16)
            for k in range(KC):
                weight_hi(act, N_U + k)

            square_o(HEADS - 1)

            def norm_step(s):
                if s < TB:
                    act.wait_ge(gv_copied, s + 1)
                    nc.scalar.activation(GV[:, s, :], GV[:, s, :], ACT.Gelu_apprx_tanh).then_inc(gv_gelu, 1)
                    act.wait_ge(gv_gelu, s + 1)
                    if s >= 2:
                        act.wait_ge(gv_summed, s - 1)
                    nc.scalar.activation(SQ[:, s % 2, :], GV[:, s, :], ACT.Square).then_inc(gv_squared, 1)
                if s >= 2:
                    act.wait_ge(gv_scaled, s - 1)
                    if s == 2:
                        act.wait_ge(os_scaled, HEADS)
                    split_hi(VN[:, s - 2, 1, :], GV[:, s - 2, :]).then_inc(vn_hi, 1)

            def gelu_u(tb):
                act.wait_ge(u_done, tb + 1)
                nc.scalar.activation(U[:, tb, :], PS[:, tb % 2, :], ACT.Gelu_apprx_tanh).then_inc(u_gelu, 1)

            def evac_merged(i, tb, half):
                act.wait_ge(mt_turned, i + 1)
                for k in range(4):
                    last = split_hi(AT_[:, 0, 4 * half + k, tok(tb)], PS[:, 2 + i % 2, tok(k)],
                                    CG[:, G_HEAD, 4 * half + k:4 * half + k + 1])
                last.then_inc(mt_hi, 1)

            def square_a(tb):
                act.wait_ge(gated, 4 * (tb // 4 + 1))
                if tb >= 2:
                    act.wait_ge(a_summed, tb - 1)
                else:
                    act.wait_ge(gv_summed, TB)
                nc.scalar.activation(SQ[:, tb % 2, :], U[:, tb, :], ACT.Square).then_inc(a_squared, 1)

            act.wait_ge(wt_turned, 1)
            split_hi(WT[:, 0, :, :], PS[:, 2, :].rearrange("p (g t) -> p g t", g=GROUPS)).then_inc(wt_hi, 1)
            for i in range(4):
                norm_step(2 * i)
                norm_step(2 * i + 1)
                gelu_u(i)
                if i == 0:
                    for tb in range(4):
                        act.dma_start(H[:, tb, :], x[tok(tb), :]).then_inc(x2_in[tb], 16)
                else:
                    evac_merged(i - 1, i - 1, 1)
            norm_step(TB)
            norm_step(TB + 1)
            gelu_u(4)
            evac_merged(3, 3, 1)
            for tb in range(4):
                square_a(tb)
            gelu_u(5)
            evac_merged(4, 4, 1)
            gelu_u(6)
            evac_merged(5, 5, 1)
            for k in range(4):
                weight_hi(act, N_OUT + k)
            gelu_u(7)
            evac_merged(6, 6, 1)
            evac_merged(7, 0, 0)
            for k in range(4, KC):
                weight_hi(act, N_OUT + k)
            evac_merged(8, 1, 0)
            for tb in range(4, TB):
                square_a(tb)
                if tb == 5:
                    evac_merged(9, 2, 0)
                if tb == 6:
                    evac_merged(10, 3, 0)
            act.wait_ge(a_scaled, TB)
            for tb in range(4, TB):
                act.dma_start(H[:, tb, :], x[tok(tb), :]).then_inc(x2_in[tb], 16)
            evac_merged(11, 7, 1)
            for tb in range(4, TB):
                evac_merged(8 + tb, tb, 0)
            for k in range(KC):
                weight_hi(act, N_OUT + 8 + k)

            def square_h(norm, tb, added, count):
                act.wait_ge(added, count)
                nc.scalar.activation(xs(XSB, tb), H[:, tb, :].rearrange("p (k n) -> p k n", k=KC), ACT.Square,
                                     accum_out=SS[:, tb:tb + 1]).then_inc(norm.squared, 1)

            act.wait_ge(mt_lo, 16)
            for tb in range(TB):
                if tb >= 3:
                    evac_turned(n_h1, tb - 3, BT_, G_CROSS)
                square_h(n_h1, tb, wout_added, TB + tb + 1)
                if tb == TB - 2:
                    for k in range(4):
                        weight_hi(act, N_CQ + k)
            evac_turned(n_h1, TB - 3, BT_, G_CROSS)
            for k in range(4, 8):
                weight_hi(act, N_CQ + k)
            act.wait_ge(wout_done, 2 * TB)
            for mt in range(MB):
                act.dma_start(XM[mt][:, :, :], mem[tok(mt), :].rearrange("p (k n) -> p k n", k=KC)).then_inc(mem_in, 16)

            def evac_q2(i, m, f):
                act.wait_ge(q2_done, i + 1)
                if m == KC - 1:
                    act.wait_ge(n_mem.turned, 2 * MB)
                split_hi(AT_[:, 0, m, f * HALF:(f + 1) * HALF], PS[:, 4 + i % 4, :]).then_inc(q2_hi, 1)

            for i in range(4):
                evac_q2(i, i, 0)
                if i < 2:
                    evac_turned(n_h1, TB - 2 + i, BT_, G_CROSS)
            act.wait_ge(mem_in, 16 * MB)
            act.wait_ge(n_h1.scaled, TB)
            for mt in range(MB):
                act.wait_ge(wout_added, 2 * TB)
                if mt:
                    act.wait_ge(n_mem.squared, mt)
                nc.scalar.activation(PS[:, 0:2, :].rearrange("p b (k n) -> p (b k) n", k=4), XM[mt][:, :, :], ACT.Square,
                                     accum_out=SS[:, mt:mt + 1]).then_inc(n_mem.squared, 1)
            for i in range(4, 8):
                evac_q2(i, i - 4, 1)
                for k in (2 * i - 8, 2 * i - 7):
                    weight_hi(act, N_CQ + 8 + k)
            for i in range(8, 12):
                evac_q2(i, i - 4, 0)
            for mt in range(MB):
                for b in range(2):
                    for k in range(4 * b, 4 * b + 4):
                        last = split_hi(MEMT[:, 0, k, tok(mt)], PS[:, 2 * mt + b, tok(k % 4)], CG[:, G_MEM, k:k + 1])
                    last.then_inc(n_mem.hi, 1)
            for i in range(12, 16):
                evac_q2(i, i - 8, 1)
                for k in (2 * i - 24, 2 * i - 23):
                    weight_hi(act, N_CK + k)

            for m in range(KC):
                act.wait_ge(k2_done, m + 1)
                split_hi(K2T[:, 0, m, :], PS[:, 4 + m % 4, 0:N_MEM]).then_inc(k2_hi, 1)
                for k in (2 * m, 2 * m + 1):
                    weight_hi(act, N_CK + 8 + k)

            def x_exp(v):
                act.wait_ge(xs_neg, v + 1)
                if v >= 2:
                    act.wait_ge(xt_done, 2 * (v - 1))
                for q in range(4):
                    nc.scalar.activation(EP[v % 2][:, q, :], PS[:, 2 * (v % 2) + q // 2, (q % 2) * N_MEM:(q % 2 + 1) * N_MEM], ACT.Exp,
                                         bias=XST[:, v % 2, 1, q:q + 1], scale=X_SCALE,
                                         accum_out=XST[:, v % 2, 2, q:q + 1]).then_inc(xs_exp, 1)

            x_exp(0)
            for c in range(2):
                for mb in range(MB):
                    if mb == MB - 1 and c == 0:
                        for k in range(KC):
                            weight_hi(act, N_CV + 8 + k)
                    act.wait_ge(v2_done, MB * c + mb + 1)
                    split_hi(v2_at(0, mb, c), PS[:, 6 + mb, :]).then_inc(v2_hi, 1)

            def x_t_hi(v):
                for mb in range(MB):
                    act.wait_ge(xt_done, 2 * v + mb + 1)
                    if v >= 2:
                        act.wait_ge(xo_done, 2 * (v - 1))
                    split_hi(pt_at(v, 0, mb), PS[:, 4 + mb, :]).then_inc(xt_hi, 1)

            def x_o_hi(v):
                h, f = divmod(v, 2)
                for d in range(2):
                    act.wait_ge(xo_done, 2 * v + d + 1)
                    split_hi(AT_[:, 0, 2 * h + d, f * HALF:(f + 1) * HALF], PS[:, 6 + d, :]).then_inc(xo_hi, 1)

            for v in range(1, 2 * XH + 3):
                if v >= 3:
                    x_o_hi(v - 3)
                if 2 <= v < 2 * XH + 2:
                    x_t_hi(v - 2)
                if 2 <= v < 6:
                    for k in (2 * v - 4, 2 * v - 3):
                        weight_hi(act, N_CO + k)
                if v < 2 * XH:
                    x_exp(v)

            act.wait_ge(xo_lo, 4 * XH)
            for tb in range(TB):
                if tb >= 3:
                    evac_turned(n_h2, tb - 3, BT_, G_FFN)
                if tb == 0:
                    for k in range(KC):
                        weight_hi(act, N_CO + 8 + k)
                square_h(n_h2, tb, down_added, TB + tb + 1)
                if tb == TB - 2:
                    for k in range(4):
                        weight_hi(act, N_FF + k)
            evac_turned(n_h2, TB - 3, BT_, G_FFN)
            for k in range(4, 8):
                weight_hi(act, N_FF + k)

            def ff_hi(j, more, dst):
                act.wait_ge(raw_in[j % 4], 16 * ((N_FF + j) // 4 + 1) + more)
                split_hi(dst[:, j % 8, 0, :], RAW[:, j % 4, :]).then_inc(w_hi, 1)

            def relu_square(g8, i):
                f, half = i % 4, i // 4
                act.wait_ge(ff_relu, g8 + i + 1)
                nc.scalar.activation(PS[:, 4 + f, :], PS[:, 4 + f, :], ACT.Square).then_inc(ff_sq, 1)
                act.wait_ge(ff_sq, g8 + i + 1)
                split_hi(HID[:, 0, f, half * HALF:(half + 1) * HALF], PS[:, 4 + f, :]).then_inc(hid_hi, 1)

            def ff_group(g, first=False):
                act.wait_ge(down_done, 2 * TB + 2 * TB * g)
                for i in range(8):
                    relu_square(8 * g, i)
                    if first and i < 2:
                        evac_turned(n_h2, TB - 2 + i, BT_, G_FFN)
                    ff_hi(8 + i, 64 * g, W2S)

            def next_ff1(g):
                for j in range(16, 24):
                    sem_free, count = freed(N_FF + j - 16)
                    act.wait_ge(sem_free, count + (4 * g if j % 2 == 0 else 8 * g))
                    ff_hi(j, 64 * g, WS)

            ff_group(0, first=True)
            next_ff1(0)
            with act.Fori(1, FG - 1) as g:
                ff_group(g)
                next_ff1(g)
            ff_group(FG - 1)
            act.wait_ge(ff1_done, 8 * FG)
            act.dma_start(GF[:, :], norm_final_g.rearrange("(a n) -> a n", a=1).to_broadcast([P, D])).then_inc(gf_in, 16)
            for tb in range(TB):
                act.wait_ge(down_added, 2 * TB * FG + 2 * tb + 2)
                if tb:
                    act.wait_ge(n_fin.squared, tb)
                nc.scalar.activation(JUNK[:, :], H[:, tb, :], ACT.Square, accum_out=SS[:, tb:tb + 1]).then_inc(n_fin.squared, 1)

        @block.vector
        def _(dve):
            def scale_rows(norm, tb, dst, src):
                dve.wait_ge(norm.rstd, tb + 1)
                nc.vector.tensor_scalar(dst, src, RS[:, tb:tb + 1], None, ALU.mult).then_inc(norm.scaled, 1)

            def lo_turned(norm, tb, dst, gain):
                for b in range(2):
                    dve.wait_ge(norm.hi, 2 * tb + b + 1)
                    for k in range(4 * b, 4 * b + 4):
                        last = split_lo(dst[:, 1, k, tok(tb)], PS[:, 2 + b, tok(k % 4)], dst[:, 0, k, tok(tb)], CG[:, gain, k:k + 1])
                    last.then_inc(norm.lo, 1)

            def lo_v(tb):
                dve.wait_ge(v_hi, tb + 1)
                nc.vector.tensor_tensor(VHL[:, tb, :, HD:2 * HD], PS[:, tb % 2, :].rearrange("p (h d) -> p h d", h=HEADS),
                                        f32(VHL[:, tb, :, 0:HD]), ALU.subtract).then_inc(v_lo, 1)

            for tb in range(2):
                scale_rows(n_x, tb, xs(XSA, tb), xs(XSA, tb))
                if tb == 0:
                    weight_lo(dve, N_V + 1)
            dve.wait_ge(mix_gain_in, 16)
            for tb in range(TB):
                lo_turned(n_x, tb, AT_, G_MIX)
                if tb == 0:
                    weight_lo(dve, N_V + 3)
                if tb + 2 < TB:
                    scale_rows(n_x, tb + 2, xs(XSA, tb + 2), xs(XSA, tb + 2))
                if tb == 0:
                    weight_lo(dve, N_V + 5)
                    weight_lo(dve, N_V + 7)
                if tb:
                    lo_v(tb - 1)
            lo_v(TB - 1)

            def lo_proj(j, i4, dst, bank):
                dve.wait_ge(qk_hi, i4 + j + 1)
                half = slice((j % 2) * HALF, (j % 2 + 1) * HALF)
                split_lo(dst[:, j // 2, 1, half], PS[:, bank, :], dst[:, j // 2, 0, half]).then_inc(qk_lo, 1)

            def take_qk(i, half):
                dve.wait_ge(z_done, 16 * i)
                dve.wait_ge(qk_lo, 4 * i + 4)
                t = slice(half * HALF, (half + 1) * HALF)
                nc.vector.tensor_copy(QKC[:, :, :, t], QKN[:, :, :, t]).then_inc(qk_now, 1)

            for j in range(4):
                lo_proj(j, 0, QKC, 4 + j)

            def scan(u, s):
                w = (s % TB + 1) * P
                m0 = sum(M_W[:s % 2])
                dve.wait_ge(sig, 2 * u + 2)
                m = MBUF[:, m0:m0 + w][:, ::-1]
                nc.vector.tensor_tensor_scan(m, m, m, 1.0, ALU.mult, ALU.bypass).then_inc(scanned, 1)

            def sum_o(u, s, head):
                dve.wait_ge(pv_done, u + 1)
                nc.vector.tensor_reduce(O[:, s % TB, bass.ds(head * HD, HD)], PS[:, 6, 0:2 * HD].rearrange("p (a d) -> p d a", a=2),
                                        AX.X, ALU.add).then_inc(o_done, 1)

            def lo_a(s, g24):
                tb = s % TB
                for g in range(1 if tb < 4 else 2):
                    n = min(4, tb + 1 - 4 * g) * P
                    dve.wait_ge(at_hi, groups_before(s) + g + 1 + g24)
                    keys = slice(g * HALF, g * HALF + n)
                    split_lo(ATR[tb % 2][:, 1, keys], PS[:, 4 + g, 0:n], ATR[tb % 2][:, 0, keys]).then_inc(at_lo, 1)

            def mask(u, s):
                tb = s % TB
                b, c = 2 * (s % 2) + tb // 4, (tb % 4) * P
                dve.wait_ge(z_done, u + 1)
                nc.vector.tensor_tensor(PS[:, b, c:c + P], PS[:, b, c:c + P], NEGM[:, :], ALU.add).then_inc(z_masked, 1)

            dve.wait_ge(const_in, 5 * 16)
            dve.wait_ge(const_made, 5)
            for u in range(4):
                mask(u, u)
                if u >= 1:
                    scan(u - 1, u - 1)
                if u >= 3:
                    lo_a(u - 3, 0)
                    lo_proj(0, 4, QKN, 7)
            def sum_squares_o(head):
                dve.wait_ge(os_squared, head + 1)
                nc.vector.tensor_reduce(VF[:, 0, head, HD:HD + TB], VF[:, :, head, 0:HD], AX.X, ALU.add).then_inc(os_summed, 1)

            def scale_o(head):
                dve.wait_ge(os_rstd, head + 1)
                o = O[:, :, head * HD:(head + 1) * HD]
                r = VF[:, 0, head, HD + TB:HD + 2 * TB].rearrange("p (t a) -> p t a", a=1).to_broadcast([P, TB, HD])
                nc.vector.tensor_tensor(o, o, r, ALU.mult).then_inc(os_scaled, 1)

            with dve.Fori(0, PAIRS - 2) as i:
                for t in range(16):
                    mask(16 * i + 4 + t, (4 + t) % 16)
                    if t in (11, 12):
                        take_qk(i + 1, t - 11)
                    scan(16 * i + 3 + t, (3 + t) % 16)
                    lo_a((t + 1) % 16, 24 * i + 24 * ((t + 1) // 16))
                    sum_o(16 * i + t, t, 2 * i + t // 8)
                    if t in EVACUATE:
                        lo_proj(EVACUATE[t], 4 * i + (8 if t > 10 else 4), QKN, 7)
            for pair in range(PAIRS - 2, PAIRS):
                last = pair == PAIRS - 1
                for t in range(16):
                    u = 16 * pair + t
                    if u + 4 < 16 * PAIRS:
                        mask(u + 4, (4 + t) % 16)
                    if not last and t in (11, 12):
                        take_qk(pair + 1, t - 11)
                    if u + 3 < 16 * PAIRS:
                        scan(u + 3, (3 + t) % 16)
                    if u + 1 < 16 * PAIRS:
                        lo_a((1 + t) % 16, 24 * (pair + (1 + t) // 16))
                    if u == 16 * PAIRS - 1:
                        for k in range(4):
                            weight_lo(dve, N_U + k)
                    sum_o(u, t, 2 * pair + t // 8)
                    if not last and t in EVACUATE and t < 10:
                        lo_proj(EVACUATE[t], 4 * pair + 4, QKN, 7)
                    if t - 1 in O_STEPS[pair]:
                        sum_squares_o(O_STEPS[pair][t - 1])
                    if t - 4 in O_STEPS[pair]:
                        scale_o(O_STEPS[pair][t - 4])
                    chunks = v_chunks(pair, t)
                    if chunks and chunks[-1][1] == KC - 1:
                        tb = chunks[-1][0]
                        dve.wait_ge(gv_done, tb + 1)
                        nc.vector.tensor_copy(GV[:, tb, :], PS[:, V_BANKS[tb], :]).then_inc(gv_copied, 1)

            for k in range(4, KC):
                weight_lo(dve, N_U + k)

            def group_sum(src_sem, which, tb, n, done):
                dve.wait_ge(src_sem, tb + 1)
                nc.vector.tensor_reduce(ST[:, 0, which, tb, 0:n], SQ[:, tb % 2, :].rearrange("p (g d) -> p g d", g=n), AX.X, ALU.add).then_inc(done, 1)

            def group_scale(which, tb, n, rstd, tile, done):
                dve.wait_ge(rstd, tb + 1)
                v = tile.rearrange("p (g d) -> p g d", g=n)
                r = ST[:, 1, which, tb, 0:n].rearrange("p (g a) -> p g a", a=1).to_broadcast([P, n, HALF // n])
                nc.vector.tensor_tensor(v, v, r, ALU.mult).then_inc(done, 1)

            def norm_step(s):
                if s < TB:
                    group_sum(gv_squared, 0, s, GROUPS, gv_summed)
                    nc.vector.tensor_tensor(GV[:, s, :], GV[:, s, :], GB[:, :], ALU.mult).then_inc(gv_gained, 1)
                if 1 <= s <= TB:
                    dve.wait_ge(gv_gained, s)
                    group_scale(0, s - 1, GROUPS, gv_rstd, GV[:, s - 1, :], gv_scaled)
                if s >= 2:
                    tb = s - 2
                    dve.wait_ge(vn_hi, tb + 1)
                    split_lo(VN[:, tb, 0, :], GV[:, tb, :], VN[:, tb, 1, :]).then_inc(vn_lo, 1)

            sum_squares_o(HEADS - 1)
            dve.wait_ge(gb_in, 16)
            dve.wait_ge(wt_hi, 1)
            split_lo(WT[:, 1, :, :], PS[:, 2, :].rearrange("p (g t) -> p g t", g=GROUPS), WT[:, 0, :, :]).then_inc(wt_lo, 1)

            def lo_merged(i, tb, half):
                dve.wait_ge(mt_hi, i + 1)
                for k in range(4):
                    c = 4 * half + k
                    last = split_lo(AT_[:, 1, c, tok(tb)], PS[:, 2 + i % 2, tok(k)], AT_[:, 0, c, tok(tb)], CG[:, G_HEAD, c:c + 1])
                last.then_inc(mt_lo, 1)

            def gate(half, g):
                dve.wait_ge(mix_done, 4 * half + g + 1)
                dve.wait_ge(u_gelu, 4 * half + 4)
                u = U[:, 4 * half:4 * half + 4, tok(g)]
                nc.vector.scalar_tensor_tensor(u, PS[:, 4 + g, :].rearrange("p (c d) -> p c d", c=4), BSP[:, g:g + 1], u,
                                               ALU.add, ALU.mult).then_inc(gated, 1)

            def finish_a(half):
                for tb in range(4 * half, 4 * half + 4):
                    group_sum(a_squared, 1, tb, GROUPS, a_summed)
                    if tb > 4 * half:
                        group_scale(1, tb - 1, GROUPS, a_rstd, U[:, tb - 1, :], a_scaled)
                    if tb == 5:
                        lo_merged(9, 2, 0)
                    if tb == 6:
                        lo_merged(10, 3, 0)
                group_scale(1, 4 * half + 3, GROUPS, a_rstd, U[:, 4 * half + 3, :], a_scaled)

            for i in range(4):
                norm_step(2 * i)
                if i == 0:
                    scale_o(HEADS - 1)
                norm_step(2 * i + 1)
                if i:
                    lo_merged(i - 1, i - 1, 1)
            norm_step(TB)
            norm_step(TB + 1)
            lo_merged(3, 3, 1)
            for g in range(GROUPS):
                gate(0, g)
            finish_a(0)
            lo_merged(4, 4, 1)
            lo_merged(5, 5, 1)
            for k in range(4):
                weight_lo(dve, N_OUT + k)
            lo_merged(6, 6, 1)
            lo_merged(7, 0, 0)
            for k in range(4, KC):
                weight_lo(dve, N_OUT + k)
            lo_merged(8, 1, 0)
            for g in range(GROUPS):
                gate(1, g)
            finish_a(1)

            def add_block(done, i, added, tb, c, bank):
                dve.wait_ge(done, i + 1)
                hc = H[:, tb, c * HALF:(c + 1) * HALF]
                nc.vector.tensor_tensor(hc, PS[:, bank, :], hc, ALU.add).then_inc(added, 1)

            for tb in range(TB):
                dve.wait_ge(x2_in[tb], 16)
                if tb == TB - 1:
                    for k in range(KC):
                        weight_lo(dve, N_OUT + 8 + k)
                add_block(wout_done, tb, wout_added, tb, 0, OUT_BANKS[tb])
                if tb == 2:
                    lo_merged(11, 7, 1)
                if 2 <= tb < 6:
                    lo_merged(10 + tb, tb + 2, 0)
            for tb in range(TB):
                if tb >= 3:
                    lo_turned(n_h1, tb - 3, BT_, G_CROSS)
                add_block(wout_done, TB + tb, wout_added, tb, 1, tb % 2)
                if tb:
                    scale_rows(n_h1, tb - 1, xs(XSB, tb - 1), H[:, tb - 1, :].rearrange("p (k n) -> p k n", k=KC))
            scale_rows(n_h1, TB - 1, xs(XSB, TB - 1), H[:, TB - 1, :].rearrange("p (k n) -> p k n", k=KC))
            lo_turned(n_h1, TB - 3, BT_, G_CROSS)

            def lo_q2(i, m, f):
                dve.wait_ge(q2_hi, i + 1)
                c = slice(f * HALF, (f + 1) * HALF)
                split_lo(AT_[:, 1, m, c], PS[:, 4 + i % 4, :], AT_[:, 0, m, c]).then_inc(q2_lo, 1)

            for i in range(4):
                lo_q2(i, i, 0)
                if i < 2:
                    lo_turned(n_h1, TB - 2 + i, BT_, G_CROSS)
            for mt in range(MB):
                scale_rows(n_mem, mt, XM[mt][:, :, :], XM[mt][:, :, :])
            for i in range(4, 8):
                lo_q2(i, i - 4, 1)
            for i in range(8, 12):
                lo_q2(i, i - 4, 0)
            for mt in range(MB):
                for b in range(2):
                    dve.wait_ge(n_mem.hi, 2 * mt + b + 1)
                    for k in range(4 * b, 4 * b + 4):
                        last = split_lo(MEMT[:, 1, k, tok(mt)], PS[:, 2 * mt + b, tok(k % 4)], MEMT[:, 0, k, tok(mt)],
                                        CG[:, G_MEM, k:k + 1])
                    last.then_inc(n_mem.lo, 1)
            for i in range(12, 16):
                lo_q2(i, i - 8, 1)
            for m in range(KC):
                dve.wait_ge(k2_hi, m + 1)
                split_lo(K2T[:, 1, m, :], PS[:, 4 + m % 4, 0:N_MEM], K2T[:, 0, m, :]).then_inc(k2_lo, 1)
                weight_lo(dve, N_CK + 8 + 2 * m + 1)

            def x_max(v):
                if v >= 2:
                    dve.wait_ge(xs_exp, 4 * (v - 1))
                for b in range(2):
                    dve.wait_ge(xs_done, 2 * v + b + 1)
                    nc.vector.tensor_reduce(XST[:, v % 2, 0, 2 * b:2 * b + 2], PS[:, 2 * (v % 2) + b, :].rearrange("p (q m) -> p q m", q=2),
                                            AX.X, ALU.max).then_inc(xs_max, 1)
                dve.wait_ge(xs_max, 2 * v + 2)
                nc.vector.tensor_scalar(XST[:, v % 2, 1, :], XST[:, v % 2, 0, :], -X_SCALE, None, ALU.mult).then_inc(xs_neg, 1)

            def x_inv(v):
                dve.wait_ge(xs_exp, 4 * v + 4)
                nc.vector.reciprocal(XST[:, v % 2, 3, :], XST[:, v % 2, 2, :]).then_inc(xs_inv, 1)

            def x_t_lo(v):
                for mb in range(MB):
                    dve.wait_ge(xt_hi, 2 * v + mb + 1)
                    split_lo(pt_at(v, 1, mb), PS[:, 4 + mb, :], pt_at(v, 0, mb)).then_inc(xt_lo, 1)

            def x_o_lo(v):
                h, f = divmod(v, 2)
                for d in range(2):
                    dve.wait_ge(xo_hi, 2 * v + d + 1)
                    c = slice(f * HALF, (f + 1) * HALF)
                    split_lo(AT_[:, 1, 2 * h + d, c], PS[:, 6 + d, :], AT_[:, 0, 2 * h + d, c]).then_inc(xo_lo, 1)

            x_max(0)
            for c in range(2):
                for mb in range(MB):
                    if mb == MB - 1 and c == 0:
                        for k in range(1, KC, 2):
                            weight_lo(dve, N_CV + 8 + k)
                    dve.wait_ge(v2_hi, MB * c + mb + 1)
                    split_lo(v2_at(1, mb, c), PS[:, 6 + mb, :], v2_at(0, mb, c)).then_inc(v2_lo, 1)

            for v in range(1, 2 * XH + 3):
                if v < 2 * XH + 1:
                    x_inv(v - 1)
                if v >= 3:
                    x_o_lo(v - 3)
                if 2 <= v < 2 * XH + 2:
                    x_t_lo(v - 2)
                if v < 2 * XH:
                    x_max(v)

            for tb in range(TB):
                if tb == TB - 1:
                    for k in range(KC):
                        weight_lo(dve, N_CO + 8 + k)
                add_block(down_done, tb, down_added, tb, 0, tb % 2)
            for tb in range(TB):
                if tb >= 3:
                    lo_turned(n_h2, tb - 3, BT_, G_FFN)
                add_block(down_done, TB + tb, down_added, tb, 1, tb % 2)
                if tb:
                    scale_rows(n_h2, tb - 1, xs(XSB, tb - 1), H[:, tb - 1, :].rearrange("p (k n) -> p k n", k=KC))
            scale_rows(n_h2, TB - 1, xs(XSB, TB - 1), H[:, TB - 1, :].rearrange("p (k n) -> p k n", k=KC))
            lo_turned(n_h2, TB - 3, BT_, G_FFN)

            def ff_hidden(g, first=False):
                for i in range(9):
                    if i < 8:
                        dve.wait_ge(ff1_done, 8 * g + i + 1)
                        nc.vector.tensor_scalar(PS[:, 4 + i % 4, :], PS[:, 4 + i % 4, :], 0.0, None, ALU.max).then_inc(ff_relu, 1)
                    if i >= 1:
                        f, half = (i - 1) % 4, (i - 1) // 4
                        c = slice(half * HALF, (half + 1) * HALF)
                        dve.wait_ge(hid_hi, 8 * g + i)
                        split_lo(HID[:, 1, f, c], PS[:, 4 + f, :], HID[:, 0, f, c]).then_inc(hid_lo, 1)
                    if first and i < 2:
                        lo_turned(n_h2, TB - 2 + i, BT_, G_FFN)

            def ff_add(g, i):
                tb, nh = divmod(i, 2)
                dve.wait_ge(down_done, 2 * TB + 2 * TB * g + i + 1)
                hc = H[:, tb, nh * HALF:(nh + 1) * HALF]
                nc.vector.tensor_tensor(hc, PS[:, i % 4, :], hc, ALU.add).then_inc(down_added, 1)

            def make_y(tb, cols=slice(0, D)):
                dve.wait_ge(n_fin.rstd, tb + 1)
                nc.vector.scalar_tensor_tensor(YT[:, tb, cols], H[:, tb, cols], RS[:, tb:tb + 1], GF[:, cols],
                                               ALU.mult, ALU.mult).then_inc(y_made, 1)

            ff_hidden(0, first=True)
            for i in range(2 * TB):
                ff_add(0, i)
            with dve.Fori(1, FG - 1) as g:
                ff_hidden(g)
                for i in range(2 * TB):
                    ff_add(g, i)
            ff_hidden(FG - 1)
            dve.wait_ge(gf_in, 16)
            for i in range(2 * TB):
                ff_add(FG - 1, i)
                if i % 2 and i > 1:
                    make_y(i // 2 - 1)
            make_y(TB - 1, halves[0])
            make_y(TB - 1, halves[1])

        @block.tensor
        def _(pe):
            mm = nc.tensor.matmul

            def three(out, w_hi_, w_lo_, m_hi, m_lo, first, last, between=iter(())):
                mm(out, w_hi_, m_hi, start=first, stop=False)
                next(between, None)
                mm(out, w_hi_, m_lo, start=False, stop=False)
                next(between, None)
                third = mm(out, w_lo_, m_hi, start=False, stop=last)
                next(between, None)
                return third

            def turn(chunk, bank, ks):
                for q, k in enumerate(ks):
                    last = nc.tensor.transpose(PS[:, bank, tok(q)], chunk(k), ident[:, :])
                return last

            def turn_block(norm, tb, stage):
                pe.wait_ge(norm.scaled, tb + 1)
                for b in range(2):
                    if tb:
                        pe.wait_ge(norm.lo, 2 * (tb - 1) + b + 1)
                    turn(lambda k: stage[:, k, tok(tb)], 2 + b, range(4 * b, 4 * b + 4)).then_inc(norm.turned, 1)

            def token_major(src, tb, bank, n0, done, last_block, ks=range(KC), late=None):
                for k in ks:
                    if late and k == late[0]:
                        pe.wait_ge(*late[1:])
                    if tb == 0:
                        wait_lo(pe, n0 + k)
                    last = three(PS[:, bank, :], src[:, 0, k, tok(tb)], src[:, 1, k, tok(tb)], WS[:, k, 0, :], WS[:, k, 1, :],
                                 k == 0, k == KC - 1)
                    if last_block and k < KC - 1:
                        last.then_inc(w_used, 1)
                if ks[-1] == KC - 1:
                    last.then_inc(done, 1)

            def feature_major(src, bank, place, n0, more, cols, done, first_half, last_half):
                for k in range(KC):
                    if first_half and k % 4 == 0:
                        wait_lo(pe, n0 + k // 4, more)
                    w = WS[:, place + k // 4, :, tok(k % 4)]
                    width = cols.stop - cols.start
                    last = three(PS[:, bank, 0:width], w[:, 0, :], w[:, 1, :], src[:, 0, k, cols], src[:, 1, k, cols], k == 0, k == KC - 1)
                    if last_half and k == 3:
                        last.then_inc(w_used, 1)
                last.then_inc(done, 1)

            pe.wait_ge(const_made, 5)
            turn_block(n_x, 0, XSA)
            pe.wait_ge(n_x.lo, 1)
            token_major(AT_, 0, 0, N_V, v_done, False, ks=range(KC // 2))
            turn_block(n_x, 1, XSA)
            for tb in range(TB):
                pe.wait_ge(n_x.lo, 2 * tb + 1)
                if tb >= 2:
                    pe.wait_ge(v_lo, tb - 1)
                token_major(AT_, tb, tb % 2, N_V, v_done, tb == TB - 1,
                            ks=range(0 if tb else KC // 2, KC), late=(KC // 2, n_x.lo, 2 * tb + 2))
                if tb + 2 < TB:
                    turn_block(n_x, tb + 2, XSA)

            def project(chunks, pair, bank, between=iter(())):
                for j, k in chunks:
                    place = 2 * (j // 2) + k // 4
                    if k == 0 and not (isinstance(pair, int) and pair == 0):
                        pe.wait_ge(qk_lo, 4 * pair + j)
                    if j % 2 == 0 and k % 4 == 0:
                        wait_lo(pe, N_QK + place, 4 * pair)
                    w = WS[:, place, :, tok(k % 4)]
                    last = three(PS[:, bank, :], w[:, 0, :], w[:, 1, :], AT_[:, 0, k, halves[j % 2]], AT_[:, 1, k, halves[j % 2]],
                                 k == 0, k == KC - 1, between)
                    if j % 2 == 1 and k == 3:
                        last.then_inc(w_used, 1)
                    if k == KC - 1:
                        last.then_inc(proj_done, 1)

            for j in range(4):
                project([(j, k) for k in range(KC)], 0, 4 + j)

            def v_product(chunks, between):
                for tb, k in chunks:
                    if k == 0:
                        pe.wait_ge(*((qk_lo, 4 * PAIRS) if tb == 0 else (gv_copied, tb) if tb < TB - 1 else (sig, 2 * 16 * PAIRS)))
                    if tb == 0:
                        wait_lo(pe, N_GV + k)
                    w = place_of(N_GV + k)
                    last = three(PS[:, V_BANKS[tb], :], AT_[:, 0, k, tok(tb)], AT_[:, 1, k, tok(tb)], w[:, 0, :], w[:, 1, :],
                                 k == 0, k == KC - 1, between)
                    if k == KC - 1:
                        last.then_inc(gv_done, 1)
                    elif tb == TB - 1:
                        last.then_inc(w_used, 1)

            def logits(u, s, pair, between=iter(())):
                hh, tb = divmod(s, TB)
                if isinstance(u, int) and u == 0:
                    pe.wait_ge(qk_lo, 4)
                elif s in (0, TB // 2 - 1) and not (isinstance(pair, int) and pair == 0):
                    pe.wait_ge(qk_now, 2 * pair - 1 + (s > 0))
                if not (isinstance(u, int) and u < 2):
                    pe.wait_ge(sig, 2 * u - 2)
                rows = slice(HD * hh, HD * hh + HD)
                w = (tb + 1) * P
                for b in range(1 if w <= HALF else 2):
                    keys = slice(b * HALF, min(w, (b + 1) * HALF))
                    last = three(PS[:, 2 * (s % 2) + b, 0:keys.stop - keys.start],
                                 QKC[rows, 0, 0, tok(tb)], QKC[rows, 0, 1, tok(tb)], QKC[rows, 1, 0, keys], QKC[rows, 1, 1, keys], True, True, between)
                last.then_inc(z_done, 1)

            def turn_a(u, s, g24, between=iter(())):
                tb = s % TB
                b0 = sum(BE_W[:s % 4])
                pe.wait_ge(a_done, u + 1)
                for g in range(1 if tb < 4 else 2):
                    if not (isinstance(u, int) and u == 0) and g <= (s - 1) % TB // 4:
                        pe.wait_ge(at_lo, groups_before(s - 1) + g + 1 + g24)
                    for k in range(4 * g, min(4 * g + 4, tb + 1)):
                        next(between, None)
                        last = nc.tensor.transpose(PS[:, 4 + g, tok(k % 4)], BEBUF[:, b0 + k * P:b0 + (k + 1) * P], ident[:, :])
                    last.then_inc(t_done, 1)

            def values(u, s, g24, head):
                tb = s % TB
                if s:
                    pe.wait_ge(o_done, u)
                for sb in range(tb + 1):
                    if sb % 4 == 0:
                        pe.wait_ge(at_lo, groups_before(s) + sb // 4 + 1 + g24)
                    for part in range(2):
                        last = mm(PS[:, 6, 0:2 * HD], ATR[tb % 2][:, part, tok(sb)], VHL[:, sb, head, :],
                                  start=sb == 0 and part == 0, stop=sb == tb and part == 1)
                        if sb == tb and part == 1:
                            last.then_inc(pv_done, 1)
                        yield

            pe.wait_ge(v_lo, TB)
            for u in range(4):
                logits(u, u, 0)
                if u >= 3:
                    turn_a(u - 3, u - 3, 0)
                for t in ((11,), (12,), (13, 14), (15,))[u]:
                    project(PARTS[t], 1, 7)
            with pe.Fori(0, PAIRS - 2) as i:
                for t in range(16):
                    value_steps = values(16 * i + t, t, 24 * i, 2 * i + t // TB)
                    logits(16 * i + 4 + t, (4 + t) % 16, i + (4 + t) // 16)
                    turn_a(16 * i + 1 + t, (1 + t) % 16, 24 * i + 24 * (t // 15), value_steps)
                    project(PARTS.get(t, ()), i + (2 if t > 10 else 1), 7, value_steps)
                    for _ in value_steps:
                        pass
                pe.wait_ge(o_done, 16 * i + 16)
            for pair in range(PAIRS - 2, PAIRS):
                for t in range(16):
                    u = 16 * pair + t
                    value_steps = values(u, t, 24 * pair, 2 * pair + t // TB)
                    if u + 4 < 16 * PAIRS:
                        logits(u + 4, (4 + t) % 16, pair + (4 + t) // 16)
                    if u + 1 < 16 * PAIRS:
                        turn_a(u + 1, (1 + t) % 16, 24 * (pair + t // 15), value_steps)
                    if pair < PAIRS - 1 and t < 10:
                        project(PARTS.get(t, ()), pair + 1, 7, value_steps)
                    v_product(v_chunks(pair, t), value_steps)
                    for _ in value_steps:
                        pass
                if pair < PAIRS - 1:
                    pe.wait_ge(o_done, 16 * pair + 16)

            pe.wait_ge(sig, 2 * 16 * PAIRS)
            pe.wait_ge(wsp_masked, 1)
            turn(lambda g: WSP[:, g, :], 2, range(GROUPS)).then_inc(wt_turned, 1)

            merged_at = {}

            def turn_merged(tb, half):
                i = len(merged_at)
                merged_at[tb, half] = i
                if half == 1:
                    pe.wait_ge(os_scaled, HEADS)
                else:
                    pe.wait_ge(a_scaled, tb + 1)
                if i >= 2:
                    pe.wait_ge(mt_lo, i - 1)
                else:
                    pe.wait_ge(wt_lo, 1)
                turn(lambda k: (O if half else U)[:, tb, tok(k)], 2 + i % 2, range(4)).then_inc(mt_turned, 1)

            def mix(half):
                pe.wait_ge(vn_lo, 4 * half + 4)
                for g in range(GROUPS):
                    if half == 0:
                        pe.wait_ge((at_lo, at_lo, o_done, gv_copied)[g], (24 * PAIRS, 24 * PAIRS, 16 * PAIRS, TB)[g])
                    else:
                        pe.wait_ge(gated, g + 1)
                    v = VN[:, 4 * half:4 * half + 4, :, tok(g)]
                    three(PS[:, 4 + g, :], WT[:, 0, g, :], WT[:, 1, g, :], v[:, :, 1], v[:, :, 0], True, True).then_inc(mix_done, 1)

            AFTER_U = {1: [(0, 1)], 2: [(1, 1)], 3: [(2, 1)], 4: [(3, 1)], 5: [(4, 1)], 6: [(5, 1)], 7: [(6, 1), (0, 0)]}
            for tb in range(TB):
                if tb:
                    pe.wait_ge(*((gv_copied, TB) if tb == 1 else (u_gelu, tb - 1)))
                token_major(AT_, tb, tb % 2, N_U, u_done, tb == TB - 1)
                for at_tb, half in AFTER_U.get(tb, ()):
                    turn_merged(at_tb, half)
                if tb == 4:
                    mix(0)
            mix(1)
            turn_merged(1, 0)

            pe.wait_ge(u_gelu, TB)
            for tb in range(TB):
                pe.wait_ge(mt_lo, max(merged_at[tb, 0], merged_at[tb, 1]) + 1)
                if tb == 2:
                    pe.wait_ge(gated, 2 * GROUPS)
                if tb >= 6:
                    pe.wait_ge(wout_added, tb - 5)
                token_major(AT_, tb, OUT_BANKS[tb], N_OUT, wout_done, tb == TB - 1)
                for at_tb, half in {0: ((2, 0), (3, 0)), 2: ((7, 1), (4, 0)), 3: ((5, 0),), 4: ((6, 0),), 5: ((7, 0),)}.get(tb, ()):
                    turn_merged(at_tb, half)
            for tb in range(TB):
                pe.wait_ge(wout_added, TB + tb - 1)
                token_major(AT_, tb, tb % 2, N_OUT + 8, wout_done, tb == TB - 1)
                if tb >= 2:
                    turn_block(n_h1, tb - 2, XSB)

            def q2(i, m, f):
                if i >= 4:
                    pe.wait_ge(q2_lo, i - 3)
                feature_major(BT_, 4 + i % 4, 2 * (m % 4), N_CQ + 2 * m, 0, halves[f], q2_done, f == 0, f == 1)

            pe.wait_ge(n_h1.lo, TB)
            for i in range(4):
                q2(i, i, 0)
                if i < 2:
                    turn_block(n_h1, TB - 2 + i, XSB)
            pe.wait_ge(n_h1.lo, 2 * TB)
            for i in range(4, 8):
                q2(i, i - 4, 1)
            for i in range(8, 12):
                if i == 9:
                    for mt in range(MB):
                        pe.wait_ge(n_mem.scaled, mt + 1)
                        for b in range(2):
                            turn(lambda k: XM[mt][:, k, :], 2 * mt + b, range(4 * b, 4 * b + 4)).then_inc(n_mem.turned, 1)
                q2(i, i - 4, 0)
            for i in range(12, 16):
                q2(i, i - 8, 1)
            pe.wait_ge(n_mem.lo, 2 * MB)
            for m in range(KC):
                if m < 4:
                    pe.wait_ge(q2_lo, 12 + m + 1)
                else:
                    pe.wait_ge(k2_lo, m - 3)
                feature_major(MEMT, 4 + m % 4, 2 * (m % 4), N_CK + 2 * m, 0, slice(0, N_MEM), k2_done, True, True)

            def x_logits(v):
                h, f = divmod(v, 2)
                if v >= 2:
                    pe.wait_ge(xs_exp, 4 * (v - 1))
                for q in range(4):
                    out = PS[:, 2 * (v % 2) + q // 2, (q % 2) * N_MEM:(q % 2 + 1) * N_MEM]
                    for c in (2 * h, 2 * h + 1):
                        t = tok(4 * f + q)
                        last = three(out, AT_[:, 0, c, t], AT_[:, 1, c, t], K2T[:, 0, c, :], K2T[:, 1, c, :], c == 2 * h, c == 2 * h + 1)
                    if q % 2:
                        last.then_inc(xs_done, 1)

            def x_turn(v):
                pe.wait_ge(xs_prob, v + 1)
                for mb in range(MB):
                    if v:
                        pe.wait_ge(xt_lo, 2 * (v - 1) + mb + 1)
                    turn(lambda q: EP[v % 2][:, q, tok(mb)], 4 + mb, range(4)).then_inc(xt_done, 1)

            def x_values(v):
                h = v // 2
                pe.wait_ge(xt_lo, 2 * v + 2)
                if v == 0:
                    pe.wait_ge(v2_lo, 2 * MB)
                for d in range(2):
                    if v:
                        pe.wait_ge(xo_lo, 2 * (v - 1) + d + 1)
                    c, part = divmod(h * XD + d * P, HALF)
                    cols = slice(part, part + P)
                    for mb in range(MB):
                        last = three(PS[:, 6 + d, :], v2_at(0, mb, c)[:, cols], v2_at(1, mb, c)[:, cols], pt_at(v, 0, mb), pt_at(v, 1, mb),
                                     mb == 0, mb == MB - 1)
                    last.then_inc(xo_done, 1)

            pe.wait_ge(k2_lo, KC)
            x_logits(0)
            for c in range(2):
                for mb in range(MB):
                    if c:
                        pe.wait_ge(v2_lo, mb + 1)
                    token_major(MEMT, mb, 6 + mb, N_CV + 8 * c, v2_done, mb == MB - 1)
            for v in range(1, 2 * XH + 2):
                if v == 2 * XH + 1:
                    pe.wait_ge(xs_exp, 4 * (v - 2))
                    pe.wait_ge(xo_lo, 2 * XH)
                    token_major(AT_, 0, 0, N_CO, down_done, False, ks=range(4))
                if v >= 3:
                    x_values(v - 3)
                if 2 <= v:
                    x_turn(v - 2)
                if v < 2 * XH:
                    x_logits(v)

            def co(i, ks=range(KC)):
                c, tb = divmod(i, TB)
                if i >= 2:
                    pe.wait_ge(down_added, i - 1)
                token_major(AT_, tb, tb % 2, N_CO + 8 * c, down_done, tb == TB - 1, ks,
                            late=(KC - 2, xo_lo, 4 * XH - 2 if i == 0 else 4 * XH) if i in (0, TB // 2) else None)
                if c and tb >= 2:
                    turn_block(n_h2, tb - 2, XSB)

            pe.wait_ge(xo_lo, 4 * XH - 4)
            pe.wait_ge(xs_exp, 8 * XH)
            co(0, range(4, KC))
            x_values(2 * XH - 1)
            for i in range(1, 2 * TB):
                co(i)

            def ff1(g, i):
                f, half = i % 4, i // 4
                if i >= 4:
                    pe.wait_ge(hid_lo, 8 * g + i - 3)
                feature_major(BT_, 4 + f, 2 * f, N_FF + 2 * f, 16 * g, halves[half], ff1_done, half == 0, half == 1)

            def down(g):
                for i in range(2 * TB):
                    tb, nh = divmod(i, 2)
                    if i == 0 or i >= 4:
                        pe.wait_ge(down_added, 2 * TB + 2 * TB * g + max(i - 3, 0))
                    if tb in (0, TB // 2) and nh == 0:
                        pe.wait_ge(hid_lo, 8 * g + 4 + tb)
                    for k in range(4):
                        if tb == 0:
                            wait_lo(pe, N_FF + 8 + 4 * nh + k, 16 * g)
                        last = three(PS[:, i % 4, :], HID[:, 0, k, tok(tb)], HID[:, 1, k, tok(tb)],
                                     W2S[:, 4 * nh + k, 0, :], W2S[:, 4 * nh + k, 1, :], k == 0, k == 3)
                    last.then_inc(down_done, 1)

            pe.wait_ge(n_h2.lo, TB)
            for i in range(8):
                if i == 4:
                    pe.wait_ge(n_h2.lo, 2 * TB)
                ff1(0, i)
                if i < 2:
                    turn_block(n_h2, TB - 2 + i, XSB)
            down(0)
            with pe.Fori(1, FG) as g:
                for i in range(8):
                    ff1(g, i)
                down(g)


_INS = ["x", "mem", "norm_mix_g", "w_in", "gm_v_norm_g", "w_spatial", "b_spatial", "head_norm_g", "w_out", "norm_cross_g",
        "norm_mem_g", "w_cq", "w_ckv", "w_co", "norm_ffn_g", "w_ff1", "w_ff2", "norm_final_g"]


def kernel(**inputs):
    import numpy as _np
    import concourse.bacc as _bacc
    from concourse import mybir as _mybir
    from concourse.bass_utils import run_bass_kernel_spmd as _run

    nc = _bacc.Bacc("TRN2", target_bir_lowering=False, num_devices=1)
    arrays, args = {}, []
    for name in _INS:
        a = _np.ascontiguousarray(inputs[name])
        if name != "norm_final_g":
            a = a.reshape(a.shape[1:])
        arrays[f"in_{name}"] = a
        args.append(nc.dram_tensor(f"in_{name}", a.shape, _mybir.dt.from_np(a.dtype), kind="ExternalInput").ap())
    out = nc.dram_tensor("out_y", (SEQ, D), F32, kind="ExternalOutput").ap()
    with nc.allow_non_contiguous_dma(reason="gains and biases go one feature to a partition"):
        build(nc, *args, out)
    r = _run(nc, [arrays], core_ids=[0])
    return r.results[0]["out_y"].reshape(1, SEQ, D)
```
